# Optimizing a Trainium2 kernel written in Bass

```python
import jax, jax.numpy as jnp
from jax import lax
import numpy as np

D_MODEL = 1024
BATCH = 1
SEQ = 1024
DEPTH = 1
DEC_BATCH = 1
DEC_SEQ = 512
PAST_LEN = 128

GRID_W = 64
HEAD_DIM = 64
ATTN_HEADS = 8
ATTN_KV_HEADS = 2
ATTN_GROUP = ATTN_HEADS // ATTN_KV_HEADS
ATTN_WIDTH = ATTN_HEADS * HEAD_DIM
KV_WIDTH = ATTN_KV_HEADS * HEAD_DIM
Q_BLOCK = 128
ROPE_THETA = 10000.0
RWKV_HEADS = 8
RWKV_HEAD = 64
RWKV_WIDTH = RWKV_HEADS * RWKV_HEAD
DECAY_LORA = 64
AAA_LORA = 64
GATE_LORA = 128
N_DIR = 2
LNX_EPS = 64e-5
N_BRANCH = 2
D_FF = ((-(-8 * D_MODEL // 3) + 255) // 256) * 256
NORM_EPS = 1e-6

OFF_Q = 0
OFF_K = OFF_Q + ATTN_WIDTH
OFF_V = OFF_K + KV_WIDTH
OFF_R = OFF_V + KV_WIDTH
OFF_RK = OFF_R + RWKV_WIDTH
OFF_RV = OFF_RK + RWKV_WIDTH
OFF_WD = OFF_RV + RWKV_WIDTH
OFF_AD = OFF_WD + N_DIR * DECAY_LORA
OFF_GD = OFF_AD + N_DIR * AAA_LORA
OFF_GATE = OFF_GD + GATE_LORA
IN_COLS = OFF_GATE + N_BRANCH * D_MODEL
SHIFT_COLS = OFF_GATE - OFF_R

kernel_name = "hybrid_axial_gqa_rwkv7_bidir_encoder"

def rms_norm(x, g, eps=NORM_EPS):
    xf = x.astype(jnp.float32)
    y = xf * lax.rsqrt(jnp.mean(xf * xf, axis=-1, keepdims=True) + eps)
    return (y * g.astype(jnp.float32)).astype(x.dtype)

def axial_rope_tables(n):
    rows = n // GRID_W
    row = jnp.broadcast_to(jnp.arange(rows)[:, None], (rows, GRID_W)).reshape(-1).astype(jnp.float32)
    col = jnp.broadcast_to(jnp.arange(GRID_W)[None, :], (rows, GRID_W)).reshape(-1).astype(jnp.float32)
    nf = HEAD_DIM // 4
    inv = ROPE_THETA ** (-jnp.arange(nf, dtype=jnp.float32) / nf)
    ang = jnp.concatenate([row[:, None] * inv, col[:, None] * inv], axis=-1)
    return jnp.cos(ang), jnp.sin(ang)

def apply_rope(x, cos, sin):
    xf = x.astype(jnp.float32).reshape(x.shape[:-1] + (HEAD_DIM // 2, 2))
    x1, x2 = xf[..., 0], xf[..., 1]
    c = cos[None, :, None, :]
    s = sin[None, :, None, :]
    out = jnp.stack([x1 * c - x2 * s, x1 * s + x2 * c], axis=-1)
    return out.reshape(x.shape).astype(x.dtype)

def axial_gqa_attention(q, k, v, q_gain, k_gain):
    b, n = q.shape[:2]
    q = rms_norm(q.reshape(b, n, ATTN_HEADS, HEAD_DIM), q_gain)
    k = rms_norm(k.reshape(b, n, ATTN_KV_HEADS, HEAD_DIM), k_gain)
    v = v.reshape(b, n, ATTN_KV_HEADS, HEAD_DIM)
    cos, sin = axial_rope_tables(n)
    q = apply_rope(q, cos, sin)
    k = apply_rope(k, cos, sin)
    nblk = n // Q_BLOCK
    qb = q.reshape(b, nblk, Q_BLOCK, ATTN_KV_HEADS, ATTN_GROUP, HEAD_DIM).transpose(1, 0, 2, 3, 4, 5)
    scale = HEAD_DIM ** -0.5

    def one_block(qi):
        s = jnp.einsum('bqhgd,bkhd->bhgqk', qi, k, preferred_element_type=jnp.float32) * scale
        p = jax.nn.softmax(s, axis=-1).astype(v.dtype)
        return jnp.einsum('bhgqk,bkhd->bqhgd', p, v)

    o = lax.map(one_block, qb)
    return o.transpose(1, 0, 2, 3, 4, 5).reshape(b, n, ATTN_WIDTH)

def centred_shift_mix(p, mu):
    prev = jnp.pad(p[:, :-1], ((0, 0), (1, 0), (0, 0)))
    nxt = jnp.pad(p[:, 1:], ((0, 0), (0, 1), (0, 0)))
    return p + (0.5 * (prev + nxt) - p) * mu

def rwkv7_scan(r, decay, k, v, a_vec, b_vec, reverse):
    b, n, h, d = r.shape

    def step(S, inp):
        r_t, w_t, k_t, v_t, a_t, b_t = inp
        sa = jnp.einsum('bhvk,bhk->bhv', S, a_t)
        S = S * w_t[:, :, None, :] + sa[..., None] * b_t[:, :, None, :] + v_t[..., None] * k_t[:, :, None, :]
        return S, jnp.einsum('bhvk,bhk->bhv', S, r_t)

    xs = tuple(jnp.swapaxes(t, 0, 1) for t in (r, decay, k, v, a_vec, b_vec))
    s0 = jnp.zeros((b, h, d, d), jnp.float32)
    _, ys = lax.scan(step, s0, xs, reverse=reverse)
    return jnp.swapaxes(ys, 0, 1)

def rwkv7_bidirectional(z, w0, w_up, a0, a_up, g_up, k_k, k_a, r_k, lnx_w, lnx_b):
    f32 = jnp.float32
    b, n = z.shape[:2]
    hs = lambda t: t.reshape(b, n, RWKV_HEADS, RWKV_HEAD)
    r = z[..., 0:RWKV_WIDTH]
    k = z[..., RWKV_WIDTH:2 * RWKV_WIDTH]
    v = z[..., 2 * RWKV_WIDTH:3 * RWKV_WIDTH]
    o_wd = OFF_WD - OFF_R
    o_ad = OFF_AD - OFF_R
    o_gd = OFF_GD - OFF_R
    wd = z[..., o_wd:o_ad].reshape(b, n, N_DIR, DECAY_LORA)
    ad = z[..., o_ad:o_gd].reshape(b, n, N_DIR, AAA_LORA)
    gd = z[..., o_gd:]
    w_log = -jax.nn.softplus(-(w0.astype(f32) + jnp.einsum('btdr,drc->btdc', jnp.tanh(wd), w_up.astype(f32)))) - 0.5
    decay = jnp.exp(-jnp.exp(w_log))
    a = jax.nn.sigmoid(a0.astype(f32) + jnp.einsum('btdr,drc->btdc', ad, a_up.astype(f32)))
    g = jax.nn.sigmoid(gd) @ g_up.astype(f32)
    kk = hs(k * k_k.astype(f32))
    kk = kk / jnp.maximum(jnp.sqrt(jnp.sum(kk * kk, axis=-1, keepdims=True)), 1e-12)
    k_dir = k[:, :, None, :] * (1.0 + (a - 1.0) * k_a.astype(f32))
    y = jnp.zeros((b, n, RWKV_HEADS, RWKV_HEAD), f32)
    for d, rev in enumerate((False, True)):
        y = y + rwkv7_scan(hs(r), hs(decay[:, :, d]), hs(k_dir[:, :, d]), hs(v), -kk, kk * hs(a[:, :, d]), rev)
    mu = jnp.mean(y, axis=-1, keepdims=True)
    var = jnp.mean(jnp.square(y - mu), axis=-1, keepdims=True)
    y = ((y - mu) * lax.rsqrt(var + LNX_EPS)).reshape(b, n, RWKV_WIDTH) * lnx_w.astype(f32) + lnx_b.astype(f32)
    k_bonus = hs(0.5 * (k_dir[:, :, 0] + k_dir[:, :, 1]))
    bonus = jnp.sum(hs(r) * k_bonus * r_k.astype(f32), axis=-1, keepdims=True) * hs(v)
    return (y + bonus.reshape(b, n, RWKV_WIDTH)) * g

def encoder_layer(x, ln_mix_pre, ln_mix_post, ln_ffn_pre, ln_ffn_post, w_in, q_gain, k_gain, shift_mu,
                  w0, w_up, a0, a_up, g_up, k_k, k_a, r_k, lnx_w, lnx_b, w_branch, w_out, w_ffn_in, w_ffn_out):
    dt = x.dtype
    b, n = x.shape[:2]
    h = rms_norm(x, ln_mix_pre)
    u = h @ w_in
    attn = axial_gqa_attention(u[..., OFF_Q:OFF_K], u[..., OFF_K:OFF_V], u[..., OFF_V:OFF_R], q_gain, k_gain)
    z = centred_shift_mix(u[..., OFF_R:OFF_GATE].astype(jnp.float32), shift_mu.astype(jnp.float32))
    rw = rwkv7_bidirectional(z, w0, w_up, a0, a_up, g_up, k_k, k_a, r_k, lnx_w, lnx_b).astype(dt)
    gates = jax.nn.sigmoid(u[..., OFF_GATE:IN_COLS].astype(jnp.float32)).reshape(b, n, N_BRANCH, D_MODEL)
    br = jnp.stack([attn.astype(dt), rw], axis=2)
    br = jnp.einsum('btjc,jcd->btjd', br, w_branch).astype(jnp.float32)
    merged = jnp.sum(gates * br, axis=2).astype(dt)
    x = x + rms_norm(merged @ w_out, ln_mix_post)
    h = rms_norm(x, ln_ffn_pre)
    gu = h @ w_ffn_in
    f = (jax.nn.silu(gu[..., :D_FF]) * gu[..., D_FF:]) @ w_ffn_out
    return x + rms_norm(f, ln_ffn_post)

def setup_inputs(seed: int = 0) -> dict:
    key = jax.random.key(seed)
    ks = jax.random.split(key, 32)
    nrm = lambda k, shape, s: jax.random.normal(k, shape, jnp.float32) * s
    gain = lambda k, shape: 1.0 + 0.05 * jax.random.normal(k, shape, jnp.float32)
    L = DEPTH
    return {
        "x_prompt": nrm(ks[0], (BATCH, SEQ, D_MODEL), 1.0),
        "x_sample": nrm(ks[1], (DEC_BATCH, DEC_SEQ, D_MODEL), 1.0),
        "ln_mix_pre": gain(ks[2], (L, D_MODEL)),
        "ln_mix_post": gain(ks[3], (L, D_MODEL)),
        "ln_ffn_pre": gain(ks[4], (L, D_MODEL)),
        "ln_ffn_post": gain(ks[5], (L, D_MODEL)),
        "w_in": nrm(ks[6], (L, D_MODEL, IN_COLS), D_MODEL ** -0.5),
        "q_gain": gain(ks[7], (L, HEAD_DIM)),
        "k_gain": gain(ks[8], (L, HEAD_DIM)),
        "shift_mu": jax.random.uniform(ks[9], (L, SHIFT_COLS), jnp.float32),
        "w0": jax.random.uniform(ks[10], (L, N_DIR, RWKV_WIDTH), jnp.float32, -6.0, 0.0),
        "w_up": nrm(ks[11], (L, N_DIR, DECAY_LORA, RWKV_WIDTH), 0.5 * DECAY_LORA ** -0.5),
        "a0": nrm(ks[12], (L, N_DIR, RWKV_WIDTH), 0.2),
        "a_up": nrm(ks[13], (L, N_DIR, AAA_LORA, RWKV_WIDTH), 0.2 * AAA_LORA ** -0.5),
        "g_up": nrm(ks[14], (L, GATE_LORA, RWKV_WIDTH), GATE_LORA ** -0.5),
        "k_k": 0.85 + nrm(ks[15], (L, RWKV_WIDTH), 0.05),
        "k_a": gain(ks[16], (L, RWKV_WIDTH)),
        "r_k": nrm(ks[17], (L, RWKV_HEADS, RWKV_HEAD), 0.1),
        "lnx_w": gain(ks[18], (L, RWKV_WIDTH)),
        "lnx_b": nrm(ks[19], (L, RWKV_WIDTH), 0.01),
        "w_branch": nrm(ks[20], (L, N_BRANCH, ATTN_WIDTH, D_MODEL), ATTN_WIDTH ** -0.5),
        "w_out": nrm(ks[21], (L, D_MODEL, D_MODEL), D_MODEL ** -0.5),
        "w_ffn_in": nrm(ks[22], (L, D_MODEL, 2 * D_FF), D_MODEL ** -0.5),
        "w_ffn_out": nrm(ks[23], (L, D_FF, D_MODEL), D_FF ** -0.5),
    }

def reference(x_prompt, x_sample, ln_mix_pre, ln_mix_post, ln_ffn_pre, ln_ffn_post, w_in, q_gain, k_gain,
              shift_mu, w0, w_up, a0, a_up, g_up, k_k, k_a, r_k, lnx_w, lnx_b, w_branch, w_out,
              w_ffn_in, w_ffn_out):
    def trunk(x):
        for l in range(DEPTH):
            x = encoder_layer(x, ln_mix_pre[l], ln_mix_post[l], ln_ffn_pre[l], ln_ffn_post[l], w_in[l],
                              q_gain[l], k_gain[l], shift_mu[l], w0[l], w_up[l], a0[l], a_up[l], g_up[l],
                              k_k[l], k_a[l], r_k[l], lnx_w[l], lnx_b[l], w_branch[l], w_out[l],
                              w_ffn_in[l], w_ffn_out[l])
        return x

    y_prompt = trunk(x_prompt)
    y_sample = trunk(x_sample)
    return (y_prompt, y_sample)


_drawn_inputs = setup_inputs


def setup_inputs(seed=0):
    import zlib

    import numpy as np

    out = dict(_drawn_inputs(seed))
    spreads = {}
    factors = {'q_gain': 8.0, 'k_gain': 8.0, 'w_up': 2.75, 'lnx_b': 26.205, 'k_k': 3.248, 'lnx_w': 3.169}
    for name, (base, spread) in spreads.items():
        noise = np.random.default_rng([zlib.crc32(name.encode()), seed]).standard_normal(out[name].shape)
        drawn = base * np.exp(spread * noise) if base else spread * noise
        out[name] = __import__('jax').numpy.asarray(drawn.astype(out[name].dtype))
    for name, factor in factors.items():
        out[name] = (out[name] * factor).astype(out[name].dtype)
    return out
```

```python
from contextlib import ExitStack

import numpy as np

import concourse.bass as bass
from concourse import mybir

F32 = mybir.dt.float32
F32R = mybir.dt.float32r
ALU = mybir.AluOpType
ACT = mybir.ActivationFunctionType
AX = mybir.AxisListType

P = 128
D = 1024
KD = D // P
N_PROMPT, N_SAMPLE = 1024, 512
N = N_PROMPT + N_SAMPLE
TG = 512
NTG = N // TG
NCH = N // P
HD = 64
HEADS = 8
WIDTH = HEADS * HD
KW = WIDTH // P
D_FF = 2816
KF = D_FF // P
KFH = KF // 2
EPS = 1e-6
LNX_EPS = 64e-5
GRID_W = 64
ROPE_THETA = 10000.0
DECAY_SCALE = float(np.exp(-0.5))

B_Q, B_K, B_V, B_R, B_RK, B_RV, B_WD, B_AD, B_GD = 0, 4, 5, 6, 10, 14, 18, 19, 20
NB_IN = 21


class Arena:

    def __init__(self, nc, ctx, tag):
        self.nc, self.ctx, self.tag = nc, ctx, tag

    def sb(self, name, shape, dt=F32):
        return self.ctx.enter_context(self.nc.sbuf_tensor(f"{self.tag}_{name}", shape, dt))

    def ps(self, name, shape=(P, TG), dt=F32):
        return self.ctx.enter_context(self.nc.psum_tensor(f"{self.tag}_{name}", list(shape), dt))


def product(pe, out, w, x, kt, start=True, stop=True):
    for k in range(kt):
        for part, (a, b) in enumerate(((0, 0), (1, 0), (0, 1))):
            mm = pe.matmul(out, w[a](k), x[b](k), start=start and k == 0 and part == 0,
                           stop=stop and k == kt - 1 and part == 2)
    return mm


def hold(eng, holds):
    eng.sem_inc(holds, 1)


def project(nc, hT, uT, xT, w_in, ln_pre, mu, ones):
    ctx = ExitStack()
    with ctx:
        a = Arena(nc, ctx, "pr")
        sem = lambda name: ctx.enter_context(nc.semaphore("pr_" + name))
        h_hi, h_lo = hT
        NS = 1540
        x_s = a.sb("x", [P, KD, TG])
        h_s = a.sb("h", [P, KD, TG])
        std = a.sb("std", [P, TG])
        rstd = a.sb("rstd", [P, TG])
        ln_s = a.sb("ln", [P, KD])
        mu_s = a.sb("mu", [P, NB_IN])
        mu1 = a.sb("mu1", [P, NB_IN])
        muh = a.sb("muh", [P, NB_IN])
        ones_s = a.sb("ones", [P, P])
        eps_s = a.sb("eps", [P, 1])
        w_s = [a.sb(f"w{i}", [P, KD * P]) for i in range(2)]
        w_hi = [a.sb(f"whi{i}", [P, KD, P], F32R) for i in range(2)]
        w_lo = [a.sb(f"wlo{i}", [P, KD, P], F32R) for i in range(2)]
        u_s = [a.sb(f"u{i}", [P, NS]) for i in range(2)]
        z_s = [a.sb(f"z{i}", [P, NS - 2]) for i in range(2)]
        t_s = a.sb("t", [P, NS - 2])
        banks = [a.ps(f"b{i}") for i in range(8)]

        par_in, x_in = sem("par_in"), sem("x_in")
        squares, sums, stds, rstds, normed = sem("squares"), sem("sums"), sem("stds"), sem("rstds"), sem("normed")
        h_hi_ready, h_lo_ready = sem("h_hi_ready"), sem("h_lo_ready")
        mu_ready, pads_zero = sem("mu_ready"), sem("pads_zero")
        w_loaded = [sem(f"w_loaded{i}") for i in range(2)]
        w_hi_ready, w_lo_ready = sem("w_hi_ready"), sem("w_lo_ready")
        u_product, u_copied, mixed, z_ready = sem("u_product"), sem("u_copied"), sem("mixed"), sem("z_ready")
        z_stored = [sem(f"z_stored{i}") for i in range(2)]
        z_free = [sem(f"z_free{i}") for i in range(2)]
        BODY = 2
        ROUNDS = (NB_IN - 1) // BODY

        with nc.Block() as block:

            @block.sync
            def _(sp):
                sp.dma_start(ones_s[:, :], ones).then_inc(par_in, 16)
                sp.dma_start(ln_s[:, :], ln_pre).then_inc(par_in, 16)
                sp.dma_start(mu_s[:, :], mu).then_inc(par_in, 16)
                for g in range(NTG):
                    if g:
                        sp.wait_ge(normed, g)
                    sp.dma_start(x_s[:, :, :], xT[g]).then_inc(x_in, 16)

                def load(j, slot):
                    sp.wait_ge(w_hi_ready, j + 1)
                    sp.wait_ge(w_lo_ready, j + 1)
                    sp.dma_start(w_s[slot][:, :], w_in[bass.ds(j, 1)].rearrange("a p n -> (a p) n"))\
                        .then_inc(w_loaded[slot], 16)

                with sp.Fori(0, ROUNDS) as i:
                    for s in range(BODY):
                        load(i * BODY + s, s)
                load(NB_IN - 1, 0)

            @block.gpsimd
            def _(pool):
                def store(j, slot, n):
                    pool.wait_ge(z_ready, j + 3)
                    dst = uT[bass.ds(j, 1)].rearrange("a p n -> (a p) n")
                    pool.dma_start(dst[:, 0:N_PROMPT], z_s[slot][:, 0:N_PROMPT]).then_inc(z_stored[slot], 16)
                    pool.dma_start(dst[:, N_PROMPT:N], z_s[slot][:, N_PROMPT + 2:N + 2])\
                        .then_inc(z_stored[slot], 16)
                    pool.wait_ge(z_stored[slot], n)
                    pool.sem_inc(z_free[slot], 1)

                for s in range(BODY):
                    pool.sem_inc(z_free[s], 1)
                with pool.Fori(0, ROUNDS) as i:
                    for s in range(BODY):
                        store(i * BODY + s, s, i * 32 + 32)
                store(NB_IN - 1, 0, 32 * ROUNDS + 32)

            @block.scalar
            def _(act):
                act.sem_inc(w_hi_ready, 2)
                act.sem_inc(u_copied, 2)
                act.wait_ge(pads_zero, 3)
                for g in range(NTG):
                    act.wait_ge(x_in, 16 * (g + 1))
                    if g:
                        act.wait_ge(h_lo_ready, g)
                    act.activation(h_s[:, :, :], x_s[:, :, :], ACT.Square).then_inc(squares, 1)
                    act.wait_ge(sums, g + 1)
                    act.activation(std[:, :], banks[g % 2][:, :], ACT.Sqrt, scale=1.0 / D,
                                   bias=eps_s[:, :]).then_inc(stds, 1)
                    act.wait_ge(normed, g + 1)
                    act.activation(h_hi[:, :, g * TG:(g + 1) * TG], h_s[:, :, :], ACT.Copy).then_inc(h_hi_ready, 1)

                def split(slot, loads, j):
                    act.wait_ge(w_loaded[slot], loads)
                    act.wait_ge(u_product, j + 1)
                    act.activation(w_hi[slot][:, :, :], w_s[slot][:, :].rearrange("p (k n) -> p k n", k=KD),
                                   ACT.Copy).then_inc(w_hi_ready, 1)

                def evacuate(slot, j):
                    act.wait_ge(u_product, j + 3)
                    act.wait_ge(z_ready, j + 1)
                    for g in range(NTG):
                        c = 1 + g * TG + (2 if g == 2 else 0)
                        ins = act.activation(u_s[slot][:, c:c + TG], banks[slot * NTG + g][:, :], ACT.Copy)
                    ins.then_inc(u_copied, 1)

                split(0, 16, 0)
                with act.Fori(0, ROUNDS) as i:
                    split(1, i * 16 + 16, i * BODY + 1)
                    evacuate(0, i * BODY)
                    split(0, i * 16 + 32, i * BODY + 2)
                    evacuate(1, i * BODY + 1)
                evacuate(0, NB_IN - 1)

            @block.vector
            def _(dve):
                dve.sem_inc(w_lo_ready, 2)
                dve.sem_inc(z_ready, 2)
                dve.memset(eps_s[:, :], EPS).then_inc(pads_zero, 1)
                for s in range(2):
                    dve.memset(u_s[s][:, :], 0.0).then_inc(pads_zero, 1)
                dve.wait_ge(par_in, 48)
                dve.tensor_scalar(mu1[:, :], mu_s[:, :], -1.0, 1.0, ALU.mult, ALU.add)
                dve.tensor_scalar(muh[:, :], mu_s[:, :], 0.5, None, ALU.mult).then_inc(mu_ready, 1)
                for g in range(NTG):
                    dve.wait_ge(stds, g + 1)
                    dve.reciprocal(rstd[:, :], std[:, :]).then_inc(rstds, 1)
                    dve.wait_ge(rstds, g + 1)
                    for k in range(KD):
                        ins = dve.scalar_tensor_tensor(out=h_s[:, k, :], in0=x_s[:, k, :], scalar=ln_s[:, k:k + 1],
                                                       in1=rstd[:, :], op0=ALU.mult, op1=ALU.mult)
                    ins.then_inc(normed, 1)
                    dve.wait_ge(normed, g + 1)
                    dve.wait_ge(h_hi_ready, g + 1)
                    dve.tensor_tensor(h_lo[:, :, g * TG:(g + 1) * TG], h_s[:, :, :],
                                      h_hi[:, :, g * TG:(g + 1) * TG].bitcast(F32), ALU.subtract)\
                        .then_inc(h_lo_ready, 1)

                def split(slot, j):
                    dve.wait_ge(w_hi_ready, j + 3)
                    dve.wait_ge(u_product, j + 1)
                    dve.tensor_tensor(w_lo[slot][:, :, :], w_s[slot][:, :].rearrange("p (k n) -> p k n", k=KD),
                                      w_hi[slot][:, :, :].bitcast(F32), ALU.subtract).then_inc(w_lo_ready, 1)

                def shift(slot, j, stored):
                    col = bass.ds(j, 1)
                    dve.wait_ge(u_copied, j + 3)
                    dve.wait_ge(z_free[slot], stored)
                    dve.wait_ge(z_ready, j + 2)
                    dve.tensor_tensor(t_s[:, :], u_s[slot][:, 0:NS - 2], u_s[slot][:, 2:NS], ALU.add)
                    dve.tensor_scalar(z_s[slot][:, :], u_s[slot][:, 1:NS - 1], mu1[:, col], None, ALU.mult)\
                        .then_inc(mixed, 1)
                    dve.wait_ge(mixed, j + 1)
                    dve.scalar_tensor_tensor(out=z_s[slot][:, :], in0=t_s[:, :], scalar=muh[:, col],
                                             in1=z_s[slot][:, :], op0=ALU.mult, op1=ALU.add).then_inc(z_ready, 1)

                dve.wait_ge(mu_ready, 1)
                split(0, 0)
                with dve.Fori(0, ROUNDS) as i:
                    split(1, i * BODY + 1)
                    shift(0, i * BODY, i + 1)
                    split(0, i * BODY + 2)
                    shift(1, i * BODY + 1, i + 1)
                shift(0, NB_IN - 1, ROUNDS + 1)

            @block.tensor
            def _(pe):
                pe.sem_inc(u_product, 2)
                pe.wait_ge(par_in, 48)
                for g in range(NTG):
                    pe.wait_ge(squares, g + 1)
                    if g >= 2:
                        pe.wait_ge(stds, g - 1)
                    for k in range(KD):
                        mm = pe.matmul(banks[g % 2][:, :], ones_s[:, :], h_s[:, k, :],
                                       start=k == 0, stop=k == KD - 1)
                    mm.then_inc(sums, 1)
                pe.wait_ge(stds, NTG)
                pe.wait_ge(h_lo_ready, NTG)

                def multiply(slot, j, copied):
                    pe.wait_ge(w_lo_ready, j + 3)
                    pe.wait_ge(w_hi_ready, j + 3)
                    pe.wait_ge(u_copied, copied)
                    for g in range(NTG):
                        t = slice(g * TG, (g + 1) * TG)
                        mm = product(pe, banks[slot * NTG + g][:, :],
                                     (lambda k: w_hi[slot][:, k, :], lambda k: w_lo[slot][:, k, :]),
                                     (lambda k: h_hi[:, k, t], lambda k: h_lo[:, k, t]), KD)
                    mm.then_inc(u_product, 1)

                with pe.Fori(0, ROUNDS) as i:
                    for s in range(BODY):
                        multiply(s, i * BODY + s, i * BODY + s + 1)
                multiply(0, NB_IN - 1, NB_IN)


def rope(nc, qkT, uT, gains, cos, sin, headsum, swap):
    ctx = ExitStack()
    with ctx:
        a = Arena(nc, ctx, "ro")
        sem = lambda name: ctx.enter_context(nc.semaphore("ro_" + name))
        NB = B_V
        q_s = [a.sb(f"q{i}", [P, N]) for i in range(2)]
        sq_s = a.sb("sq", [P, N])
        std = a.sb("std", [P, N])
        n_s = a.sb("n", [P, N])
        c_s = a.sb("c", [P, N])
        o_s = a.sb("o", [P, N])
        cos_s, sin_s = a.sb("cos", [P, N]), a.sb("sin", [P, N])
        g_s = a.sb("g", [P, NB])
        sum_s, swap_s, eps_s = a.sb("sum", [P, P]), a.sb("swap", [P, P]), a.sb("eps", [P, 1])
        sum_ps, rot_ps = a.ps("sums", [P, N]), a.ps("rot", [P, N])
        par_in, eps_set, q_in = sem("par_in"), sem("eps_set"), [sem("q_in0"), sem("q_in1")]
        squares, sums, stds, inverted, normed = sem("squares"), sem("sums"), sem("stds"), sem("inverted"), sem("normed")
        rotated, with_cos, with_sin, summed, stored = (
            sem("rotated"), sem("with_cos"), sem("with_sin"), sem("summed"), sem("stored"))

        with nc.Block() as block:

            @block.sync
            def _(sp):
                for tile, src in ((sum_s, headsum), (swap_s, swap), (g_s, gains), (cos_s, cos), (sin_s, sin)):
                    sp.dma_start(tile[:, :], src).then_inc(par_in, 16)
                for b in range(NB):
                    if b >= 2:
                        sp.wait_ge(normed, b - 1)
                    sp.dma_start(q_s[b % 2][:, :], uT[b]).then_inc(q_in[b % 2], 16)

            @block.gpsimd
            def _(pool):
                for b in range(NB):
                    pool.wait_ge(summed, b + 1)
                    pool.dma_start(qkT[b * P:(b + 1) * P, :], o_s[:, :]).then_inc(stored, 16)
                    pool.wait_ge(stored, 16 * (b + 1))

            @block.scalar
            def _(act):
                act.wait_ge(eps_set, 1)
                for b in range(NB):
                    act.wait_ge(q_in[b % 2], 16 * (b // 2 + 1))
                    if b:
                        act.wait_ge(sums, 3 * b)
                    act.activation(sq_s[:, :], q_s[b % 2][:, :], ACT.Square).then_inc(squares, 1)
                    if b:
                        act.wait_ge(normed, b)
                    for g in range(NTG):
                        act.wait_ge(sums, 3 * b + g + 1)
                        t = slice(g * TG, (g + 1) * TG)
                        act.activation(std[:, t], sum_ps[:, t], ACT.Sqrt, scale=1.0 / HD, bias=eps_s[:, :])\
                            .then_inc(stds, 1)

            @block.vector
            def _(dve):
                dve.memset(eps_s[:, :], EPS).then_inc(eps_set, 1)
                dve.wait_ge(par_in, 80)
                for b in range(NB):
                    dve.wait_ge(stds, 3 * b + 3)
                    dve.reciprocal(std[:, :], std[:, :]).then_inc(inverted, 1)
                    dve.wait_ge(inverted, b + 1)
                    if b:
                        dve.wait_ge(rotated, 3 * b)
                        dve.wait_ge(with_cos, b)
                    dve.scalar_tensor_tensor(out=n_s[:, :], in0=q_s[b % 2][:, :], scalar=g_s[:, b:b + 1],
                                             in1=std[:, :], op0=ALU.mult, op1=ALU.mult).then_inc(normed, 1)
                    dve.wait_ge(normed, b + 1)
                    if b:
                        dve.wait_ge(summed, b)
                        dve.wait_ge(stored, 16 * b)
                    dve.tensor_tensor(c_s[:, :], n_s[:, :], cos_s[:, :], ALU.mult).then_inc(with_cos, 1)
                    for g in range(NTG):
                        t = slice(g * TG, (g + 1) * TG)
                        dve.wait_ge(rotated, 3 * b + g + 1)
                        ins = dve.tensor_tensor(o_s[:, t], rot_ps[:, t], sin_s[:, t], ALU.mult)
                    ins.then_inc(with_sin, 1)
                    dve.wait_ge(with_sin, b + 1)
                    dve.wait_ge(with_cos, b + 1)
                    dve.tensor_tensor(o_s[:, :], o_s[:, :], c_s[:, :], ALU.add).then_inc(summed, 1)

            @block.tensor
            def _(pe):
                pe.wait_ge(par_in, 80)
                for b in range(NB):
                    pe.wait_ge(squares, b + 1)
                    if b:
                        pe.wait_ge(stds, 3 * b)
                    for g in range(NTG):
                        t = slice(g * TG, (g + 1) * TG)
                        pe.matmul(sum_ps[:, t], sum_s[:, :], sq_s[:, t], start=True, stop=True).then_inc(sums, 1)
                    pe.wait_ge(normed, b + 1)
                    if b:
                        pe.wait_ge(with_sin, b)
                    for g in range(NTG):
                        t = slice(g * TG, (g + 1) * TG)
                        pe.matmul(rot_ps[:, t], swap_s[:, :], n_s[:, t], start=True, stop=True).then_inc(rotated, 1)


def attention(nc, attnT, qkT, uT, ident, t0, n, tag):
    ctx = ExitStack()
    with ctx:
        a = Arena(nc, ctx, tag)
        sem = lambda name: ctx.enter_context(nc.semaphore(f"{tag}_{name}"))
        NT, NG = n // P, n // TG
        NU = NT * NG
        SCALE = HD ** -0.5
        q_s = [a.sb(f"q{i}", [P, n]) for i in range(2)]
        k_s = [a.sb(f"k{i}", [P, n]) for i in range(2)]
        v_s = a.sb("v", [P, n])
        va = a.sb("va", [P, NT, 2, P])
        e_s = a.sb("e", [P, NT, n])
        vh = [a.sb(f"vh{i}", [P, NT, P]) for i in range(2)]
        o_s = [a.sb(f"o{i}", [HD, n]) for i in range(2)]
        mx = [a.sb(f"mx{i}", [P, NT]) for i in range(2)]
        mrow = [a.sb(f"mrow{i}", [NT, P]) for i in range(2)]
        rec = a.sb("rec", [HD, TG])
        id_s = a.sb("id", [P, P])
        first = [a.ps(f"first{i}", [P, NG * TG]) for i in range(2)]
        second = [a.ps(f"second{i}") for i in range(2)]
        third = [a.ps(f"third{i}") for i in range(2)]

        par_in, v_in, ones_set = sem("par_in"), sem("v_in"), sem("ones_set")
        v_turned, va_ready = sem("v_turned"), sem("va_ready")
        q_in, k_in = [sem("q_in0"), sem("q_in1")], [sem("k_in0"), sem("k_in1")]
        row_zero, row_in = sem("row_zero"), [sem("row_in0"), sem("row_in1")]
        scored, max_ready, max_turned, mrow_ready = sem("scored"), sem("max_ready"), sem("max_turned"), sem("mrow_ready")
        shifted, exp_ready, summed, norm_step = sem("shifted"), sem("exp_ready"), sem("summed"), sem("norm_step")
        vh_ready, o_stored, o_free = sem("vh_ready"), [sem("o_stored0"), sem("o_stored1")], sem("o_free")

        def heads(first_stage, second_stage):
            def both(eng):
                first_stage(0, 0, 0)
                with eng.Fori(0, HEADS // 2 - 1) as i:
                    first_stage(i * 2 + 1, 1, i)
                    second_stage(i * 2, 0, i)
                    first_stage(i * 2 + 2, 0, i + 1)
                    second_stage(i * 2 + 1, 1, i)
                last = HEADS // 2 - 1
                first_stage(HEADS - 1, 1, last)
                second_stage(HEADS - 2, 0, last)
                second_stage(HEADS - 1, 1, last)
            return both

        with nc.Block() as block:

            @block.sync
            def _(sp):
                sp.dma_start(id_s[:, :], ident).then_inc(par_in, 16)
                sp.dma_start(v_s[:, :], uT[B_V][:, t0:t0 + n]).then_inc(v_in, 16)

                def load(h, s, i):
                    sp.wait_ge(shifted, h * NU + NU)
                    sp.dma_start(q_s[s][0:HD, :], qkT[bass.ds(h * HD, HD), t0:t0 + n]).then_inc(q_in[s], 16)
                    kv = h // 4
                    sp.dma_start(k_s[s][0:HD, :], qkT[bass.ds(kv * HD + WIDTH, HD), t0:t0 + n])\
                        .then_inc(k_in[s], 16)

                def load_row(h, s, i):
                    sp.wait_ge(mrow_ready, h + 2)
                    sp.dma_start(q_s[s][HD:HD + 1, :].rearrange("a (t p) -> a t p", p=P), mrow[s][:, :])\
                        .then_inc(row_in[s], 16)

                load(0, 0, 0)
                load_row(0, 0, 0)
                with sp.Fori(0, HEADS // 2 - 1) as i:
                    load(i * 2 + 1, 1, i)
                    load_row(i * 2 + 1, 1, i)
                    load(i * 2 + 2, 0, i)
                    load_row(i * 2 + 2, 0, i)
                load(HEADS - 1, 1, 0)
                load_row(HEADS - 1, 1, 0)

            @block.gpsimd
            def _(pool):
                def values(h, s, i):
                    kv = h // 4
                    pool.wait_ge(summed, h * NG + NG)
                    pool.tensor_copy(vh[s][:, :, :], va[:, :, bass.ds(kv, 1), :].rearrange("p t a c -> p t (a c)"))\
                        .then_inc(vh_ready, 1)

                def store(h, s, i):
                    pool.wait_ge(norm_step, h * 2 * NG + 2 * NG + 2)
                    pool.dma_start(attnT[bass.ds(h * HD, HD), t0:t0 + n], o_s[s][:, :]).then_inc(o_stored[s], 16)
                    pool.wait_ge(o_stored[s], i * 16 + 16)
                    pool.sem_inc(o_free, 1)

                pool.sem_inc(o_free, 2)
                pool.wait_ge(va_ready, NT)
                heads(values, store)(pool)

            @block.scalar
            def _(act):
                def exponents(h, s, i):
                    for u in range(NU):
                        kt, g = u // NG, u % NG
                        act.wait_ge(shifted, h * NU + 2 * NU + u + 1)
                        act.activation(e_s[:, kt, g * TG:(g + 1) * TG], second[u % 2][:, :], ACT.Exp, scale=SCALE)\
                            .then_inc(exp_ready, 1)

                act.sem_inc(exp_ready, 2)
                heads(lambda *_: None, exponents)(act)

            @block.vector
            def _(dve):
                dve.sem_inc(mrow_ready, 1)
                dve.sem_inc(max_ready, 2)
                dve.sem_inc(norm_step, 2)
                for s in range(2):
                    dve.memset(k_s[s][HD:P, :], 0.0)
                    dve.memset(q_s[s][HD:P, :], 0.0)
                dve.memset(va[:, :, :, :], 1.0).then_inc(ones_set, 1)
                dve.wait_ge(ones_set, 1)
                for s in range(2):
                    dve.memset(k_s[s][HD:HD + 1, :], 1.0).then_inc(ones_set, 1)
                for t in range(NT):
                    dve.wait_ge(v_turned, t + 1)
                    dve.tensor_copy(va[:, t, :, 0:HD],
                                    third[t % 2][:, 0:P].rearrange("p (a b) -> p a b", a=2)).then_inc(va_ready, 1)

                def maxima(h, s, i):
                    dve.wait_ge(shifted, h * NU + NU)
                    dve.memset(q_s[s][HD:HD + 1, :], 0.0).then_inc(row_zero, 1)
                    for t in range(NT):
                        dve.wait_ge(scored, h * NT + t + 1)
                        dve.tensor_reduce(mx[s][:, t:t + 1], first[t % 2][:, :], AX.X, ALU.max).then_inc(max_ready, 1)
                    dve.wait_ge(max_turned, h + 1)
                    dve.tensor_scalar(mrow[s][:, :], first[0][0:NT, 0:P], -1.0, None, ALU.mult)\
                        .then_inc(mrow_ready, 1)

                def normalise(h, s, i):
                    dve.wait_ge(o_free, h + 1)
                    for g in range(NG):
                        n0 = h * 2 * NG + 2 * g + 2
                        dve.wait_ge(summed, h * NG + 2 * NG + g + 1)
                        dve.wait_ge(norm_step, n0)
                        dve.reciprocal(rec[:, :], third[g % 2][HD:P, :]).then_inc(norm_step, 1)
                        dve.wait_ge(norm_step, n0 + 1)
                        dve.tensor_tensor(o_s[s][:, g * TG:(g + 1) * TG], third[g % 2][0:HD, :], rec[:, :],
                                          ALU.mult).then_inc(norm_step, 1)

                dve.wait_ge(ones_set, 3)
                heads(maxima, normalise)(dve)

            @block.tensor
            def _(pe):
                pe.sem_inc(shifted, 2 * NU)
                pe.sem_inc(summed, 2 * NG)
                pe.wait_ge(par_in, 16)
                pe.wait_ge(v_in, 16)
                for t in range(NT):
                    if t >= 2:
                        pe.wait_ge(va_ready, t - 1)
                    pe.transpose(third[t % 2][:, 0:P], v_s[:, t * P:(t + 1) * P], id_s[:, :]).then_inc(v_turned, 1)
                pe.wait_ge(va_ready, NT)

                def scores(h, s, i):
                    pe.wait_ge(q_in[s], i * 16 + 16)
                    pe.wait_ge(k_in[s], i * 16 + 16)
                    pe.wait_ge(row_zero, h + 1)
                    pe.wait_ge(mrow_ready, h + 1)
                    for t in range(NT):
                        pe.wait_ge(max_ready, h * NT + t + 1)
                        for g in range(NG):
                            mm = pe.matmul(first[t % 2][:, g * TG:(g + 1) * TG], q_s[s][:, t * P:(t + 1) * P],
                                           k_s[s][:, g * TG:(g + 1) * TG], start=True, stop=True)
                        mm.then_inc(scored, 1)

                def turn_maxima(h, s):
                    pe.wait_ge(max_ready, h * NT + NT + 2)
                    pe.transpose(first[0][0:NT, 0:P], mx[s][:, :], id_s[:, :]).then_inc(max_turned, 1)

                def shifted_scores(h, s, i):
                    pe.wait_ge(row_in[s], i * 16 + 16)
                    for u in range(NU):
                        kt, g = u // NG, u % NG
                        pe.wait_ge(exp_ready, h * NU + u + 1)
                        pe.matmul(second[u % 2][:, :], k_s[s][:, kt * P:(kt + 1) * P],
                                  q_s[s][:, g * TG:(g + 1) * TG], start=True, stop=True).then_inc(shifted, 1)

                def with_values(h, s, i):
                    pe.wait_ge(vh_ready, h + 1)
                    for g in range(NG):
                        pe.wait_ge(norm_step, h * 2 * NG + 2)
                        for kt in range(NT):
                            if g == 0:
                                pe.wait_ge(exp_ready, h * NU + (kt + 1) * NG + 2)
                            mm = pe.matmul(third[g % 2][:, :], vh[s][:, kt, :], e_s[:, kt, g * TG:(g + 1) * TG],
                                           start=kt == 0, stop=kt == NT - 1)
                        mm.then_inc(summed, 1)

                def first_stage(h, s, i):
                    scores(h, s, i)
                    if isinstance(h, int) and h == 0:
                        turn_maxima(h, s)

                def second_stage(h, s, i):
                    shifted_scores(h, s, i)
                    if not (isinstance(h, int) and h == HEADS - 1):
                        turn_maxima(h + 1, 1 - s)
                    with_values(h, s, i)

                heads(first_stage, second_stage)(pe)

LEVELS = 6
PAIRS = KW


class Steps:

    def __init__(self, sem, names):
        self.sem, self.names, self.n = sem, names, len(names)
        self.at = {name: i + 1 for i, name in enumerate(names)}
        self.next = 0

    def start(self, eng):
        eng.sem_inc(self.sem, self.n)

    def value(self, rnd, name):
        return rnd * self.n + self.n + self.at[name]

    def last(self, rnd, name):
        return rnd * self.n + self.at[name]

    def whole(self, rounds):
        return rounds * self.n + self.n

    def done(self, ins, name):
        assert self.names[self.next % self.n] == name, (name, self.names[self.next % self.n])
        self.next += 1
        ins.then_inc(self.sem, 1)


def recurrence(nc, y_out, bonusT, gT, uT, w_up, a_up, g_up, par, consts):
    ctx = ExitStack()
    with ctx:
        a = Arena(nc, ctx, "rw")
        sem = lambda name: ctx.enter_context(nc.semaphore("rw_" + name))
        C = DECAY_SCALE
        NPAR = 9
        K_K, K_A, R_K, W0, A0 = 0, 1, 2, 3, 5
        wd_s, ad_s, gd_s = (a.sb(n, [P, N]) for n in ("wd", "ad", "gd"))
        par_s = a.sb("par", [P, NPAR, PAIRS])
        rkh_s, ka1_s = a.sb("rkh", [P, PAIRS]), a.sb("ka1", [P, PAIRS])
        hs_s, id_s = a.sb("hs", [P, P]), a.sb("id", [P, P])
        restart_s = a.sb("restart", [P, TG])
        causal_s, pair_s = a.sb("causal", [P, 2, 4 * P]), a.sb("pair", [P, 2, 2 * P])
        id2_s, level_s = a.sb("id2", [P, 2 * P]), a.sb("level", [P, 2, LEVELS, P])
        wup_s, aup_s, gup_s = a.sb("wup", [P, 2, P]), a.sb("aup", [P, 2, P]), a.sb("gup", [P, P])
        r_s, k_s, v_s = (a.sb(n, [P, TG]) for n in ("r", "k", "v"))
        bo_s, gt_s = (a.sb(n, [P, TG]) for n in ("bo", "gt"))
        x_s = [a.sb(f"x{d}", [P, 4, N]) for d in range(2)]
        mid_s, end_s, scale_s = (a.sb(n, [P, 2, NCH]) for n in ("mid", "end", "scale"))
        vt_s, vp_s = a.sb("vt", [P, NCH, P]), a.sb("vp", [P, NCH, 2, P])
        y_s = a.sb("y", [P, NCH, WIDTH])
        G = [(u, d) for u in range(2) for d in range(2)]
        st_s = [a.sb(f"st{g}", [P, 4, P]) for g in range(4)]
        pad_s = [a.sb(f"pad{g}", [P, 4, P]) for g in range(4)]
        with ExitStack() as shared:
            b = Arena(nc, shared, "rw")
            kk_s, t_s, kb_s, sq_s = (b.sb(n, [P, TG]) for n in ("kk", "t", "kb", "sq"))
            sig_s, al_s, cum_s = ([b.sb(f"{n}{d}", [P, TG]) for d in range(2)] for n in ("sig", "al", "cum"))
            e_s = [b.sb(f"e{i}", [P, TG]) for i in range(3)]
        ab_s = [a.sb(f"ab{g}", [P, 4 * P]) for g in range(4)]
        ak_s = [a.sb(f"ak{g}", [P, 4 * P]) for g in range(4)]
        bk_s = [a.sb(f"bk{g}", [P, 2 * P]) for g in range(4)]
        X = [a.sb(f"X{g}", [P, 2 * P]) for g in range(4)]
        Z = [a.sb(f"Z{g}", [P, 2 * P]) for g in range(4)]
        T = [a.sb(f"T{g}", [P, 2 * P]) for g in range(4)]
        p_s = [a.sb(f"p{d}", [P, P]) for d in range(2)]
        up_s = [a.sb(f"up{d}", [P, 2, P]) for d in range(2)]
        uf_s = [a.sb(f"uf{d}", [P, P]) for d in range(2)]
        S = [a.sb(f"S{d}", [P, P]) for d in range(2)]
        banks = [a.ps(f"b{i}") for i in range(8)]
        SC, INV, SN = banks[0:2], banks[2:6], banks[6:8]

        const_in, lora_in, w_in = sem("const_in"), sem("lora_in"), sem("w_in")
        r_in, k_in, v_in = sem("r_in"), sem("k_in"), sem("v_in")
        bonus_stored, g_stored, y_stored = sem("bonus_stored"), sem("g_stored"), sem("y_stored")
        zeroed, lora_ready, scales_done, par_ready = sem("zeroed"), sem("lora_ready"), sem("scales_done"), sem("par_ready")
        exps_done, holds = sem("exps_done"), [sem("hold0"), sem("hold1")]

        dve_prep = Steps(sem("dve_prep"), [
            "kkraw", "clamp", "invert", "kk", *(f"{n}{d}" for d in range(2) for n in ("cum", "mid", "end")),
            *(f"{n}{d}" for d in range(2) for n in ("kfac", "kdir", "kka")), "kb", "rb", "bonus",
            "vp0", "vp1",
            *(f"{n}{d}" for d in range(2) for n in ("centre", "before", "xr", "xa", "xb", "xk"))])
        act_prep = Steps(sem("act_prep"), [
            "sig0", "sig1", "al0", "al1", "square", "norm", "g", "vt",
            *(f"{n}{d}" for d in range(2) for n in ("er", "ea", "eb"))])
        pe_prep = Steps(sem("pe_prep"), ["xw0", "xw1", "xa0", "xa1", "xg", "sumsq", "turnv", "sumrb"])
        pool_round = Steps(sem("pool_round"), [f"st{g}" for g in range(4)])
        act_round = Steps(sem("act_round"), [
            *(f"pad{h}_{g}" for g in range(4) for h in range(2)),
            *(f"bk{g}" for g in range(4)), *(f"X{g}" for g in range(4)),
            *(f"Z{n}_{g}" for n in range(LEVELS) for g in range(4)),
            *(f"{n}_{u}{d}" for u in range(2) for n in ("p", "uf", "S0", "S1") for d in range(2))])
        dve_round = Steps(sem("dve_round"), [
            *(f"{n}{g}" for g in range(4) for n in ("ab", "ak")),
            *(f"Zp{g}" for g in range(4)), *(f"Z{g}" for g in range(4)),
            *(f"{n}{l}_{g}" for l in range(LEVELS) for n in ("T", "X") for g in range(4)),
            *(f"{n}_{u}{d}" for u in range(2) for n in ("up", "y") for d in range(2))])
        pe_round = Steps(sem("pe_round"), [
            *(f"{n}{g}" for g in range(4) for n in ("ab", "ak")), *(f"bk{g}" for g in range(4)),
            *(f"X{g}" for g in range(4)),
            *(f"{n}{l}_{g}" for l in range(LEVELS) for n in ("T", "X", "Z") for g in range(4)),
            *(f"{n}_{u}{d}" for u in range(2) for n in ("p", "u", "ys") for d in range(2))])

        def both(eng, prep, middle, rnd):
            with eng.Fori(0, PAIRS) as p:
                with eng.Fori(0, NTG) as g:
                    prep(p, g, p * NTG + g)
                middle(p)
                with eng.Fori(0, 4) as i:
                    rnd(p, p * 6 + i, (i * 2, i * (-2) + 7))
                with eng.Fori(0, 2) as i:
                    rnd(p, p * 6 + 4 + i, (i * 2 + 8, i * (-2) + 11))

        def chunk(cs, g):
            u, d = G[g]
            return cs[d] + (u if d == 0 else -u)

        def nothing(*_):
            pass

        with nc.Block() as block:

            @block.sync
            def _(sp):
                for tile, src in ((par_s, par), (hs_s, consts["headsum"]), (id_s, consts["ident"]),
                                  (restart_s, consts["restart"]), (id2_s, consts["ident2"])):
                    sp.dma_start(tile[:], src).then_inc(const_in, 16)
                for tile, src in ((causal_s, consts["causal"]), (pair_s, consts["pair"])):
                    sp.dma_start(tile[:, :, :], src.rearrange("d p n -> p d n")).then_inc(const_in, 16)
                for d in range(2):
                    sp.dma_start(level_s[:, d, :, :], consts["levels"][d].rearrange("l p n -> p l n"))\
                        .then_inc(const_in, 16)
                for tile, b in ((wd_s, B_WD), (ad_s, B_AD), (gd_s, B_GD)):
                    sp.dma_start(tile[:, :], uT[b]).then_inc(lora_in, 16)
                sp.sem_inc(bonus_stored, 16)
                sp.sem_inc(g_stored, 16)
                sp.wait_ge(zeroed, 1)

                def prep(p, g, it):
                    t = bass.ds(g * TG, TG)
                    sp.wait_ge(dve_prep.sem, dve_prep.whole(it))
                    sp.wait_ge(pe_prep.sem, pe_prep.whole(it))
                    for tile, b, s in ((r_s, B_R, r_in), (k_s, B_RK, k_in), (v_s, B_RV, v_in)):
                        sp.dma_start(tile[:, :], uT[bass.ds(p + b, 1), :, t].rearrange("a p n -> (a p) n"))\
                            .then_inc(s, 16)
                    dst = lambda z: z[bass.ds(p, 1), :, t].rearrange("a p n -> (a p) n")
                    sp.wait_ge(act_prep.sem, act_prep.value(it, "g"))
                    sp.dma_start(dst(gT), gt_s[:, :]).then_inc(g_stored, 16)
                    sp.wait_ge(dve_prep.sem, dve_prep.value(it, "bonus"))
                    sp.dma_start(dst(bonusT), bo_s[:, :]).then_inc(bonus_stored, 16)

                with sp.Fori(0, PAIRS) as p:
                    sp.wait_ge(pe_prep.sem, pe_prep.whole(p * NTG))
                    for src, tile in ((w_up, wup_s), (a_up, aup_s)):
                        for d in range(2):
                            h = slice(d * HD, (d + 1) * HD)
                            sp.dma_start(tile[h, d, :], src[bass.ds(p, 1), h, :].rearrange("a p n -> (a p) n"))\
                                .then_inc(w_in, 16)
                    sp.dma_start(gup_s[:, :], g_up[bass.ds(p, 1)].rearrange("a p n -> (a p) n")).then_inc(w_in, 16)
                    with sp.Fori(0, NTG) as g:
                        prep(p, g, p * NTG + g)
                sp.wait_ge(dve_round.sem, dve_round.whole(PAIRS * 6))
                sp.dma_start(y_out, y_s[:, :, :]).then_inc(y_stored, 16)
                sp.wait_ge(y_stored, 16)
                sp.wait_ge(bonus_stored, 16 * (PAIRS * NTG + 1))
                sp.wait_ge(g_stored, 16 * (PAIRS * NTG + 1))

            @block.gpsimd
            def _(pool):
                pool_round.start(pool)

                def rnd(p, it, cs):
                    for g, (u, d) in enumerate(G):
                        pool.wait_ge(pe_round.sem, pe_round.last(it, f"ys_{u}{d}"))
                        pool.wait_ge(act_round.sem, act_round.last(it, f"pad1_{g}"))
                        pool_round.done(pool.tensor_copy(st_s[g][:, :, :],
                                                         x_s[d][:, :, bass.ds(chunk(cs, g) * P, P)]), f"st{g}")

                def middle(p):
                    pool.wait_ge(dve_prep.sem, dve_prep.whole((p + 1) * NTG))
                    hold(pool, holds[0])

                both(pool, nothing, middle, rnd)

            @block.scalar
            def _(act):
                act_prep.start(act)
                act_round.start(act)
                act.wait_ge(lora_in, 48)
                act.activation(wd_s[:, :], wd_s[:, :], ACT.Tanh).then_inc(lora_ready, 1)
                act.activation(gd_s[:, :], gd_s[:, :], ACT.Sigmoid).then_inc(lora_ready, 1)
                act.wait_ge(const_in, 16 * 9)
                act.wait_ge(zeroed, 1)
                par = lambda n, p: par_s[:, n, bass.ds(p, 1)]

                def prep(p, g, it):
                    act.wait_ge(dve_prep.sem, dve_prep.whole(it))
                    for d in range(2):
                        act.wait_ge(pe_prep.sem, pe_prep.value(it, f"xw{d}"))
                        act_prep.done(act.activation(sig_s[d][:, :], banks[d][:, :], ACT.Sigmoid, bias=par(W0 + d, p)),
                                      f"sig{d}")
                    for d in range(2):
                        act.wait_ge(pe_prep.sem, pe_prep.value(it, f"xa{d}"))
                        act_prep.done(act.activation(al_s[d][:, :], banks[2 + d][:, :], ACT.Sigmoid,
                                                     bias=par(A0 + d, p)), f"al{d}")
                    act.wait_ge(dve_prep.sem, dve_prep.value(it, "kkraw"))
                    act.wait_ge(pe_prep.sem, pe_prep.whole(it))
                    act_prep.done(act.activation(sq_s[:, :], kk_s[:, :], ACT.Square), "square")
                    act.wait_ge(pe_prep.sem, pe_prep.value(it, "sumsq"))
                    act_prep.done(act.activation(t_s[:, :], banks[5][:, :], ACT.Sqrt), "norm")
                    act.wait_ge(g_stored, it * 16 + 16)
                    act_prep.done(act.activation(gt_s[:, :], banks[4][:, :], ACT.Copy), "g")
                    act.wait_ge(pe_prep.sem, pe_prep.value(it, "turnv"))
                    act_prep.done(act.activation(vt_s[:, bass.ds(g * 4, 4), :].rearrange("p a b -> p (a b)"),
                                                 banks[7][:, :], ACT.Copy), "vt")
                    for d in range(2):
                        at, before = cum_s[d], sig_s[d]
                        act.wait_ge(dve_prep.sem, dve_prep.value(it, f"before{d}"))
                        for n, (src, scale) in enumerate(((at, -C), (before, -C), (at, C)) if d == 0 else
                                                         ((before, C), (at, C), (before, -C))):
                            if d:
                                act.wait_ge(dve_prep.sem, dve_prep.value(it, ("xr0", "xa0", "xk0")[n]))
                            act_prep.done(act.activation(e_s[n][:, :], src[:, :], ACT.Exp, scale=scale),
                                          ("er", "ea", "eb")[n] + str(d))

                def middle(p):
                    act.wait_ge(scales_done, p * 2 + 1)
                    for n in (mid_s, end_s):
                        act.activation(n[:, :, :], n[:, :, :], ACT.Exp, scale=-C).then_inc(exps_done, 1)
                    act.wait_ge(scales_done, p * 2 + 2)

                def rnd(p, it, cs):
                    for g, (u, d) in enumerate(G):
                        c = chunk(cs, g)
                        act.wait_ge(pool_round.sem, pool_round.value(it, f"st{g}"))
                        act.wait_ge(pe_round.sem, pe_round.last(it, f"ak{g}"))
                        for h in range(2):
                            r = slice(h * HD, (h + 1) * HD)
                            act_round.done(act.activation(pad_s[g][r, h::2, :], st_s[g][r, 0:2, :], ACT.Copy),
                                           f"pad{h}_{g}")
                    for g, (u, d) in enumerate(G):
                        act.wait_ge(pe_round.sem, pe_round.value(it, f"bk{g}"))
                        act_round.done(act.activation(bk_s[g][:, :], INV[g][:, 0:2 * P], ACT.Copy), f"bk{g}")
                    for g in range(4):
                        act.wait_ge(pe_round.sem, pe_round.value(it, f"X{g}"))
                        act.wait_ge(dve_round.sem, dve_round.last(it, f"X{LEVELS - 1}_{g}"))
                        act_round.done(act.activation(X[g][:, :], INV[g][:, 2 * P:4 * P], ACT.Copy), f"X{g}")
                    for n in range(LEVELS):
                        for g in range(4):
                            act.wait_ge(pe_round.sem, pe_round.value(it, f"Z{n}_{g}"))
                            act_round.done(act.activation(Z[g][:, :], INV[g][:, 0:2 * P], ACT.Copy), f"Z{n}_{g}")
                    for u in range(2):
                        for d in range(2):
                            act.wait_ge(pe_round.sem, pe_round.value(it, f"p_{u}{d}"))
                            act_round.done(act.activation(p_s[d][:, :], SN[d][:, 0:P], ACT.Copy), f"p_{u}{d}")
                        for d in range(2):
                            act.wait_ge(dve_round.sem, dve_round.value(it, f"up_{u}{d}"))
                            act_round.done(act.activation(
                                uf_s[d][:, :].rearrange("p (h n) -> p h n", h=2),
                                bass_diag(SN[d][:, P:3 * P]), ACT.Copy), f"uf_{u}{d}")
                        for h in range(2):
                            for d in range(2):
                                r = slice(h * HD, (h + 1) * HD)
                                if h == 0:
                                    act.wait_ge(pe_round.sem, pe_round.value(it, f"ys_{u}{d}"))
                                c = chunk(cs, u * 2 + d)
                                act_round.done(act.activation(S[d][r, r], SN[d][r, r], ACT.Copy,
                                                              scale=scale_s[r, d, bass.ds(c, 1)]), f"S{h}_{u}{d}")

                both(act, prep, middle, rnd)

            @block.vector
            def _(dve):
                dve_prep.start(dve)
                dve_round.start(dve)
                for tile in (wup_s, aup_s, vp_s, y_s, *pad_s, *up_s, *S):
                    ins = dve.memset(tile[:], 0.0)
                ins.then_inc(zeroed, 1)
                dve.wait_ge(zeroed, 1)
                dve.wait_ge(const_in, 16 * 9)
                dve.tensor_scalar(rkh_s[:, :], par_s[:, R_K, :], 0.5, None, ALU.mult)
                dve.tensor_scalar(ka1_s[:, :], par_s[:, K_A, :], -1.0, 1.0, ALU.mult, ALU.add).then_inc(par_ready, 1)
                dve.wait_ge(par_ready, 1)
                par = lambda n, p: par_s[:, n, bass.ds(p, 1)]
                chunks = lambda tile: tile[:, :].rearrange("p (c n) -> p c n", n=P)

                def prep(p, g, it):
                    def own(name):
                        dve.wait_ge(dve_prep.sem, dve_prep.value(it, name))

                    def act_did(name):
                        dve.wait_ge(act_prep.sem, act_prep.value(it, name))

                    done = dve_prep.done
                    t = bass.ds(g * TG, TG)
                    dve.wait_ge(k_in, it * 16 + 16)
                    dve.wait_ge(dve_prep.sem, dve_prep.whole(it))
                    done(dve.tensor_scalar(kk_s[:, :], k_s[:, :], par(K_K, p), None, ALU.mult), "kkraw")
                    act_did("norm")
                    done(dve.tensor_scalar(t_s[:, :], t_s[:, :], 1e-12, None, ALU.max), "clamp")
                    own("clamp")
                    done(dve.reciprocal(t_s[:, :], t_s[:, :]), "invert")
                    own("invert")
                    done(dve.tensor_tensor(kk_s[:, :], kk_s[:, :], t_s[:, :], ALU.mult), "kk")
                    for d in range(2):
                        act_did(f"sig{d}")
                        done(dve.tensor_tensor_scan(cum_s[d][:, :], restart_s[:, :], sig_s[d][:, :], 0.0,
                                                    ALU.mult, ALU.add), f"cum{d}")
                        own(f"cum{d}")
                        c4 = bass.ds(g * 4, 4)
                        done(dve.tensor_copy(mid_s[:, d, c4], chunks(cum_s[d])[:, :, P // 2 - 1]), f"mid{d}")
                        done(dve.tensor_tensor(end_s[:, d, c4], chunks(cum_s[d])[:, :, P - 1],
                                               chunks(cum_s[d])[:, :, P // 2 - 1], ALU.subtract), f"end{d}")
                    for d in range(2):
                        act_did(f"al{d}")
                        kd = (kb_s, t_s)[d]
                        own("kk")
                        done(dve.tensor_scalar(kd[:, :], al_s[d][:, :], par(K_A, p), ka1_s[:, bass.ds(p, 1)],
                                               ALU.mult, ALU.add), f"kfac{d}")
                        own(f"kfac{d}")
                        done(dve.tensor_tensor(kd[:, :], kd[:, :], k_s[:, :], ALU.mult), f"kdir{d}")
                        done(dve.tensor_tensor(al_s[d][:, :], al_s[d][:, :], kk_s[:, :], ALU.mult), f"kka{d}")
                    own("kdir1")
                    act_did("square")
                    dve.wait_ge(pe_prep.sem, pe_prep.value(it, "sumsq"))
                    done(dve.tensor_tensor(sq_s[:, :], kb_s[:, :], t_s[:, :], ALU.add), "kb")
                    own("kb")
                    dve.wait_ge(r_in, it * 16 + 16)
                    done(dve.scalar_tensor_tensor(out=sq_s[:, :], in0=r_s[:, :], scalar=rkh_s[:, bass.ds(p, 1)],
                                                  in1=sq_s[:, :], op0=ALU.mult, op1=ALU.mult), "rb")
                    dve.wait_ge(pe_prep.sem, pe_prep.value(it, "sumrb"))
                    dve.wait_ge(v_in, it * 16 + 16)
                    dve.wait_ge(bonus_stored, it * 16 + 16)
                    done(dve.tensor_tensor(bo_s[:, :], banks[6][:, :], v_s[:, :], ALU.mult), "bonus")
                    act_did("vt")
                    for h in range(2):
                        cols = slice(h * HD, (h + 1) * HD)
                        done(dve.tensor_copy(vp_s[:, bass.ds(g * 4, 4), h, cols], vt_s[:, bass.ds(g * 4, 4), cols]),
                             f"vp{h}")
                    for d in range(2):
                        mid = chunks(cum_s[d])[:, :, P // 2 - 1:P // 2]
                        own(f"end{d}")
                        done(dve.tensor_tensor(chunks(cum_s[d]), chunks(cum_s[d]),
                                               mid_s[:, d, bass.ds(g * 4, 4)].unsqueeze(2).broadcast_to([P, 4, P]),
                                               ALU.subtract), f"centre{d}")
                        own(f"centre{d}")
                        done(dve.tensor_tensor(sig_s[d][:, :], cum_s[d][:, :], sig_s[d][:, :], ALU.subtract),
                             f"before{d}")
                        act_did(f"er{d}")
                        done(dve.tensor_tensor(x_s[d][:, 1, t], r_s[:, :], e_s[0][:, :], ALU.mult), f"xr{d}")
                        act_did(f"ea{d}")
                        done(dve.scalar_tensor_tensor(out=x_s[d][:, 0, t], in0=kk_s[:, :], scalar=-1.0, in1=e_s[1][:, :],
                                                      op0=ALU.mult, op1=ALU.mult), f"xa{d}")
                        act_did(f"eb{d}")
                        done(dve.tensor_tensor(x_s[d][:, 2, t], al_s[d][:, :], e_s[2][:, :], ALU.mult), f"xb{d}")
                        done(dve.tensor_tensor(x_s[d][:, 3, t], (kb_s, t_s)[d][:, :], e_s[2][:, :], ALU.mult), f"xk{d}")

                def middle(p):
                    dve.wait_ge(dve_prep.sem, dve_prep.whole((p + 1) * NTG))
                    dve.memset(scale_s[:, :, :], 0.0).then_inc(scales_done, 1)
                    dve.wait_ge(scales_done, p * 2 + 1)
                    dve.wait_ge(exps_done, p * 2 + 2)
                    for c0, c1 in ((0, N_PROMPT // P), (N_PROMPT // P, NCH)):
                        dve.tensor_tensor(scale_s[:, 0, c0:c1 - 1], end_s[:, 0, c0:c1 - 1], mid_s[:, 0, c0 + 1:c1],
                                          ALU.mult)
                        ins = dve.tensor_tensor(scale_s[:, 1, c0 + 1:c1], mid_s[:, 1, c0 + 1:c1],
                                                end_s[:, 1, c0:c1 - 1], ALU.mult)
                    ins.then_inc(scales_done, 1)

                def rnd(p, it, cs):
                    def pe_did(name):
                        dve.wait_ge(pe_round.sem, pe_round.value(it, name))

                    def own(name):
                        dve.wait_ge(dve_round.sem, dve_round.value(it, name))

                    done = dve_round.done
                    for g, (u, d) in enumerate(G):
                        pe_did(f"ab{g}")
                        done(dve.tensor_tensor(ab_s[g][:, :], SC[0][:, :], causal_s[:, d, :], ALU.mult), f"ab{g}")
                        pe_did(f"ak{g}")
                        done(dve.tensor_tensor(ak_s[g][:, :], SC[1][:, :], causal_s[:, d, :], ALU.mult), f"ak{g}")
                    for g, (u, d) in enumerate(G):
                        own(f"ab{g}")
                        done(dve.tensor_tensor(Z[g][:, :], ab_s[g][:, 0:2 * P], pair_s[:, d, :], ALU.mult), f"Zp{g}")
                    for g in range(4):
                        own(f"Zp{g}")
                        done(dve.tensor_tensor(Z[g][:, :], Z[g][:, :], id2_s[:, :], ALU.add), f"Z{g}")
                    for n in range(LEVELS):
                        for g, (u, d) in enumerate(G):
                            pe_did(f"T{n}_{g}")
                            mask = level_s[:, d, n, :].unsqueeze(1).broadcast_to([P, 2, P])
                            done(dve.tensor_tensor(T[g][:, :].rearrange("p (h n) -> p h n", h=2),
                                                   INV[g][:, 0:2 * P].rearrange("p (h n) -> p h n", h=2),
                                                   mask, ALU.mult), f"T{n}_{g}")
                        for g in range(4):
                            pe_did(f"X{n}_{g}")
                            done(dve.tensor_tensor(X[g][:, :], INV[g][:, 2 * P:4 * P], X[g][:, :], ALU.add),
                                 f"X{n}_{g}")
                    for u in range(2):
                        for d in range(2):
                            pe_did(f"u_{u}{d}")
                            done(dve.tensor_copy(bass_diag(up_s[d][:, :, :].rearrange("p h n -> p (h n)")),
                                                 bass_diag(SN[d][:, P:3 * P])), f"up_{u}{d}")
                        for d in range(2):
                            c = chunk(cs, u * 2 + d)
                            pe_did(f"ys_{u}{d}")
                            dve.wait_ge(act_round.sem, act_round.value(it, f"S1_{u}{d}"))
                            y = y_s[:, bass.ds(c, 1), bass.ds(p * P, P)].rearrange("p a n -> p (a n)")
                            done(dve.tensor_tensor(y, SN[d][:, 3 * P:4 * P], y, ALU.add), f"y_{u}{d}")

                both(dve, prep, middle, rnd)

            @block.tensor
            def _(pe):
                pe_prep.start(pe)
                pe_round.start(pe)
                pe.wait_ge(const_in, 16 * 9)
                pe.wait_ge(lora_ready, 2)

                def prep(p, g, it):
                    done = pe_prep.done
                    t = bass.ds(g * TG, TG)
                    pe.wait_ge(w_in, p * 80 + 80)
                    pe.wait_ge(act_prep.sem, act_prep.whole(it))
                    pe.wait_ge(dve_prep.sem, dve_prep.whole(it))
                    pe.wait_ge(act_round.sem, act_round.whole(p * 6))
                    pe.wait_ge(dve_round.sem, dve_round.whole(p * 6))
                    for d in range(2):
                        done(pe.matmul(banks[d][:, :], wup_s[:, d, :], wd_s[:, t], start=True, stop=True), f"xw{d}")
                    for d in range(2):
                        done(pe.matmul(banks[2 + d][:, :], aup_s[:, d, :], ad_s[:, t], start=True, stop=True), f"xa{d}")
                    done(pe.matmul(banks[4][:, :], gup_s[:, :], gd_s[:, t], start=True, stop=True), "xg")
                    pe.wait_ge(act_prep.sem, act_prep.value(it, "square"))
                    done(pe.matmul(banks[5][:, :], hs_s[:, :], sq_s[:, :], start=True, stop=True), "sumsq")
                    pe.wait_ge(v_in, it * 16 + 16)
                    for c in range(4):
                        mm = pe.transpose(banks[7][:, c * P:(c + 1) * P], v_s[:, c * P:(c + 1) * P], id_s[:, :])
                    done(mm, "turnv")
                    pe.wait_ge(dve_prep.sem, dve_prep.value(it, "rb"))
                    done(pe.matmul(banks[6][:, :], hs_s[:, :], sq_s[:, :], start=True, stop=True), "sumrb")

                def middle(p):
                    pe.wait_ge(act_prep.sem, act_prep.whole((p + 1) * NTG))
                    pe.wait_ge(dve_prep.sem, dve_prep.whole((p + 1) * NTG))
                    hold(pe, holds[1])

                def rnd(p, it, cs):
                    done = pe_round.done

                    def act_did(name):
                        pe.wait_ge(act_round.sem, act_round.value(it, name))

                    def dve_did(name):
                        pe.wait_ge(dve_round.sem, dve_round.value(it, name))

                    head = lambda h: slice(h * P, (h + 1) * P)
                    for g in range(4):
                        pad = pad_s[g][:, :, :].rearrange("p a n -> p (a n)")
                        act_did(f"pad1_{g}")
                        for n, name in enumerate(("ab", "ak")):
                            if g:
                                dve_did(f"{name}{g - 1}")
                            else:
                                pe.wait_ge(dve_round.sem, dve_round.last(it, f"{name}3"))
                            done(pe.matmul(SC[n][:, :], st_s[g][:, 2 + n, :], pad, start=True, stop=True), f"{name}{g}")
                    for g in range(4):
                        pe.wait_ge(act_round.sem, act_round.last(it, f"Z{LEVELS - 1}_{g}"))
                        for n in range(2):
                            mm = pe.transpose(INV[g][:, head(n)], st_s[g][:, 2 + n, :], id_s[:, :])
                        done(mm, f"bk{g}")
                    for g in range(4):
                        act_did(f"bk{g}")
                        dve_did(f"Z{g}")
                        for h in range(2):
                            mm = pe.transpose(INV[g][:, head(2 + h)], Z[g][:, head(h)], id_s[:, :])
                        done(mm, f"X{g}")
                    for n in range(LEVELS):
                        for g in range(4):
                            if n:
                                act_did(f"Z{n - 1}_{g}")
                            else:
                                act_did(f"X{g}")
                            for h in range(2):
                                mm = pe.matmul(INV[g][:, head(h)], ab_s[g][:, head(h)], X[g][:, head(h)],
                                               start=True, stop=True)
                            done(mm, f"T{n}_{g}")
                        for g in range(4):
                            dve_did(f"T{n}_{g}")
                            for h in range(2):
                                mm = pe.matmul(INV[g][:, head(2 + h)], Z[g][:, head(h)], T[g][:, head(h)],
                                               start=True, stop=True)
                            done(mm, f"X{n}_{g}")
                        for g in range(4):
                            dve_did(f"X{n}_{g}")
                            for h in range(2):
                                mm = pe.transpose(INV[g][:, head(h)], X[g][:, head(h)], id_s[:, :])
                            done(mm, f"Z{n}_{g}")
                    for u in range(2):
                        for d in range(2):
                            g, c = u * 2 + d, chunk(cs, u * 2 + d)
                            vp = lambda h: vp_s[:, bass.ds(c, 1), h, :].rearrange("p a n -> p (a n)")
                            if u:
                                dve_did(f"y_{u - 1}{d}")
                                act_did(f"S1_{u - 1}{d}")
                            else:
                                pe.wait_ge(dve_round.sem, dve_round.last(it, f"y_1{d}"))
                                pe.wait_ge(act_round.sem, act_round.last(it, f"S1_1{d}"))
                            pe.matmul(SN[d][:, 0:P], st_s[g][:, 0, :], S[d][:, :], start=True, stop=False)
                            for h in range(2):
                                mm = pe.matmul(SN[d][:, 0:P], ak_s[g][:, head(h)], vp(h), start=False, stop=h == 1)
                            done(mm, f"p_{u}{d}")
                        for d in range(2):
                            g = u * 2 + d
                            act_did(f"Z{LEVELS - 1}_{g}")
                            act_did(f"p_{u}{d}")
                            for h in range(2):
                                mm = pe.matmul(SN[d][:, head(1 + h)], Z[g][:, head(h)], p_s[d][:, :],
                                               start=True, stop=True)
                            done(mm, f"u_{u}{d}")
                        for d in range(2):
                            g, c = u * 2 + d, chunk(cs, u * 2 + d)
                            vp = lambda h: vp_s[:, bass.ds(c, 1), h, :].rearrange("p a n -> p (a n)")
                            act_did(f"uf_{u}{d}")
                            Y = SN[d][:, 3 * P:4 * P]
                            pe.matmul(Y, st_s[g][:, 1, :], S[d][:, :], start=True, stop=False)
                            for h in range(2):
                                pe.matmul(Y, ak_s[g][:, head(2 + h)], vp(h), start=False, stop=False)
                                pe.matmul(Y, ab_s[g][:, head(2 + h)], up_s[d][:, h, :], start=False, stop=h == 1)
                            pe.matmul(SN[d][:, 0:P], id_s[:, :], S[d][:, :], start=True, stop=False)
                            pe.matmul(SN[d][:, 0:P], bk_s[g][:, 0:P], uf_s[d][:, :], start=False, stop=False)
                            mm = pe.matmul(SN[d][:, 0:P], bk_s[g][:, P:2 * P],
                                           vt_s[:, bass.ds(c, 1), :].rearrange("p a n -> p (a n)"),
                                           start=False, stop=True)
                            done(mm, f"ys_{u}{d}")

                both(pe, prep, middle, rnd)


def bass_diag(ap):
    return ap.rearrange("p (x n) -> p x n", n=HD)[:, 0:4:3, :]


def branch_output(nc, rwkvT, y_in, bonusT, gT, par, ident):
    ctx = ExitStack()
    with ctx:
        a = Arena(nc, ctx, "bo")
        sem = lambda name: ctx.enter_context(nc.semaphore("bo_" + name))
        LN_W, LN_B = 7, 8
        CG, H4 = TG // P, TG // P * HEADS
        y_s = [a.sb(f"y{i}", [P, CG, WIDTH]) for i in range(2)]
        sq_s = a.sb("sq", [P, CG * WIDTH])
        mean, var = a.sb("mean", [P, H4]), a.sb("var", [P, H4])
        bo_s = [a.sb(f"bo{i}", [P, KW, TG]) for i in range(2)]
        g_s = [a.sb(f"g{i}", [P, KW, TG]) for i in range(2)]
        par_s, id_s, eps_s = a.sb("par", [P, 9, PAIRS]), a.sb("id", [P, P]), a.sb("eps", [P, 1])
        banks = [a.ps(f"b{i}") for i in range(8)]
        par_in, eps_set = sem("par_in"), sem("eps_set")
        y_in_sb, bo_in, g_in = ([sem(f"{n}{i}") for i in range(2)] for n in ("y_in", "bo_in", "g_in"))
        stat, squares, stds, turned, mixed, stored = (
            sem("stat"), sem("squares"), sem("stds"), sem("turned"), sem("mixed"), sem("stored"))
        STAT = 6

        with nc.Block() as block:

            @block.sync
            def _(sp):
                sp.dma_start(par_s[:, :, :], par).then_inc(par_in, 16)
                sp.dma_start(id_s[:, :], ident).then_inc(par_in, 16)
                for g in range(NTG):
                    t = slice(g * TG, (g + 1) * TG)
                    if g >= 2:
                        sp.wait_ge(stored, 16 * (g - 1))
                        sp.wait_ge(turned, KW * (g - 1))
                    sp.dma_start(y_s[g % 2][:, :, :], y_in[:, g * CG:(g + 1) * CG, :]).then_inc(y_in_sb[g % 2], 16)
                    for tile, src, s in ((bo_s, bonusT, bo_in), (g_s, gT, g_in)):
                        sp.dma_start(tile[g % 2][:, :, :], src[:, :, t].rearrange("k p n -> p k n"))\
                            .then_inc(s[g % 2], 16)

            @block.gpsimd
            def _(pool):
                for g in range(NTG):
                    pool.wait_ge(mixed, 2 * KW * (g + 1))
                    pool.dma_start(rwkvT[:, :, g * TG:(g + 1) * TG].rearrange("k p n -> p k n"), bo_s[g % 2][:, :, :])\
                        .then_inc(stored, 16)
                    pool.wait_ge(stored, 16 * (g + 1))

            @block.scalar
            def _(act):
                act.wait_ge(eps_set, 1)
                for g in range(NTG):
                    act.wait_ge(stat, STAT * g + 3)
                    act.activation(sq_s[:, :], y_s[g % 2][:, :, :].rearrange("p c n -> p (c n)"), ACT.Square)\
                        .then_inc(squares, 1)
                    act.wait_ge(stat, STAT * g + 4)
                    act.activation(var[:, :], var[:, :], ACT.Sqrt, scale=1.0 / HD, bias=eps_s[:, :]).then_inc(stds, 1)

            @block.vector
            def _(dve):
                dve.memset(eps_s[:, :], LNX_EPS).then_inc(eps_set, 1)
                dve.wait_ge(par_in, 32)
                for g in range(NTG):
                    y = y_s[g % 2][:, :, :].rearrange("p c (h n) -> p (c h) n", n=HD)
                    over = lambda s: s[:, :].unsqueeze(2).broadcast_to([P, H4, HD])
                    dve.wait_ge(y_in_sb[g % 2], 16 * (g // 2 + 1))
                    dve.tensor_reduce(mean[:, :], y, AX.X, ALU.add).then_inc(stat, 1)
                    dve.wait_ge(stat, STAT * g + 1)
                    dve.tensor_scalar(mean[:, :], mean[:, :], 1.0 / HD, None, ALU.mult).then_inc(stat, 1)
                    dve.wait_ge(stat, STAT * g + 2)
                    dve.tensor_tensor(y, y, over(mean), ALU.subtract).then_inc(stat, 1)
                    dve.wait_ge(squares, g + 1)
                    dve.tensor_reduce(var[:, :], sq_s[:, :].rearrange("p (h n) -> p h n", n=HD), AX.X, ALU.add)\
                        .then_inc(stat, 1)
                    dve.wait_ge(stds, g + 1)
                    dve.reciprocal(var[:, :], var[:, :]).then_inc(stat, 1)
                    dve.wait_ge(stat, STAT * g + 5)
                    dve.tensor_tensor(y, y, over(var), ALU.mult).then_inc(stat, 1)
                    dve.wait_ge(bo_in[g % 2], 16 * (g // 2 + 1))
                    dve.wait_ge(g_in[g % 2], 16 * (g // 2 + 1))
                    for b in range(KW):
                        dve.wait_ge(turned, KW * g + b + 1)
                        o = bo_s[g % 2][:, b, :]
                        dve.scalar_tensor_tensor(out=o, in0=banks[(g * KW + b) % 8][:, :], scalar=par_s[:, LN_W, b:b + 1],
                                                 in1=o, op0=ALU.mult, op1=ALU.add).then_inc(mixed, 1)
                        dve.wait_ge(mixed, 2 * (KW * g + b) + 1)
                        dve.scalar_tensor_tensor(out=o, in0=o, scalar=par_s[:, LN_B, b:b + 1], in1=g_s[g % 2][:, b, :],
                                                 op0=ALU.add, op1=ALU.mult).then_inc(mixed, 1)

            @block.tensor
            def _(pe):
                pe.wait_ge(par_in, 32)
                for g in range(NTG):
                    pe.wait_ge(stat, STAT * (g + 1))
                    if g >= 2:
                        pe.wait_ge(mixed, 2 * KW * (g - 1))
                    for b in range(KW):
                        for c in range(CG):
                            mm = pe.transpose(banks[(g * KW + b) % 8][:, c * P:(c + 1) * P],
                                              y_s[g % 2][:, c, b * P:(b + 1) * P], id_s[:, :])
                        mm.then_inc(turned, 1)


def finish(nc, yT, xT, attnT, rwkvT, weights, ln_pre, ln_post, ln_ffn_pre, ln_ffn_post, ones):
    ctx = ExitStack()
    with ctx:
        a = Arena(nc, ctx, "fi")
        sem = lambda name: ctx.enter_context(nc.semaphore("fi_" + name))
        RING = 4
        AHEAD = 2
        FFN_KT = (8, 8, KF - 16)
        J_OUT, J_FFN, J_LAST = 3 * KD, 4 * KD, 4 * KD + 2 * KF
        JOBS = J_LAST + 3 * KD
        assert JOBS % RING == 0
        x_s = a.sb("x", [P, KD, TG])
        m_s = a.sb("m", [P, KD, TG])
        ln_s = [a.sb(f"ln{i}", [P, KD]) for i in range(4)]
        ones_s = a.sb("ones", [P, P])
        eps_s = a.sb("eps", [P, 1])
        h_hi = a.sb("h_hi", [P, KD, TG], F32R)
        h_lo = a.sb("h_lo", [P, KD, TG], F32R)
        w_s = [a.sb(f"w{i}", [P, KD * P]) for i in range(RING)]
        w_hi = [a.sb(f"whi{i}", [P, KD, P], F32R) for i in range(RING)]
        w_lo = [a.sb(f"wlo{i}", [P, KD, P], F32R) for i in range(RING)]
        s_s = [a.sb(f"s{i}", [P, TG]) for i in range(2)]
        p_s = a.sb("p", [P, TG])
        std, rstd = s_s[0], p_s
        with ExitStack() as first:
            b = Arena(nc, first, "fi")
            br_s = b.sb("br", [P, 2 * KW, TG])
            br_hi = b.sb("br_hi", [P, 2 * KW, TG], F32R)
            br_lo = b.sb("br_lo", [P, 2 * KW, TG], F32R)
            g_hi = b.sb("g_hi", [P, KD, TG], F32R)
            g_lo = b.sb("g_lo", [P, KD, TG], F32R)
            q_s = b.sb("q", [P, TG])
        f_hi = a.sb("f_hi", [P, KF, TG], F32R)
        f_lo = a.sb("f_lo", [P, KF, TG], F32R)
        banks = [a.ps(f"b{i}") for i in range(8)]
        SUM = banks[7]

        par_in, eps_set, x_in, br_in = sem("par_in"), sem("eps_set"), sem("x_in"), [sem("br_in0"), sem("br_in1")]
        squares, sums, stds, rstds = sem("squares"), sem("sums"), sem("stds"), sem("rstds")
        normed, h_hi_ready, h_lo_ready = sem("normed"), sem("h_hi_ready"), sem("h_lo_ready")
        br_hi_ready, br_lo_ready = sem("br_hi_ready"), sem("br_lo_ready")
        w_loaded = [sem(f"w_loaded{i}") for i in range(RING)]
        w_hi_ready, w_lo_ready, product_done = sem("w_hi_ready"), sem("w_lo_ready"), sem("product_done")
        gate_ready, gated, merge_step = sem("gate_ready"), sem("gated"), sem("merge_step")
        out_copied, scaled, x2_ready = sem("out_copied"), sem("scaled"), sem("x2_ready")
        silu_ready, ffn_step = sem("silu_ready"), sem("ffn_step")
        ffn_copied, y_stored = sem("ffn_copied"), sem("y_stored")
        holds = [sem("hold0"), sem("hold1")]

        def jobs(eng, t, job, after):
            j0 = t * JOBS
            with eng.Fori(0, KD // 4) as i:
                for s in range(12):
                    row = i * 12 + s
                    j, k = j0 + row, i * 4 + s // 3
                    job(j, s, KD, "merge", k, row)
                    after("gate" if s % 3 < 2 else "merge", k, s, j)
            for k in range(KD):
                job(j0 + J_OUT + k, k, KD, "out", k, J_OUT + k)
                after("out", k, k, j0 + J_OUT + k)
            after("mixed", 0, 0, 0)
            with eng.Fori(0, KF // 2) as i:
                for s in range(4):
                    row = i * 4 + J_FFN + s
                    j, k = j0 + row, i * 2 + s // 2
                    job(j, s, KD, "ffn_in", k, row)
                    after("silu" if s % 2 == 0 else "ffn_in", k, s, j)
            for s in range(3 * KD):
                job(j0 + J_LAST + s, s, FFN_KT[s % 3], "ffn_out", s // 3, J_LAST + s)
                if s % 3 == 2:
                    after("ffn_out", s // 3, s, j0 + J_LAST + s)
            after("done", 0, 0, 0)

        def nothing(*_):
            pass

        with nc.Block() as block:

            @block.sync
            def _(sp):
                sp.dma_start(ones_s[:, :], ones).then_inc(par_in, 16)
                for tile, src in zip(ln_s, (ln_pre, ln_post, ln_ffn_pre, ln_ffn_post)):
                    sp.dma_start(tile[:, :], src).then_inc(par_in, 16)

                def load(j, s, row, kt):
                    sp.wait_ge(w_lo_ready, j + 1)
                    sp.dma_start(w_s[s % RING][:, 0:kt * P],
                                 weights[bass.ds(row, 1)].rearrange("a p n -> (a p) n")[:, 0:kt * P])\
                        .then_inc(w_loaded[s % RING], 16)

                with sp.Fori(0, NTG) as t:
                    jobs(sp, t, lambda j, s, kt, kind, k, row: load(j, s, row, kt), nothing)
                for s in range(AHEAD):
                    load(NTG * JOBS + s, s, s, KD)

            @block.gpsimd
            def _(pool):
                pool.sem_inc(w_lo_ready, RING)

                def split(j, s, kt, kind, k, row):
                    pool.wait_ge(w_hi_ready, j + 1)
                    pool.tensor_tensor(w_lo[s % RING][:, 0:kt, :],
                                       w_s[s % RING][:, 0:kt * P].rearrange("p (k n) -> p k n", k=kt),
                                       w_hi[s % RING][:, 0:kt, :].bitcast(F32), ALU.subtract)\
                        .then_inc(w_lo_ready, 1)

                with pool.Fori(0, NTG) as t:
                    pool.dma_start(x_s[:, :, :], xT[bass.ds(t, 1)].rearrange("a p k n -> (a p) k n"))\
                        .then_inc(x_in, 16)
                    for b, src in enumerate((attnT, rwkvT)):
                        pool.dma_start(br_s[:, b * KW:(b + 1) * KW, :],
                                       src[:, :, bass.ds(t * TG, TG)].rearrange("k p n -> p k n"))\
                            .then_inc(br_in[b], 16)
                    jobs(pool, t, split, nothing)
                    pool.wait_ge(x2_ready, t * 16 + 16)
                    hold(pool, holds[0])
                    pool.dma_start(yT[bass.ds(t, 1)].rearrange("a p k n -> (a p) k n"), x_s[:, :, :])\
                        .then_inc(y_stored, 16)
                    pool.wait_ge(y_stored, t * 16 + 16)

            @block.scalar
            def _(act):
                def split(j, s):
                    act.wait_ge(w_loaded[s % RING], 4 * (j - s % RING) + 16)
                    act.wait_ge(product_done, j + 1)
                    act.activation(w_hi[s % RING][:, :, :], w_s[s % RING][:, :].rearrange("p (k n) -> p k n", k=KD),
                                   ACT.Copy).then_inc(w_hi_ready, 1)

                act.wait_ge(eps_set, 1)
                for s in range(AHEAD):
                    split(s, s)
                with act.Fori(0, NTG) as t:
                    def root(n):
                        act.wait_ge(sums, t * 32 + 8 * n)
                        act.activation(std[:, :], SUM[:, :], ACT.Sqrt, scale=1.0 / D, bias=eps_s[:, :])\
                            .then_inc(stds, 1)

                    def h_high(n):
                        for k in range(KD):
                            act.wait_ge(normed, t * 16 + n * KD + k + 1)
                            act.activation(h_hi[:, k, :], m_s[:, k, :], ACT.Copy).then_inc(h_hi_ready, 1)

                    act.wait_ge(x_in, t * 16 + 16)
                    for k in range(KD):
                        act.activation(m_s[:, k, :], x_s[:, k, :], ACT.Square).then_inc(squares, 1)
                    root(1)
                    for b in range(2):
                        act.wait_ge(br_in[b], t * 16 + 16)
                    act.activation(br_hi[:, :, :], br_s[:, :, :], ACT.Copy).then_inc(br_hi_ready, 1)
                    h_high(0)

                    def after(kind, k, s, j):
                        if kind == "gate":
                            act.wait_ge(product_done, j + RING + 1)
                            act.wait_ge(gated, t * KD + k + 2)
                            act.activation(s_s[s % 3][:, :], banks[s // 3 % 2 * 4 + s % 3][:, :], ACT.Sigmoid)\
                                .then_inc(gate_ready, 1)
                        if kind in ("out", "ffn_out"):
                            copied, base = (out_copied, 8) if kind == "out" else (ffn_copied, 24)
                            act.wait_ge(copied, t * KD + k + (5 if kind == "out" else 3))
                            if k >= 2:
                                act.wait_ge(sums, t * 32 + base + k - 1)
                            act.activation(s_s[k % 2][:, :], m_s[:, k, :], ACT.Square).then_inc(squares, 1)
                        if kind == "mixed":
                            root(2)
                            for k in range(KD):
                                act.wait_ge(x2_ready, t * 16 + k + 1)
                                act.activation(m_s[:, k, :], x_s[:, k, :], ACT.Square).then_inc(squares, 1)
                            root(3)
                            h_high(1)
                        if kind == "silu":
                            act.wait_ge(product_done, j + RING + 1)
                            act.wait_ge(ffn_step, t * 3 * KF + 3 * k + 1)
                            act.activation(s_s[s // 2][:, :], banks[s // 2 * 2][:, :], ACT.Silu)\
                                .then_inc(silu_ready, 1)
                        if kind == "done":
                            root(4)

                    jobs(act, t, lambda j, s, kt, kind, k, row: split(j + AHEAD, s + AHEAD), after)

            @block.vector
            def _(dve):
                dve.memset(eps_s[:, :], EPS).then_inc(eps_set, 1)
                dve.sem_inc(gated, 2)
                dve.sem_inc(merge_step, 1)
                dve.sem_inc(out_copied, 4)
                dve.sem_inc(ffn_step, 6)
                dve.sem_inc(ffn_copied, 2)
                dve.wait_ge(par_in, 80)
                with dve.Fori(0, NTG) as t:
                    def invert(n):
                        dve.wait_ge(stds, t * 4 + n + 1)
                        dve.reciprocal(rstd[:, :], std[:, :]).then_inc(rstds, 1)
                        dve.wait_ge(rstds, t * 4 + n)

                    def norm(n, ln):
                        invert(2 * n + 1)
                        for k in range(KD):
                            dve.scalar_tensor_tensor(out=m_s[:, k, :], in0=x_s[:, k, :], scalar=ln[:, k:k + 1],
                                                     in1=rstd[:, :], op0=ALU.mult, op1=ALU.mult).then_inc(normed, 1)
                        for k in range(KD):
                            dve.wait_ge(h_hi_ready, t * 16 + n * KD + k + 1)
                            dve.tensor_tensor(h_lo[:, k, :], m_s[:, k, :], h_hi[:, k, :].bitcast(F32), ALU.subtract)\
                                .then_inc(h_lo_ready, 1)

                    def add_normed(n, ln):
                        invert(2 * n + 2)
                        for k in range(KD):
                            dve.scalar_tensor_tensor(out=m_s[:, k, :], in0=m_s[:, k, :], scalar=ln[:, k:k + 1],
                                                     in1=rstd[:, :], op0=ALU.mult, op1=ALU.mult).then_inc(scaled, 1)
                            dve.wait_ge(scaled, t * 16 + n * KD + k + 1)
                            dve.tensor_tensor(x_s[:, k, :], x_s[:, k, :], m_s[:, k, :], ALU.add).then_inc(x2_ready, 1)

                    norm(0, ln_s[0])
                    dve.wait_ge(br_hi_ready, t + 1)
                    dve.tensor_tensor(br_lo[:, :, :], br_s[:, :, :], br_hi[:, :, :].bitcast(F32), ALU.subtract)\
                        .then_inc(br_lo_ready, 1)

                    def three(step, n, hi, lo, k):
                        dve.wait_ge(step, n)
                        dve.tensor_copy(hi[:, bass.ds(k, 1), :], p_s[:, :].rearrange("p (a n) -> p a n", a=1))\
                            .then_inc(step, 1)
                        dve.wait_ge(step, n + 1)
                        dve.tensor_tensor(lo[:, bass.ds(k, 1), :], p_s[:, :].rearrange("p (a n) -> p a n", a=1),
                                          hi[:, bass.ds(k, 1), :].bitcast(F32), ALU.subtract).then_inc(step, 1)

                    def after(kind, k, s, j):
                        if kind == "merge":
                            bank = s // 3 % 2 * 4
                            n = t * 3 * KD + 3 * k + 1
                            dve.wait_ge(gate_ready, t * 2 * KD + 2 * k + 2)
                            dve.wait_ge(product_done, j + RING + 1)
                            dve.wait_ge(merge_step, n)
                            dve.tensor_tensor(p_s[:, :], s_s[0][:, :], banks[bank + 2][:, :], ALU.mult)
                            dve.tensor_tensor(q_s[:, :], s_s[1][:, :], banks[bank + 3][:, :], ALU.mult)\
                                .then_inc(gated, 1)
                            dve.wait_ge(gated, t * KD + k + 3)
                            dve.tensor_tensor(p_s[:, :], p_s[:, :], q_s[:, :], ALU.add).then_inc(merge_step, 1)
                            three(merge_step, n + 1, g_hi, g_lo, k)
                        if kind in ("out", "ffn_out"):
                            dve.wait_ge(product_done, j + RING + 1)
                            if kind == "out":
                                dve.tensor_copy(m_s[:, k, :], banks[k % 4][:, :]).then_inc(out_copied, 1)
                            else:
                                dve.tensor_copy(m_s[:, k, :], banks[4 + k % 2][:, :]).then_inc(ffn_copied, 1)
                        if kind == "mixed":
                            add_normed(0, ln_s[1])
                            norm(1, ln_s[2])
                        if kind == "ffn_in":
                            n = t * 3 * KF + 3 * k + 6
                            dve.wait_ge(silu_ready, t * KF + k + 1)
                            dve.wait_ge(product_done, j + RING + 1)
                            dve.wait_ge(ffn_step, n)
                            dve.tensor_tensor(p_s[:, :], s_s[s // 2][:, :], banks[s // 2 * 2 + 1][:, :], ALU.mult)\
                                .then_inc(ffn_step, 1)
                            three(ffn_step, n + 1, f_hi, f_lo, k)
                        if kind == "done":
                            add_normed(1, ln_s[3])

                    jobs(dve, t, nothing, after)

            @block.tensor
            def _(pe):
                pe.sem_inc(product_done, RING)
                pe.sem_inc(stds, 1)
                pe.wait_ge(par_in, 80)
                with pe.Fori(0, NTG) as t:
                    def add_squares(n, k, sq):
                        if k == 0:
                            pe.wait_ge(stds, t * 4 + n)
                        pe.wait_ge(squares, t * 32 + (n - 1) * KD + k + 1)
                        pe.matmul(SUM[:, :], ones_s[:, :], sq, start=k == 0, stop=k == KD - 1)\
                            .then_inc(sums, 1)

                    for k in range(KD):
                        add_squares(1, k, m_s[:, k, :])
                    pe.wait_ge(h_lo_ready, t * 16 + KD)
                    pe.wait_ge(br_lo_ready, t + 1)
                    hold(pe, holds[1])

                    def job(j, s, kt, kind, k, row):
                        pe.wait_ge(w_lo_ready, j + RING + 1)
                        whi, wlo = w_hi[s % RING], w_lo[s % RING]

                        def part(out, w0, n, xs, **flags):
                            return product(pe, out[:, :], (lambda k: whi[:, w0 + k, :], lambda k: wlo[:, w0 + k, :]),
                                           tuple((lambda k, x=x: x[:, k, :]) for x in xs), n, **flags)

                        if kind == "merge":
                            bank = s // 3 % 2 * 4
                            if s % 3 == 0:
                                pe.wait_ge(gated, t * KD + k + 1)
                            if s % 3 < 2:
                                mm = part(banks[bank + s % 3], 0, KD, (h_hi, h_lo))
                            else:
                                part(banks[bank + 2], 0, KW, (br_hi[:, 0:KW, :], br_lo[:, 0:KW, :]))
                                mm = part(banks[bank + 3], KW, KW, (br_hi[:, KW:2 * KW, :], br_lo[:, KW:2 * KW, :]))
                        elif kind == "out":
                            if s == 0:
                                pe.wait_ge(merge_step, (t + 1) * 3 * KD + 1)
                            pe.wait_ge(out_copied, t * KD + s + 1)
                            mm = part(banks[s % 4], 0, KD, (g_hi, g_lo))
                        elif kind == "ffn_in":
                            if s % 2 == 0:
                                pe.wait_ge(ffn_step, t * 3 * KF + 3 * k + 1)
                            mm = part(banks[s], 0, KD, (h_hi, h_lo))
                        else:
                            if s == 0:
                                pe.wait_ge(ffn_step, (t + 1) * 3 * KF + 6)
                            if s % 3 == 0:
                                pe.wait_ge(ffn_copied, t * KD + s // 3 + 1)
                            k0 = 8 * (s % 3)
                            mm = part(banks[4 + s // 3 % 2], 0, kt, (f_hi[:, k0:k0 + kt, :], f_lo[:, k0:k0 + kt, :]),
                                      start=s % 3 == 0, stop=s % 3 == 2)
                        mm.then_inc(product_done, 1)

                    def after(kind, k, s, j):
                        if kind in ("out", "ffn_out") and k >= 1:
                            add_squares(2 if kind == "out" else 4, k - 1, s_s[(k - 1) % 2][:, :])
                        if kind == "mixed":
                            add_squares(2, KD - 1, s_s[1][:, :])
                            for k in range(KD):
                                add_squares(3, k, m_s[:, k, :])
                            pe.wait_ge(h_lo_ready, t * 16 + 2 * KD)
                            hold(pe, holds[1])
                        if kind == "done":
                            add_squares(4, KD - 1, s_s[1][:, :])

                    jobs(pe, t, job, after)


def blocks(w):
    k, c = w.shape
    return np.ascontiguousarray(w.reshape(k // P, P, c // P, P).transpose(2, 1, 0, 3)).reshape(c // P, P, k)


def columns(v):
    return np.ascontiguousarray(v.reshape(-1, P).T)


def shape_constants():
    r = np.arange(P)
    c = {}
    c["ones"] = np.ones((P, P), np.float32)
    c["ident"] = np.eye(P, dtype=np.float32)
    c["headsum"] = (r[:, None] // HD == r[None, :] // HD).astype(np.float32)
    swap = np.zeros((P, P), np.float32)
    e = np.arange(0, P, 2)
    swap[e + 1, e] = -1.0
    swap[e, e + 1] = 1.0
    c["swap"] = swap
    t = np.arange(N_PROMPT)
    nf = HD // 4
    inv = (ROPE_THETA ** (-np.arange(nf, dtype=np.float32) / nf)).astype(np.float32)
    ang = np.concatenate([(t // GRID_W).astype(np.float32)[:, None] * inv,
                          (t % GRID_W).astype(np.float32)[:, None] * inv], -1)
    tab = ang[:, (r % HD) // 2].T
    tab = np.concatenate([tab, tab[:, :N_SAMPLE]], 1)
    c["cos"], c["sin"] = np.cos(tab).astype(np.float32), np.sin(tab).astype(np.float32)
    s, q = r[:, None], r[None, :]
    strict = [(s < q), (s > q)]
    loose = [(s <= q), (s >= q)]
    c["causal"] = np.stack([np.concatenate([strict[d]] * 2 + [loose[d]] * 2, 1) for d in range(2)]).astype(np.float32)
    pair = [strict[d] & (s // 2 == q // 2) for d in range(2)]
    c["pair"] = np.stack([np.concatenate([pair[d]] * 2, 1) for d in range(2)]).astype(np.float32)
    c["ident2"] = np.concatenate([np.eye(P)] * 2, 1).astype(np.float32)
    levels = np.zeros((2, LEVELS, P, P), np.float32)
    for d in range(2):
        for n in range(LEVELS):
            m = 2 << n
            levels[d, n] = (s // (2 * m) == q // (2 * m)) & ((s // m) % 2 == 1 - d) & ((q // m) % 2 == d)
    c["levels"] = levels
    c["restart"] = np.where(np.arange(TG) % P == 0, 0.0, 1.0).astype(np.float32)[None].repeat(P, 0)
    return {n: np.ascontiguousarray(x) for n, x in c.items()}


PARAMS = ("k_k", "k_a", "r_k", "w0", "a0", "lnx_w", "lnx_b")
CONSTS = ("ones", "ident", "headsum", "swap", "cos", "sin", "causal", "pair", "ident2", "levels", "restart")


def build(nc, at):
    def scratch(name, shape):
        return nc.dram_tensor(name, shape, F32, kind="Internal").ap()

    uT = scratch("uT", [NB_IN, P, N])
    qkT = scratch("qkT", [(B_V - B_Q) * P, N])
    attnT = scratch("attnT", [WIDTH, N])
    y = scratch("y", [P, NCH, WIDTH])
    bonusT, gT, rwkvT = (scratch(n, [KW, P, N]) for n in ("bonusT", "gT", "rwkvT"))
    with nc.sbuf_tensor("h_hi", [P, KD, N], F32R) as h_hi, nc.sbuf_tensor("h_lo", [P, KD, N], F32R) as h_lo:
        project(nc, (h_hi, h_lo), uT, at["xT"], at["w_in"], at["ln_mix_pre"], at["mu"], at["ones"])
    rope(nc, qkT, uT, at["gains"], at["cos"], at["sin"], at["headsum"], at["swap"])
    attention(nc, attnT, qkT, uT, at["ident"], 0, N_PROMPT, "ap")
    attention(nc, attnT, qkT, uT, at["ident"], N_PROMPT, N_SAMPLE, "as")
    recurrence(nc, y, bonusT, gT, uT, at["w_up"], at["a_up"], at["g_up"], at["par"], at)
    branch_output(nc, rwkvT, y, bonusT, gT, at["par"], at["ident"])
    finish(nc, at["yT"], at["xT"], attnT.rearrange("(k p) n -> k p n", p=P), rwkvT, at["w_rest"],
           at["ln_mix_pre"], at["ln_mix_post"], at["ln_ffn_pre"], at["ln_ffn_post"], at["ones"])


def layout(inputs):
    f = {n: np.asarray(v)[0] for n, v in inputs.items()}
    x = np.concatenate([f["x_prompt"], f["x_sample"]], 0)
    out = {"xT": np.ascontiguousarray(x.reshape(NTG, TG, KD, P).transpose(0, 3, 2, 1))}
    w_in, gate = f["w_in"][:, :NB_IN * P], f["w_in"][:, NB_IN * P:]
    out["w_in"] = blocks(w_in)
    for n in ("ln_mix_pre", "ln_mix_post", "ln_ffn_pre", "ln_ffn_post"):
        out[n] = columns(f[n])
    mu = np.concatenate([np.zeros(B_R * P, np.float32), f["shift_mu"]])
    out["mu"] = columns(mu)
    out["gains"] = columns(np.concatenate([f["q_gain"]] * HEADS + [f["k_gain"]] * 2))
    out["par"] = np.ascontiguousarray(np.stack(
        [columns(v) for n in PARAMS for v in np.reshape(f[n], (-1, WIDTH))], 1))
    for n in ("w_up", "a_up", "g_up"):
        out[n] = np.ascontiguousarray(f[n].reshape(P, PAIRS, P).transpose(1, 0, 2))
    branch = blocks(f["w_branch"].reshape(2 * WIDTH, D))
    last = blocks(f["w_ffn_out"])
    last = np.pad(last, ((0, 0), (0, 0), (0, 3 * D - D_FF))).reshape(KD, P, 3, D).transpose(0, 2, 1, 3)
    out["w_rest"] = np.ascontiguousarray(np.concatenate([
        np.stack([blocks(gate[:, :D]), blocks(gate[:, D:]), branch], 1).reshape(3 * KD, P, D),
        blocks(f["w_out"]),
        np.stack([blocks(f["w_ffn_in"][:, :D_FF]), blocks(f["w_ffn_in"][:, D_FF:])], 1).reshape(2 * KF, P, D),
        last.reshape(3 * KD, P, D)], 0))
    return {**out, **{n: v for n, v in shape_constants().items() if n in CONSTS}}


def kernel(**inputs):
    import concourse.bacc as bacc
    from concourse.bass_utils import run_bass_kernel_spmd

    nc = bacc.Bacc("TRN2", target_bir_lowering=False, num_devices=1)
    arrays = layout(inputs)
    at = {n: nc.dram_tensor(n, v.shape, F32, kind="ExternalInput").ap() for n, v in arrays.items()}
    at["yT"] = nc.dram_tensor("yT", (NTG, P, KD, TG), F32, kind="ExternalOutput").ap()
    build(nc, at)
    got = run_bass_kernel_spmd(nc, [arrays], core_ids=[0]).results[0]["yT"]
    y = got.transpose(0, 3, 2, 1).reshape(N, D)
    return y[None, :N_PROMPT], y[None, N_PROMPT:]
```

```python
from contextlib import ExitStack

import numpy as np

import concourse.bass as bass
from concourse import mybir

F32 = mybir.dt.float32
F32R = mybir.dt.float32r
ALU = mybir.AluOpType
ACT = mybir.ActivationFunctionType
AX = mybir.AxisListType

P = 128
D = 1024
KD = D // P
N_PROMPT, N_SAMPLE = 1024, 512
N = N_PROMPT + N_SAMPLE
TG = 512
NTG = N // TG
NCH = N // P
HD = 64
HEADS = 8
WIDTH = HEADS * HD
KW = WIDTH // P
D_FF = 2816
KF = D_FF // P
KFH = KF // 2
EPS = 1e-6
LNX_EPS = 64e-5
GRID_W = 64
ROPE_THETA = 10000.0
DECAY_SCALE = float(np.exp(-0.5))

B_Q, B_K, B_V, B_R, B_RK, B_RV, B_WD, B_AD, B_GD = 0, 4, 5, 6, 10, 14, 18, 19, 20
NB_IN = 21


class Arena:

    def __init__(self, nc, ctx, tag):
        self.nc, self.ctx, self.tag = nc, ctx, tag

    def sb(self, name, shape, dt=F32):
        return self.ctx.enter_context(self.nc.sbuf_tensor(f"{self.tag}_{name}", shape, dt))

    def ps(self, name, shape=(P, TG), dt=F32):
        return self.ctx.enter_context(self.nc.psum_tensor(f"{self.tag}_{name}", list(shape), dt))


def product(pe, out, w, x, kt, start=True, stop=True):
    for k in range(kt):
        for part, (a, b) in enumerate(((0, 0), (1, 0), (0, 1))):
            mm = pe.matmul(out, w[a](k), x[b](k), start=start and k == 0 and part == 0,
                           stop=stop and k == kt - 1 and part == 2)
    return mm


def hold(eng, holds):
    eng.sem_inc(holds, 1)


def project(nc, hT, uT, xT, w_in, ln_pre, mu, ones):
    ctx = ExitStack()
    with ctx:
        a = Arena(nc, ctx, "pr")
        sem = lambda name: ctx.enter_context(nc.semaphore("pr_" + name))
        h_hi, h_lo = hT
        NS = 1540
        x_s = a.sb("x", [P, KD, TG])
        h_s = a.sb("h", [P, KD, TG])
        std = a.sb("std", [P, TG])
        rstd = a.sb("rstd", [P, TG])
        ln_s = a.sb("ln", [P, KD])
        mu_s = a.sb("mu", [P, NB_IN])
        mu1 = a.sb("mu1", [P, NB_IN])
        muh = a.sb("muh", [P, NB_IN])
        ones_s = a.sb("ones", [P, P])
        eps_s = a.sb("eps", [P, 1])
        w_s = [a.sb(f"w{i}", [P, KD * P]) for i in range(2)]
        w_hi = [a.sb(f"whi{i}", [P, KD, P], F32R) for i in range(2)]
        w_lo = [a.sb(f"wlo{i}", [P, KD, P], F32R) for i in range(2)]
        u_s = [a.sb(f"u{i}", [P, NS]) for i in range(2)]
        z_s = [a.sb(f"z{i}", [P, NS - 2]) for i in range(2)]
        t_s = a.sb("t", [P, NS - 2])
        banks = [a.ps(f"b{i}") for i in range(8)]

        par_in, x_in = sem("par_in"), sem("x_in")
        squares, sums, stds, rstds, normed = sem("squares"), sem("sums"), sem("stds"), sem("rstds"), sem("normed")
        h_hi_ready, h_lo_ready = sem("h_hi_ready"), sem("h_lo_ready")
        mu_ready, pads_zero = sem("mu_ready"), sem("pads_zero")
        w_loaded = [sem(f"w_loaded{i}") for i in range(2)]
        w_hi_ready, w_lo_ready = sem("w_hi_ready"), sem("w_lo_ready")
        u_product, u_copied, mixed, z_ready = sem("u_product"), sem("u_copied"), sem("mixed"), sem("z_ready")
        z_stored = [sem(f"z_stored{i}") for i in range(2)]
        z_free = [sem(f"z_free{i}") for i in range(2)]
        BODY = 2
        ROUNDS = (NB_IN - 1) // BODY

        with nc.Block() as block:

            @block.sync
            def _(sp):
                sp.dma_start(ones_s[:, :], ones).then_inc(par_in, 16)
                sp.dma_start(ln_s[:, :], ln_pre).then_inc(par_in, 16)
                sp.dma_start(mu_s[:, :], mu).then_inc(par_in, 16)
                for g in range(NTG):
                    if g:
                        sp.wait_ge(normed, g)
                    sp.dma_start(x_s[:, :, :], xT[g]).then_inc(x_in, 16)

                def load(j, slot):
                    sp.wait_ge(w_hi_ready, j + 1)
                    sp.wait_ge(w_lo_ready, j + 1)
                    sp.dma_start(w_s[slot][:, :], w_in[bass.ds(j, 1)].rearrange("a p n -> (a p) n"))\
                        .then_inc(w_loaded[slot], 16)

                with sp.Fori(0, ROUNDS) as i:
                    for s in range(BODY):
                        load(i * BODY + s, s)
                load(NB_IN - 1, 0)

            @block.gpsimd
            def _(pool):
                def store(j, slot, n):
                    pool.wait_ge(z_ready, j + 3)
                    dst = uT[bass.ds(j, 1)].rearrange("a p n -> (a p) n")
                    pool.dma_start(dst[:, 0:N_PROMPT], z_s[slot][:, 0:N_PROMPT]).then_inc(z_stored[slot], 16)
                    pool.dma_start(dst[:, N_PROMPT:N], z_s[slot][:, N_PROMPT + 2:N + 2])\
                        .then_inc(z_stored[slot], 16)
                    pool.wait_ge(z_stored[slot], n)
                    pool.sem_inc(z_free[slot], 1)

                for s in range(BODY):
                    pool.sem_inc(z_free[s], 1)
                with pool.Fori(0, ROUNDS) as i:
                    for s in range(BODY):
                        store(i * BODY + s, s, i * 32 + 32)
                store(NB_IN - 1, 0, 32 * ROUNDS + 32)

            @block.scalar
            def _(act):
                act.sem_inc(w_hi_ready, 2)
                act.sem_inc(u_copied, 2)
                act.wait_ge(pads_zero, 3)
                for g in range(NTG):
                    act.wait_ge(x_in, 16 * (g + 1))
                    if g:
                        act.wait_ge(h_lo_ready, g)
                    act.activation(h_s[:, :, :], x_s[:, :, :], ACT.Square).then_inc(squares, 1)
                    act.wait_ge(sums, g + 1)
                    act.activation(std[:, :], banks[g % 2][:, :], ACT.Sqrt, scale=1.0 / D,
                                   bias=eps_s[:, :]).then_inc(stds, 1)
                    act.wait_ge(normed, g + 1)
                    act.activation(h_hi[:, :, g * TG:(g + 1) * TG], h_s[:, :, :], ACT.Copy).then_inc(h_hi_ready, 1)

                def split(slot, loads, j):
                    act.wait_ge(w_loaded[slot], loads)
                    act.wait_ge(u_product, j + 1)
                    act.activation(w_hi[slot][:, :, :], w_s[slot][:, :].rearrange("p (k n) -> p k n", k=KD),
                                   ACT.Copy).then_inc(w_hi_ready, 1)

                def evacuate(slot, j):
                    act.wait_ge(u_product, j + 3)
                    act.wait_ge(z_ready, j + 1)
                    for g in range(NTG):
                        c = 1 + g * TG + (2 if g == 2 else 0)
                        ins = act.activation(u_s[slot][:, c:c + TG], banks[slot * NTG + g][:, :], ACT.Copy)
                    ins.then_inc(u_copied, 1)

                split(0, 16, 0)
                with act.Fori(0, ROUNDS) as i:
                    split(1, i * 16 + 16, i * BODY + 1)
                    evacuate(0, i * BODY)
                    split(0, i * 16 + 32, i * BODY + 2)
                    evacuate(1, i * BODY + 1)
                evacuate(0, NB_IN - 1)

            @block.vector
            def _(dve):
                dve.sem_inc(w_lo_ready, 2)
                dve.sem_inc(z_ready, 2)
                dve.memset(eps_s[:, :], EPS).then_inc(pads_zero, 1)
                for s in range(2):
                    dve.memset(u_s[s][:, :], 0.0).then_inc(pads_zero, 1)
                dve.wait_ge(par_in, 48)
                dve.tensor_scalar(mu1[:, :], mu_s[:, :], -1.0, 1.0, ALU.mult, ALU.add)
                dve.tensor_scalar(muh[:, :], mu_s[:, :], 0.5, None, ALU.mult).then_inc(mu_ready, 1)
                for g in range(NTG):
                    dve.wait_ge(stds, g + 1)
                    dve.reciprocal(rstd[:, :], std[:, :]).then_inc(rstds, 1)
                    dve.wait_ge(rstds, g + 1)
                    for k in range(KD):
                        ins = dve.scalar_tensor_tensor(out=h_s[:, k, :], in0=x_s[:, k, :], scalar=ln_s[:, k:k + 1],
                                                       in1=rstd[:, :], op0=ALU.mult, op1=ALU.mult)
                    ins.then_inc(normed, 1)
                    dve.wait_ge(normed, g + 1)
                    dve.wait_ge(h_hi_ready, g + 1)
                    dve.tensor_tensor(h_lo[:, :, g * TG:(g + 1) * TG], h_s[:, :, :],
                                      h_hi[:, :, g * TG:(g + 1) * TG].bitcast(F32), ALU.subtract)\
                        .then_inc(h_lo_ready, 1)

                def split(slot, j):
                    dve.wait_ge(w_hi_ready, j + 3)
                    dve.wait_ge(u_product, j + 1)
                    dve.tensor_tensor(w_lo[slot][:, :, :], w_s[slot][:, :].rearrange("p (k n) -> p k n", k=KD),
                                      w_hi[slot][:, :, :].bitcast(F32), ALU.subtract).then_inc(w_lo_ready, 1)

                def shift(slot, j, stored):
                    col = bass.ds(j, 1)
                    dve.wait_ge(u_copied, j + 3)
                    dve.wait_ge(z_free[slot], stored)
                    dve.wait_ge(z_ready, j + 2)
                    dve.tensor_tensor(t_s[:, :], u_s[slot][:, 0:NS - 2], u_s[slot][:, 2:NS], ALU.add)
                    dve.tensor_scalar(z_s[slot][:, :], u_s[slot][:, 1:NS - 1], mu1[:, col], None, ALU.mult)\
                        .then_inc(mixed, 1)
                    dve.wait_ge(mixed, j + 1)
                    dve.scalar_tensor_tensor(out=z_s[slot][:, :], in0=t_s[:, :], scalar=muh[:, col],
                                             in1=z_s[slot][:, :], op0=ALU.mult, op1=ALU.add).then_inc(z_ready, 1)

                dve.wait_ge(mu_ready, 1)
                split(0, 0)
                with dve.Fori(0, ROUNDS) as i:
                    split(1, i * BODY + 1)
                    shift(0, i * BODY, i + 1)
                    split(0, i * BODY + 2)
                    shift(1, i * BODY + 1, i + 1)
                shift(0, NB_IN - 1, ROUNDS + 1)

            @block.tensor
            def _(pe):
                pe.sem_inc(u_product, 2)
                pe.wait_ge(par_in, 48)
                for g in range(NTG):
                    pe.wait_ge(squares, g + 1)
                    if g >= 2:
                        pe.wait_ge(stds, g - 1)
                    for k in range(KD):
                        mm = pe.matmul(banks[g % 2][:, :], ones_s[:, :], h_s[:, k, :],
                                       start=k == 0, stop=k == KD - 1)
                    mm.then_inc(sums, 1)
                pe.wait_ge(stds, NTG)
                pe.wait_ge(h_lo_ready, NTG)

                def multiply(slot, j, copied):
                    pe.wait_ge(w_lo_ready, j + 3)
                    pe.wait_ge(w_hi_ready, j + 3)
                    pe.wait_ge(u_copied, copied)
                    for g in range(NTG):
                        t = slice(g * TG, (g + 1) * TG)
                        mm = product(pe, banks[slot * NTG + g][:, :],
                                     (lambda k: w_hi[slot][:, k, :], lambda k: w_lo[slot][:, k, :]),
                                     (lambda k: h_hi[:, k, t], lambda k: h_lo[:, k, t]), KD)
                    mm.then_inc(u_product, 1)

                with pe.Fori(0, ROUNDS) as i:
                    for s in range(BODY):
                        multiply(s, i * BODY + s, i * BODY + s + 1)
                multiply(0, NB_IN - 1, NB_IN)


def rope(nc, qkT, uT, gains, cos, sin, headsum, swap):
    ctx = ExitStack()
    with ctx:
        a = Arena(nc, ctx, "ro")
        sem = lambda name: ctx.enter_context(nc.semaphore("ro_" + name))
        NB = B_V
        q_s = [a.sb(f"q{i}", [P, N]) for i in range(2)]
        sq_s = a.sb("sq", [P, N])
        std = a.sb("std", [P, N])
        n_s = a.sb("n", [P, N])
        c_s = a.sb("c", [P, N])
        o_s = a.sb("o", [P, N])
        cos_s, sin_s = a.sb("cos", [P, N]), a.sb("sin", [P, N])
        g_s = a.sb("g", [P, NB])
        sum_s, swap_s, eps_s = a.sb("sum", [P, P]), a.sb("swap", [P, P]), a.sb("eps", [P, 1])
        sum_ps, rot_ps = a.ps("sums", [P, N]), a.ps("rot", [P, N])
        par_in, eps_set, q_in = sem("par_in"), sem("eps_set"), [sem("q_in0"), sem("q_in1")]
        squares, sums, stds, inverted, normed = sem("squares"), sem("sums"), sem("stds"), sem("inverted"), sem("normed")
        rotated, with_cos, with_sin, summed, stored = (
            sem("rotated"), sem("with_cos"), sem("with_sin"), sem("summed"), sem("stored"))

        with nc.Block() as block:

            @block.sync
            def _(sp):
                for tile, src in ((sum_s, headsum), (swap_s, swap), (g_s, gains), (cos_s, cos), (sin_s, sin)):
                    sp.dma_start(tile[:, :], src).then_inc(par_in, 16)
                for b in range(NB):
                    if b >= 2:
                        sp.wait_ge(normed, b - 1)
                    sp.dma_start(q_s[b % 2][:, :], uT[b]).then_inc(q_in[b % 2], 16)

            @block.gpsimd
            def _(pool):
                for b in range(NB):
                    pool.wait_ge(summed, b + 1)
                    pool.dma_start(qkT[b * P:(b + 1) * P, :], o_s[:, :]).then_inc(stored, 16)
                    pool.wait_ge(stored, 16 * (b + 1))

            @block.scalar
            def _(act):
                act.wait_ge(eps_set, 1)
                for b in range(NB):
                    act.wait_ge(q_in[b % 2], 16 * (b // 2 + 1))
                    if b:
                        act.wait_ge(sums, 3 * b)
                    act.activation(sq_s[:, :], q_s[b % 2][:, :], ACT.Square).then_inc(squares, 1)
                    if b:
                        act.wait_ge(normed, b)
                    for g in range(NTG):
                        act.wait_ge(sums, 3 * b + g + 1)
                        t = slice(g * TG, (g + 1) * TG)
                        act.activation(std[:, t], sum_ps[:, t], ACT.Sqrt, scale=1.0 / HD, bias=eps_s[:, :])\
                            .then_inc(stds, 1)

            @block.vector
            def _(dve):
                dve.memset(eps_s[:, :], EPS).then_inc(eps_set, 1)
                dve.wait_ge(par_in, 80)
                for b in range(NB):
                    dve.wait_ge(stds, 3 * b + 3)
                    dve.reciprocal(std[:, :], std[:, :]).then_inc(inverted, 1)
                    dve.wait_ge(inverted, b + 1)
                    if b:
                        dve.wait_ge(rotated, 3 * b)
                        dve.wait_ge(with_cos, b)
                    dve.scalar_tensor_tensor(out=n_s[:, :], in0=q_s[b % 2][:, :], scalar=g_s[:, b:b + 1],
                                             in1=std[:, :], op0=ALU.mult, op1=ALU.mult).then_inc(normed, 1)
                    dve.wait_ge(normed, b + 1)
                    if b:
                        dve.wait_ge(summed, b)
                        dve.wait_ge(stored, 16 * b)
                    dve.tensor_tensor(c_s[:, :], n_s[:, :], cos_s[:, :], ALU.mult).then_inc(with_cos, 1)
                    for g in range(NTG):
                        t = slice(g * TG, (g + 1) * TG)
                        dve.wait_ge(rotated, 3 * b + g + 1)
                        ins = dve.tensor_tensor(o_s[:, t], rot_ps[:, t], sin_s[:, t], ALU.mult)
                    ins.then_inc(with_sin, 1)
                    dve.wait_ge(with_sin, b + 1)
                    dve.wait_ge(with_cos, b + 1)
                    dve.tensor_tensor(o_s[:, :], o_s[:, :], c_s[:, :], ALU.add).then_inc(summed, 1)

            @block.tensor
            def _(pe):
                pe.wait_ge(par_in, 80)
                for b in range(NB):
                    pe.wait_ge(squares, b + 1)
                    if b:
                        pe.wait_ge(stds, 3 * b)
                    for g in range(NTG):
                        t = slice(g * TG, (g + 1) * TG)
                        pe.matmul(sum_ps[:, t], sum_s[:, :], sq_s[:, t], start=True, stop=True).then_inc(sums, 1)
                    pe.wait_ge(normed, b + 1)
                    if b:
                        pe.wait_ge(with_sin, b)
                    for g in range(NTG):
                        t = slice(g * TG, (g + 1) * TG)
                        pe.matmul(rot_ps[:, t], swap_s[:, :], n_s[:, t], start=True, stop=True).then_inc(rotated, 1)


def attention(nc, attnT, qkT, uT, ident, t0, n, tag):
    ctx = ExitStack()
    with ctx:
        a = Arena(nc, ctx, tag)
        sems = []

        def sem(name):
            sems.append(nc.alloc_semaphore(name=f"{tag}_{name}"))
            return sems[-1]

        NT, NG = n // P, n // TG
        NU = NT * NG
        SCALE = HD ** -0.5
        q_s = [a.sb(f"q{i}", [P, n]) for i in range(2)]
        k_s = [a.sb(f"k{i}", [P, n]) for i in range(2)]
        v_s = a.sb("v", [P, n])
        va = a.sb("va", [P, NT, 2, P])
        e_s = a.sb("e", [P, NT, n])
        vh = [a.sb(f"vh{i}", [P, NT, P]) for i in range(2)]
        o_s = [a.sb(f"o{i}", [HD, n]) for i in range(2)]
        mx = [a.sb(f"mx{i}", [P, NT]) for i in range(2)]
        mrow = [a.sb(f"mrow{i}", [NT, P]) for i in range(2)]
        rec = a.sb("rec", [HD, TG])
        id_s = a.sb("id", [P, P])
        first = [a.ps(f"first{i}", [P, NG * TG]) for i in range(2)]
        second = [a.ps(f"second{i}") for i in range(2)]
        third = [a.ps(f"third{i}") for i in range(2)]

        par_in, v_in, ones_set = sem("par_in"), sem("v_in"), sem("ones_set")
        v_turned, va_ready = sem("v_turned"), sem("va_ready")
        q_in, k_in = [sem("q_in0"), sem("q_in1")], [sem("k_in0"), sem("k_in1")]
        row_zero, row_in = sem("row_zero"), [sem("row_in0"), sem("row_in1")]
        scored, max_ready, max_turned, mrow_ready = sem("scored"), sem("max_ready"), sem("max_turned"), sem("mrow_ready")
        shifted, exp_ready, summed, norm_step = sem("shifted"), sem("exp_ready"), sem("summed"), sem("norm_step")
        vh_ready, o_stored, o_free = sem("vh_ready"), [sem("o_stored0"), sem("o_stored1")], sem("o_free")

        def heads(first_stage, second_stage):
            def both(eng):
                first_stage(0, 0, 0)
                with eng.Fori(0, HEADS // 2 - 1) as i:
                    first_stage(i * 2 + 1, 1, i)
                    second_stage(i * 2, 0, i)
                    first_stage(i * 2 + 2, 0, i + 1)
                    second_stage(i * 2 + 1, 1, i)
                last = HEADS // 2 - 1
                first_stage(HEADS - 1, 1, last)
                second_stage(HEADS - 2, 0, last)
                second_stage(HEADS - 1, 1, last)
            return both

        with nc.Block() as block:

            @block.sync
            def _(sp):
                sp.dma_start(id_s[:, :], ident).then_inc(par_in, 16)
                sp.dma_start(v_s[:, :], uT[B_V][:, t0:t0 + n]).then_inc(v_in, 16)

                def load(h, s, i):
                    sp.wait_ge(shifted, h * NU + NU)
                    sp.dma_start(q_s[s][0:HD, :], qkT[bass.ds(h * HD, HD), t0:t0 + n]).then_inc(q_in[s], 16)
                    kv = h // 4
                    sp.dma_start(k_s[s][0:HD, :], qkT[bass.ds(kv * HD + WIDTH, HD), t0:t0 + n])\
                        .then_inc(k_in[s], 16)

                def load_row(h, s, i):
                    sp.wait_ge(mrow_ready, h + 2)
                    sp.dma_start(q_s[s][HD:HD + 1, :].rearrange("a (t p) -> a t p", p=P), mrow[s][:, :])\
                        .then_inc(row_in[s], 16)

                load(0, 0, 0)
                load_row(0, 0, 0)
                with sp.Fori(0, HEADS // 2 - 1) as i:
                    load(i * 2 + 1, 1, i)
                    load_row(i * 2 + 1, 1, i)
                    load(i * 2 + 2, 0, i)
                    load_row(i * 2 + 2, 0, i)
                load(HEADS - 1, 1, 0)
                load_row(HEADS - 1, 1, 0)

            @block.gpsimd
            def _(pool):
                def values(h, s, i):
                    kv = h // 4
                    pool.wait_ge(summed, h * NG + NG)
                    pool.tensor_copy(vh[s][:, :, :], va[:, :, bass.ds(kv, 1), :].rearrange("p t a c -> p t (a c)"))\
                        .then_inc(vh_ready, 1)

                def store(h, s, i):
                    pool.wait_ge(norm_step, h * 2 * NG + 2 * NG + 2)
                    pool.dma_start(attnT[bass.ds(h * HD, HD), t0:t0 + n], o_s[s][:, :]).then_inc(o_stored[s], 16)
                    pool.wait_ge(o_stored[s], i * 16 + 16)
                    pool.sem_inc(o_free, 1)

                pool.sem_inc(o_free, 2)
                pool.wait_ge(va_ready, NT)
                heads(values, store)(pool)

            @block.scalar
            def _(act):
                def exponents(h, s, i):
                    for u in range(NU):
                        kt, g = u // NG, u % NG
                        act.wait_ge(shifted, h * NU + 2 * NU + u + 1)
                        act.activation(e_s[:, kt, g * TG:(g + 1) * TG], second[u % 2][:, :], ACT.Exp, scale=SCALE)\
                            .then_inc(exp_ready, 1)

                act.sem_inc(exp_ready, 2)
                heads(lambda *_: None, exponents)(act)

            @block.vector
            def _(dve):
                dve.sem_inc(mrow_ready, 1)
                dve.sem_inc(max_ready, 2)
                dve.sem_inc(norm_step, 2)
                for s in range(2):
                    dve.memset(k_s[s][HD:P, :], 0.0)
                    dve.memset(q_s[s][HD:P, :], 0.0)
                dve.memset(va[:, :, :, :], 1.0).then_inc(ones_set, 1)
                dve.wait_ge(ones_set, 1)
                for s in range(2):
                    dve.memset(k_s[s][HD:HD + 1, :], 1.0).then_inc(ones_set, 1)
                for t in range(NT):
                    dve.wait_ge(v_turned, t + 1)
                    dve.tensor_copy(va[:, t, :, 0:HD],
                                    third[t % 2][:, 0:P].rearrange("p (a b) -> p a b", a=2)).then_inc(va_ready, 1)

                def maxima(h, s, i):
                    dve.wait_ge(shifted, h * NU + NU)
                    dve.memset(q_s[s][HD:HD + 1, :], 0.0).then_inc(row_zero, 1)
                    for t in range(NT):
                        dve.wait_ge(scored, h * NT + t + 1)
                        dve.tensor_reduce(mx[s][:, t:t + 1], first[t % 2][:, :], AX.X, ALU.max).then_inc(max_ready, 1)
                    dve.wait_ge(max_turned, h + 1)
                    dve.tensor_scalar(mrow[s][:, :], first[0][0:NT, 0:P], -1.0, None, ALU.mult)\
                        .then_inc(mrow_ready, 1)

                def normalise(h, s, i):
                    dve.wait_ge(o_free, h + 1)
                    for g in range(NG):
                        n0 = h * 2 * NG + 2 * g + 2
                        dve.wait_ge(summed, h * NG + 2 * NG + g + 1)
                        dve.wait_ge(norm_step, n0)
                        dve.reciprocal(rec[:, :], third[g % 2][HD:P, :]).then_inc(norm_step, 1)
                        dve.wait_ge(norm_step, n0 + 1)
                        dve.tensor_tensor(o_s[s][:, g * TG:(g + 1) * TG], third[g % 2][0:HD, :], rec[:, :],
                                          ALU.mult).then_inc(norm_step, 1)

                dve.wait_ge(ones_set, 3)
                heads(maxima, normalise)(dve)

            @block.tensor
            def _(pe):
                pe.sem_inc(shifted, 2 * NU)
                pe.sem_inc(summed, 2 * NG)
                pe.wait_ge(par_in, 16)
                pe.wait_ge(v_in, 16)
                for t in range(NT):
                    if t >= 2:
                        pe.wait_ge(va_ready, t - 1)
                    pe.transpose(third[t % 2][:, 0:P], v_s[:, t * P:(t + 1) * P], id_s[:, :]).then_inc(v_turned, 1)
                pe.wait_ge(va_ready, NT)

                def scores(h, s, i):
                    pe.wait_ge(q_in[s], i * 16 + 16)
                    pe.wait_ge(k_in[s], i * 16 + 16)
                    pe.wait_ge(row_zero, h + 1)
                    pe.wait_ge(mrow_ready, h + 1)
                    for t in range(NT):
                        pe.wait_ge(max_ready, h * NT + t + 1)
                        for g in range(NG):
                            mm = pe.matmul(first[t % 2][:, g * TG:(g + 1) * TG], q_s[s][:, t * P:(t + 1) * P],
                                           k_s[s][:, g * TG:(g + 1) * TG], start=True, stop=True)
                        mm.then_inc(scored, 1)

                def turn_maxima(h, s):
                    pe.wait_ge(max_ready, h * NT + NT + 2)
                    pe.transpose(first[0][0:NT, 0:P], mx[s][:, :], id_s[:, :]).then_inc(max_turned, 1)

                def shifted_scores(h, s, i):
                    pe.wait_ge(row_in[s], i * 16 + 16)
                    for u in range(NU):
                        kt, g = u // NG, u % NG
                        pe.wait_ge(exp_ready, h * NU + u + 1)
                        pe.matmul(second[u % 2][:, :], k_s[s][:, kt * P:(kt + 1) * P],
                                  q_s[s][:, g * TG:(g + 1) * TG], start=True, stop=True).then_inc(shifted, 1)

                def with_values(h, s, i):
                    pe.wait_ge(vh_ready, h + 1)
                    for g in range(NG):
                        pe.wait_ge(norm_step, h * 2 * NG + 2)
                        for kt in range(NT):
                            if g == 0:
                                pe.wait_ge(exp_ready, h * NU + (kt + 1) * NG + 2)
                            mm = pe.matmul(third[g % 2][:, :], vh[s][:, kt, :], e_s[:, kt, g * TG:(g + 1) * TG],
                                           start=kt == 0, stop=kt == NT - 1)
                        mm.then_inc(summed, 1)

                def first_stage(h, s, i):
                    scores(h, s, i)
                    if isinstance(h, int) and h == 0:
                        turn_maxima(h, s)

                def second_stage(h, s, i):
                    shifted_scores(h, s, i)
                    if not (isinstance(h, int) and h == HEADS - 1):
                        turn_maxima(h + 1, 1 - s)
                    with_values(h, s, i)

                heads(first_stage, second_stage)(pe)
        nc.clear_and_free_semaphores(sems)
        nc.all_engine_barrier()

LEVELS = 6
PAIRS = KW


class Steps:
    CREDIT = 3

    def __init__(self, sem, names):
        self.sem, self.names, self.n = sem, names, len(names)
        self.at = {name: i + 1 for i, name in enumerate(names)}
        self.next = 0

    def start(self, eng):
        eng.sem_inc(self.sem, self.CREDIT * self.n)

    def value(self, rnd, name):
        return rnd * self.n + (self.CREDIT * self.n + self.at[name])

    def last(self, rnd, name):
        return rnd * self.n + ((self.CREDIT - 1) * self.n + self.at[name])

    def whole(self, rounds, back=0):
        return rounds * self.n + (self.CREDIT - back) * self.n

    def done(self, ins, name):
        assert self.names[self.next % self.n] == name, (name, self.names[self.next % self.n])
        self.next += 1
        ins.then_inc(self.sem, 1)


def recurrence(nc, y_out, bonusT, gT, uT, w_up, a_up, g_up, par, consts):
    ctx = ExitStack()
    with ctx:
        a = Arena(nc, ctx, "rw")
        sem = lambda name: ctx.enter_context(nc.semaphore("rw_" + name))
        C = DECAY_SCALE
        NPAR = 9
        K_K, K_A, R_K, W0, A0 = 0, 1, 2, 3, 5
        SLOTS = 3
        NS_CH = N_SAMPLE // P
        G_SAMPLE = N_PROMPT // TG
        wd_s, ad_s, gd_s = (a.sb(n, [P, N]) for n in ("wd", "ad", "gd"))
        par_s = a.sb("par", [P, NPAR, PAIRS])
        rkh_s, ka1_s = a.sb("rkh", [P, PAIRS]), a.sb("ka1", [P, PAIRS])
        hs_s, id_s = a.sb("hs", [P, P]), a.sb("id", [P, P])
        restart_s = a.sb("restart", [P, TG])
        causal_s, pair_s = a.sb("causal", [P, 2, 2, P]), a.sb("pair", [P, 2, P])
        level_s = a.sb("level", [P, 2, LEVELS, P])
        wup_s, aup_s, gup_s = a.sb("wup", [P, 2, P]), a.sb("aup", [P, 2, P]), a.sb("gup", [P, P])
        r_s, k_s, v_s = (a.sb(n, [P, TG]) for n in ("r", "k", "v"))
        bo_s, gt_s = (a.sb(n, [P, TG]) for n in ("bo", "gt"))
        x_s = [a.sb(f"x{d}", [P, 4, N]) for d in range(2)]
        mid_s, end_s, scale_s = (a.sb(n, [P, 2, NCH]) for n in ("mid", "end", "scale"))
        vt_s, vp_s = a.sb("vt", [P, NCH, P]), a.sb("vp", [P, NCH, 2, P])
        y_s = a.sb("y", [P, NCH, WIDTH])
        kk_s, t_s, kb_s, sq_s = (a.sb(n, [P, TG]) for n in ("kk", "t", "kb", "sq"))
        sig_s, al_s, cum_s = ([a.sb(f"{n}{d}", [P, TG]) for d in range(2)] for n in ("sig", "al", "cum"))
        e_s = [a.sb(f"e{i}", [P, TG]) for i in range(3)]
        pad_s = [a.sb(f"pad{d}", [P, 4, P]) for d in range(2)]
        ab_s, ak_s = ([[a.sb(f"{n}{s}{d}", [P, 4 * P]) for d in range(2)] for s in range(SLOTS)] for n in ("ab", "ak"))
        bk_s = [a.sb(f"bk{s}", [P, 2, 2, P]) for s in range(2)]
        Z = [[a.sb(f"Z{s}{d}", [P, 2 * P]) for d in range(2)] for s in range(2)]
        X = [a.sb(f"X{s}", [P, 2, 2 * P]) for s in range(2)]
        T = [a.sb(f"T{d}", [P, 2 * P]) for d in range(2)]
        p_s = [a.sb(f"p{d}", [P, P]) for d in range(2)]
        up_s = [a.sb(f"up{d}", [P, 2, P]) for d in range(2)]
        uf_s = [a.sb(f"uf{d}", [P, P]) for d in range(2)]
        S = [a.sb(f"S{d}", [P, P]) for d in range(2)]
        banks = [a.ps(f"b{i}") for i in range(8)]
        FR, INV, SN, PR = banks[0:2], banks[2:4], banks[4:6], banks[6:8]

        const_in, lora_in, w_in = sem("const_in"), sem("lora_in"), sem("w_in")
        r_in, k_in, v_in = sem("r_in"), sem("k_in"), sem("v_in")
        bonus_stored, g_stored, y_stored = sem("bonus_stored"), sem("g_stored"), sem("y_stored")
        zeroed, lora_ready, par_ready = sem("zeroed"), sem("lora_ready"), sem("par_ready")
        exps_done, scales_done, holds = sem("exps_done"), sem("scales_done"), [sem("hold0"), sem("hold1")]

        D2 = range(2)
        dve_prep = Steps(sem("dve_prep"), [
            "kkraw", "cum0", "mid0", "end0", "cum1", "mid1", "end1", "clamp", "invert", "kk", "kfac0", "kfac1",
            "kb", "rb", "centre0", "before0", "bonus", "vp0", "vp1",
            "xr0", "xa0", "xb0", "xk0", "centre1", "before1", "xr1", "xa1", "xb1", "xk1"])
        act_prep = Steps(sem("act_prep"), [
            "sig0", "sig1", "al0", "al1", "square", "norm", "g", "vt",
            *(f"{n}{d}" for d in D2 for n in ("er", "ea", "eb"))])
        pool_prep = Steps(sem("pool_prep"), ["kdir0", "kdir1", "kka0", "kka1"])
        pe_prep = Steps(sem("pe_prep"), ["xw0", "xw1", "xa0", "xa1", "sumsq", "xg", "turnv", "sumrb"])
        pool_front = Steps(sem("pool_front"), ["pad0", "pad1", "Zp0", "Zp1", "Z0", "Z1"])
        pe_front = Steps(sem("pe_front"), ["ab0", "ak0", "ab1", "ak1", "X", "bk"])
        dve_front = Steps(sem("dve_front"), ["ab0", "ak0", "ab1", "ak1"])
        act_front = Steps(sem("act_front"), ["X", "bk"])
        END = LEVELS - 1
        pe_level = Steps(sem("pe_level"), [
            *(f"{m}{n}_{d}" for n in range(END) for m in ("T", "X", "Z") for d in D2),
            *(f"{m}{END}_{d}" for m in ("T", "Z") for d in D2)])
        dve_level = Steps(sem("dve_level"), [
            *(f"{m}{n}_{d}" for n in range(END) for m in ("T", "X") for d in D2),
            *(f"{m}{END}_{d}" for m in ("T", "Z") for d in D2)])
        act_level = Steps(sem("act_level"), [f"Z{n}_{d}" for n in range(END) for d in D2])
        pe_scan = Steps(sem("pe_scan"), [f"{m}_{d}" for m in ("p", "u", "ys") for d in D2])
        dve_scan = Steps(sem("dve_scan"), [f"{m}_{d}" for m in ("up", "y") for d in D2])
        act_scan = Steps(sem("act_scan"), [*(f"{m}_{d}" for m in ("p", "uf") for d in D2),
                                           *(f"S{h}_{d}" for d in D2 for h in range(2))])

        def cols(r, d):
            c = NCH - 1 - r if d else (r + NCH - NS_CH if r < NS_CH else r - NS_CH)
            return c, slice(c * P, (c + 1) * P)

        PIECES = 9

        def pair(p, last, prep, scales, front, level, scan):
            for r in range(NCH):
                for n in range(LEVELS):
                    slot = r * LEVELS + n
                    level(p, r, n, "T")
                    if r:
                        scan(p, r - 1, 2 * n)
                    level(p, r, n, "X" if n < END else "end")
                    if r:
                        scan(p, r - 1, 2 * n + 1)
                    if n < END:
                        level(p, r, n, "Z")
                    if r < NCH - 1:
                        front(p, r + 1, n)
                    if slot < 2 * PIECES:
                        prep(p, slot // PIECES, slot % PIECES, p * 3 + slot // PIECES + 1)
                    elif slot == 2 * PIECES:
                        scales(p, 0, N_PROMPT // P, p * 2 + 1)
                    first = 6 * LEVELS
                    if not last and first <= slot < first + 2 * PIECES and slot % 2 == 0:
                        prep(p + 1, G_SAMPLE, (slot - first) // 2, p * 3 + 3)
                    elif not last and slot == first + 2 * PIECES:
                        scales(p + 1, N_PROMPT // P, NCH, p * 2 + 2)
            for n in range(LEVELS):
                scan(p, NCH - 1, 2 * n)
                scan(p, NCH - 1, 2 * n + 1)
                if not last:
                    front(p + 1, 0, n)

        def pairs(eng, *stages):
            prep, scales, front = stages[:3]
            for piece in range(PIECES):
                prep(0, G_SAMPLE, piece, 0)
            scales(0, N_PROMPT // P, NCH, 0)
            for n in range(LEVELS):
                front(0, 0, n)
            with eng.Fori(0, PAIRS - 1) as p:
                pair(p, False, *stages)
            pair(PAIRS - 1, True, *stages)

        def nothing(*_):
            pass

        def heads(ap):
            return ap.rearrange("p (h n) -> p h n", n=P)

        def both(mask):
            return mask.unsqueeze(1).broadcast_to([P, 2, P])

        def round_of(p, r):
            return p * NCH + r

        with nc.Block() as block:

            @block.sync
            def _(sp):
                for tile, src in ((par_s, par), (hs_s, consts["headsum"]), (id_s, consts["ident"]),
                                  (restart_s, consts["restart"])):
                    sp.dma_start(tile[:], src).then_inc(const_in, 16)
                sp.dma_start(causal_s[:, :, :, :], consts["causal"].rearrange("d a p n -> p d a n")).then_inc(const_in, 16)
                sp.dma_start(pair_s[:, :, :], consts["pair"].rearrange("d p n -> p d n")).then_inc(const_in, 16)
                for d in D2:
                    sp.dma_start(level_s[:, d, :, :], consts["levels"][d].rearrange("l p n -> p l n"))\
                        .then_inc(const_in, 16)
                for tile, b in ((wd_s, B_WD), (ad_s, B_AD), (gd_s, B_GD)):
                    sp.dma_start(tile[:, :], uT[b]).then_inc(lora_in, 16)
                sp.sem_inc(bonus_stored, 16)
                sp.sem_inc(g_stored, 16)
                sp.wait_ge(zeroed, 1)
                with sp.Fori(0, PAIRS) as p:
                    sp.wait_ge(pe_prep.sem, pe_prep.whole(p * NTG))
                    for src, tile in ((w_up, wup_s), (a_up, aup_s)):
                        for d in D2:
                            h = slice(d * HD, (d + 1) * HD)
                            sp.dma_start(tile[h, d, :], src[bass.ds(p, 1), h, :].rearrange("a p n -> (a p) n"))\
                                .then_inc(w_in, 16)
                    sp.dma_start(gup_s[:, :], g_up[bass.ds(p, 1)].rearrange("a p n -> (a p) n")).then_inc(w_in, 16)
                    for i, g in enumerate((G_SAMPLE, 0, 1)):
                        it, t = p * NTG + i, slice(g * TG, (g + 1) * TG)
                        sp.wait_ge(dve_prep.sem, dve_prep.whole(it))
                        sp.wait_ge(pe_prep.sem, pe_prep.whole(it))
                        sp.wait_ge(pool_prep.sem, pool_prep.whole(it))
                        hold(sp, holds[1])
                        for tile, b, s in ((k_s, B_RK, k_in), (v_s, B_RV, v_in), (r_s, B_R, r_in)):
                            sp.dma_start(tile[:, :], uT[bass.ds(p + b, 1), :, t].rearrange("a p n -> (a p) n"))\
                                .then_inc(s, 16)
                        dst = lambda z: z[bass.ds(p, 1), :, t].rearrange("a p n -> (a p) n")
                        sp.wait_ge(act_prep.sem, act_prep.value(it, "g"))
                        hold(sp, holds[1])
                        sp.dma_start(dst(gT), gt_s[:, :]).then_inc(g_stored, 16)
                        sp.wait_ge(dve_prep.sem, dve_prep.value(it, "bonus"))
                        sp.dma_start(dst(bonusT), bo_s[:, :]).then_inc(bonus_stored, 16)
                sp.wait_ge(dve_scan.sem, dve_scan.whole(PAIRS * NCH))
                sp.dma_start(y_out, y_s[:, :, :]).then_inc(y_stored, 16)
                sp.wait_ge(y_stored, 16)
                sp.wait_ge(bonus_stored, 16 * (PAIRS * NTG + 1))
                sp.wait_ge(g_stored, 16 * (PAIRS * NTG + 1))

            @block.gpsimd
            def _(pool):
                pool_prep.start(pool)
                pool_front.start(pool)
                pool.wait_ge(const_in, 16 * 8)
                pool.wait_ge(zeroed, 1)

                def prep(p, g, piece, it):
                    if piece == 4:
                        for d in D2:
                            kd = (kb_s, t_s)[d]
                            if d:
                                pool.wait_ge(pool_prep.sem, pool_prep.value(it, "kdir0"))
                            pool.wait_ge(dve_prep.sem, dve_prep.value(it, f"kfac{d}"))
                            pool_prep.done(pool.tensor_tensor(kd[:, :], kd[:, :], k_s[:, :], ALU.mult), f"kdir{d}")
                        for d in D2:
                            pool.wait_ge(pool_prep.sem, pool_prep.value(it, ("kdir1", "kka0")[d]))
                            pool_prep.done(pool.tensor_tensor(al_s[d][:, :], al_s[d][:, :], kk_s[:, :], ALU.mult),
                                           f"kka{d}")

                def front(p, r, n):
                    it, s = round_of(p, r), r % SLOTS
                    if n == 0:
                        if r in (0, NS_CH):
                            pool.wait_ge(dve_prep.sem, dve_prep.whole(p * 3 + (1 if r == 0 else 3)))
                        pool.wait_ge(pe_front.sem, pe_front.last(it, "ak1"))
                        four = lambda ap: ap.broadcast_to([P, 2, 2, P])
                        for d in D2:
                            pool.wait_ge(pool_front.sem, pool_front.last(it, "Z1") if d == 0 else
                                         pool_front.value(it, "pad0"))
                            pool_front.done(pool.tensor_tensor(
                                pad_s[d][:, :, :].rearrange("p (a h) n -> p a h n", a=2),
                                four(x_s[d][:, 0:2, cols(r, d)[1]].unsqueeze(2)),
                                four(hs_s[:, 0:P:HD].unsqueeze(1).unsqueeze(3)), ALU.mult), f"pad{d}")
                    if n == 3:
                        pool.wait_ge(pe_scan.sem, pe_scan.value(it - 2, "u_1"))
                        for d in D2:
                            pool.wait_ge(pool_front.sem, pool_front.value(it, ("pad1", "Zp0")[d]))
                            pool.wait_ge(dve_front.sem, dve_front.value(it, f"ab{d}"))
                            pool_front.done(pool.tensor_tensor(heads(Z[r % 2][d][:, :]), heads(ab_s[s][d][:, 0:2 * P]),
                                                               both(pair_s[:, d, :]), ALU.mult), f"Zp{d}")
                        for d in D2:
                            pool.wait_ge(pool_front.sem, pool_front.value(it, ("Zp1", "Z0")[d]))
                            z = heads(Z[r % 2][d][:, :])
                            pool_front.done(pool.tensor_tensor(z, z, both(id_s[:, :]), ALU.add), f"Z{d}")

                pairs(pool, prep, nothing, front, nothing, nothing)

            @block.scalar
            def _(act):
                for steps in (act_prep, act_front, act_level, act_scan):
                    steps.start(act)
                act.wait_ge(lora_in, 48)
                act.activation(wd_s[:, :], wd_s[:, :], ACT.Tanh).then_inc(lora_ready, 1)
                act.activation(gd_s[:, :], gd_s[:, :], ACT.Sigmoid).then_inc(lora_ready, 1)
                act.wait_ge(const_in, 16 * 8)
                act.wait_ge(zeroed, 1)
                par = lambda n, p: par_s[:, n, bass.ds(p, 1)]

                def prep(p, g, piece, it):
                    done = act_prep.done

                    def pe_did(name):
                        act.wait_ge(pe_prep.sem, pe_prep.value(it, name))

                    if piece == 0:
                        act.wait_ge(dve_prep.sem, dve_prep.whole(it))
                        act.wait_ge(pool_prep.sem, pool_prep.whole(it))
                        for d in D2:
                            pe_did(f"xw{d}")
                            hold(act, holds[0])
                            done(act.activation(sig_s[d][:, :], PR[d][:, :], ACT.Sigmoid, bias=par(W0 + d, p)), f"sig{d}")
                    if piece == 1:
                        for d in D2:
                            pe_did(f"xa{d}")
                            hold(act, holds[0])
                            done(act.activation(al_s[d][:, :], PR[d][:, :], ACT.Sigmoid, bias=par(A0 + d, p)), f"al{d}")
                        act.wait_ge(dve_prep.sem, dve_prep.value(it, "kkraw"))
                        act.wait_ge(pe_prep.sem, pe_prep.whole(it))
                        done(act.activation(sq_s[:, :], kk_s[:, :], ACT.Square), "square")
                    if piece == 2:
                        pe_did("sumsq")
                        done(act.activation(t_s[:, :], PR[0][:, :], ACT.Sqrt), "norm")
                        act.wait_ge(g_stored, it * 16 + 16)
                        pe_did("xg")
                        done(act.activation(gt_s[:, :], PR[1][:, :], ACT.Copy), "g")
                    if piece == 3:
                        if g != G_SAMPLE:
                            act.wait_ge(pe_scan.sem, pe_scan.whole(p * NCH))
                        elif not (isinstance(p, int) and p == 0):
                            act.wait_ge(pe_scan.sem, pe_scan.whole(p * NCH, NCH - NS_CH))
                        pe_did("turnv")
                        done(act.activation(vt_s[:, 4 * g:4 * g + 4, :].rearrange("p a b -> p (a b)"), PR[1][:, :],
                                            ACT.Copy), "vt")
                    for d in D2:
                        if piece == 6 + d:
                            at, before = cum_s[d], sig_s[d]
                            act.wait_ge(dve_prep.sem, dve_prep.value(it, f"before{d}"))
                            for n, (src, scale) in enumerate(((at, -C), (before, -C), (at, C)) if d == 0 else
                                                             ((before, C), (at, C), (before, -C))):
                                if d:
                                    act.wait_ge(dve_prep.sem, dve_prep.value(it, ("xr0", "xa0", "xk0")[n]))
                                done(act.activation(e_s[n][:, :], src[:, :], ACT.Exp, scale=scale),
                                     ("er", "ea", "eb")[n] + str(d))

                def scales(p, c0, c1, n):
                    act.wait_ge(dve_prep.sem, dve_prep.whole(p * 3 + (1 if c0 else 3)))
                    for tile in (mid_s, end_s):
                        act.activation(tile[:, :, c0:c1], tile[:, :, c0:c1], ACT.Exp, scale=-C).then_inc(exps_done, 1)

                def front(p, r, n):
                    it, s = round_of(p, r), r % SLOTS
                    if n == 4:
                        act.wait_ge(dve_level.sem, dve_level.whole(it, 1))
                        act.wait_ge(pe_front.sem, pe_front.value(it, "X"))
                        act_front.done(act.activation(X[r % 2][:, :, :].rearrange("p a n -> p (a n)"), FR[0][:, :],
                                                      ACT.Copy), "X")
                    if n == 5:
                        act.wait_ge(pe_scan.sem, pe_scan.value(it - 2, "ys_1"))
                        act.wait_ge(pe_front.sem, pe_front.value(it, "bk"))
                        act_front.done(act.activation(bk_s[r % 2][:, :, :, :].rearrange("p a b n -> p (a b n)"),
                                                      FR[1][:, :], ACT.Copy), "bk")

                def level(p, r, n, part):
                    it, s = round_of(p, r), r % SLOTS
                    if part == "Z":
                        for d in D2:
                            act.wait_ge(pe_level.sem, pe_level.value(it, f"Z{n}_{d}"))
                            act_level.done(act.activation(Z[r % 2][d][:, :], INV[d][:, 0:2 * P], ACT.Copy), f"Z{n}_{d}")

                def scan(p, r, n):
                    it = round_of(p, r)
                    for d in D2:
                        if n == d:
                            act.wait_ge(pe_scan.sem, pe_scan.value(it, f"p_{d}"))
                            act_scan.done(act.activation(p_s[d][:, :], SN[d][:, 0:P], ACT.Copy), f"p_{d}")
                        if n == 2 + d:
                            act.wait_ge(dve_scan.sem, dve_scan.value(it, f"up_{d}"))
                            act_scan.done(act.activation(uf_s[d][:, :].rearrange("p (h n) -> p h n", h=2),
                                                         bass_diag(SN[d][:, P:3 * P]), ACT.Copy), f"uf_{d}")
                        if n == 6 + 3 * d:
                            if d == 0 and r in (0, NS_CH):
                                act.wait_ge(scales_done, p * 2 + (3 if r == 0 else 4))
                            c = cols(r, d)[0]
                            act.wait_ge(pe_scan.sem, pe_scan.value(it, f"ys_{d}"))
                            for h in range(2):
                                q = slice(h * HD, (h + 1) * HD)
                                act_scan.done(act.activation(S[d][q, q], SN[d][q, q], ACT.Copy,
                                                             scale=scale_s[q, d, c:c + 1]), f"S{h}_{d}")

                pairs(act, prep, scales, front, level, scan)

            @block.vector
            def _(dve):
                for steps in (dve_prep, dve_front, dve_level, dve_scan):
                    steps.start(dve)
                dve.sem_inc(scales_done, 2)
                for tile in (wup_s, aup_s, vp_s, y_s, scale_s, *up_s, *S):
                    ins = dve.memset(tile[:], 0.0)
                ins.then_inc(zeroed, 1)
                dve.wait_ge(zeroed, 1)
                dve.wait_ge(const_in, 16 * 8)
                dve.tensor_scalar(rkh_s[:, :], par_s[:, R_K, :], 0.5, None, ALU.mult)
                dve.tensor_scalar(ka1_s[:, :], par_s[:, K_A, :], -1.0, 1.0, ALU.mult, ALU.add).then_inc(par_ready, 1)
                dve.wait_ge(par_ready, 1)
                par = lambda n, p: par_s[:, n, bass.ds(p, 1)]
                chunks = lambda tile: tile[:, :].rearrange("p (c n) -> p c n", n=P)

                def prep(p, g, piece, it):
                    def own(name):
                        dve.wait_ge(dve_prep.sem, dve_prep.value(it, name))

                    def act_did(name):
                        dve.wait_ge(act_prep.sem, act_prep.value(it, name))

                    done = dve_prep.done
                    t, c4 = slice(g * TG, (g + 1) * TG), slice(4 * g, 4 * g + 4)

                    def total(d):
                        act_did(f"sig{d}")
                        done(dve.tensor_tensor_scan(cum_s[d][:, :], restart_s[:, :], sig_s[d][:, :], 0.0,
                                                    ALU.mult, ALU.add), f"cum{d}")
                        own(f"cum{d}")
                        done(dve.tensor_copy(mid_s[:, d, c4], chunks(cum_s[d])[:, :, P // 2 - 1]), f"mid{d}")
                        done(dve.tensor_tensor(end_s[:, d, c4], chunks(cum_s[d])[:, :, P - 1],
                                               chunks(cum_s[d])[:, :, P // 2 - 1], ALU.subtract), f"end{d}")

                    def centre(d):
                        own(f"end{d}")
                        done(dve.tensor_tensor(chunks(cum_s[d]), chunks(cum_s[d]),
                                               mid_s[:, d, c4].unsqueeze(2).broadcast_to([P, 4, P]),
                                               ALU.subtract), f"centre{d}")
                        own(f"centre{d}")
                        done(dve.tensor_tensor(sig_s[d][:, :], cum_s[d][:, :], sig_s[d][:, :], ALU.subtract),
                             f"before{d}")

                    def inputs(d):
                        act_did(f"er{d}")
                        done(dve.tensor_tensor(x_s[d][:, 1, t], r_s[:, :], e_s[0][:, :], ALU.mult), f"xr{d}")
                        act_did(f"ea{d}")
                        done(dve.scalar_tensor_tensor(out=x_s[d][:, 0, t], in0=kk_s[:, :], scalar=-1.0, in1=e_s[1][:, :],
                                                      op0=ALU.mult, op1=ALU.mult), f"xa{d}")
                        act_did(f"eb{d}")
                        done(dve.tensor_tensor(x_s[d][:, 2, t], al_s[d][:, :], e_s[2][:, :], ALU.mult), f"xb{d}")
                        done(dve.tensor_tensor(x_s[d][:, 3, t], (kb_s, t_s)[d][:, :], e_s[2][:, :], ALU.mult), f"xk{d}")

                    if piece == 1:
                        dve.wait_ge(scales_done, p * 2 + (1 if g == G_SAMPLE else 2))
                        dve.wait_ge(k_in, it * 16 + 16)
                        dve.wait_ge(dve_prep.sem, dve_prep.whole(it))
                        dve.wait_ge(pool_prep.sem, pool_prep.whole(it))
                        done(dve.tensor_scalar(kk_s[:, :], k_s[:, :], par(K_K, p), None, ALU.mult), "kkraw")
                        total(0)
                    if piece == 2:
                        total(1)
                    if piece == 3:
                        act_did("norm")
                        done(dve.tensor_scalar(t_s[:, :], t_s[:, :], 1e-12, None, ALU.max), "clamp")
                        own("clamp")
                        done(dve.reciprocal(t_s[:, :], t_s[:, :]), "invert")
                        own("invert")
                        done(dve.tensor_tensor(kk_s[:, :], kk_s[:, :], t_s[:, :], ALU.mult), "kk")
                    if piece == 4:
                        own("kk")
                        for d in D2:
                            act_did(f"al{d}")
                            done(dve.tensor_scalar((kb_s, t_s)[d][:, :], al_s[d][:, :], par(K_A, p),
                                                   ka1_s[:, bass.ds(p, 1)], ALU.mult, ALU.add), f"kfac{d}")
                    if piece == 5:
                        act_did("square")
                        dve.wait_ge(pe_prep.sem, pe_prep.value(it, "sumsq"))
                        dve.wait_ge(pool_prep.sem, pool_prep.value(it, "kdir1"))
                        done(dve.tensor_tensor(sq_s[:, :], kb_s[:, :], t_s[:, :], ALU.add), "kb")
                        own("kb")
                        dve.wait_ge(r_in, it * 16 + 16)
                        done(dve.scalar_tensor_tensor(out=sq_s[:, :], in0=r_s[:, :], scalar=rkh_s[:, bass.ds(p, 1)],
                                                      in1=sq_s[:, :], op0=ALU.mult, op1=ALU.mult), "rb")
                        centre(0)
                    if piece == 6:
                        dve.wait_ge(pe_prep.sem, pe_prep.value(it, "sumrb"))
                        dve.wait_ge(v_in, it * 16 + 16)
                        dve.wait_ge(bonus_stored, it * 16 + 16)
                        done(dve.tensor_tensor(bo_s[:, :], PR[0][:, :], v_s[:, :], ALU.mult), "bonus")
                        act_did("vt")
                        for h in range(2):
                            q = slice(h * HD, (h + 1) * HD)
                            done(dve.tensor_copy(vp_s[:, c4, h, q], vt_s[:, c4, q]), f"vp{h}")
                    if piece == 7:
                        dve.wait_ge(pool_prep.sem, pool_prep.value(it, "kka1"))
                        inputs(0)
                        centre(1)
                    if piece == 8:
                        inputs(1)

                def scales(p, c0, c1, n):
                    dve.wait_ge(exps_done, 2 * n + 2)
                    dve.tensor_tensor(scale_s[:, 0, c0:c1 - 1], end_s[:, 0, c0:c1 - 1], mid_s[:, 0, c0 + 1:c1], ALU.mult)
                    dve.tensor_tensor(scale_s[:, 1, c0 + 1:c1], mid_s[:, 1, c0 + 1:c1], end_s[:, 1, c0:c1 - 1],
                                      ALU.mult).then_inc(scales_done, 1)

                def front(p, r, n):
                    it, s = round_of(p, r), r % SLOTS
                    if n == 0:
                        dve.wait_ge(pe_scan.sem, pe_scan.whole(it, 2))
                    if n < 4:
                        d, m = n // 2, n % 2
                        tile, name = ((ab_s, "ab"), (ak_s, "ak"))[m]
                        dve.wait_ge(pe_front.sem, pe_front.value(it, f"{name}{d}"))
                        four = lambda ap: ap.rearrange("p (a h n) -> p a h n", a=2, h=2)
                        mask = causal_s[:, d, :, :].unsqueeze(2).broadcast_to([P, 2, 2, P])
                        dve_front.done(dve.tensor_tensor(four(tile[s][d][:, :]), four(FR[m][:, :]), mask, ALU.mult),
                                       f"{name}{d}")

                def level(p, r, n, part):
                    it, s = round_of(p, r), r % SLOTS
                    for d in D2:
                        if part == "T":
                            dve.wait_ge(pe_level.sem, pe_level.value(it, f"T{n}_{d}"))
                            dve_level.done(dve.tensor_tensor(heads(T[d][:, :]), heads(INV[d][:, 0:2 * P]),
                                                             both(level_s[:, d, n, :]), ALU.mult), f"T{n}_{d}")
                        if part == "X":
                            dve.wait_ge(pe_level.sem, pe_level.value(it, f"X{n}_{d}"))
                            x = X[r % 2][:, d, :]
                            dve_level.done(dve.tensor_tensor(x, INV[d][:, 2 * P:4 * P], x, ALU.add), f"X{n}_{d}")
                        if part == "end":
                            dve.wait_ge(pe_level.sem, pe_level.value(it, f"Z{n}_{d}"))
                            dve_level.done(dve.tensor_tensor(Z[r % 2][d][:, :], INV[d][:, 2 * P:4 * P], Z[r % 2][d][:, :],
                                                             ALU.add), f"Z{n}_{d}")

                def scan(p, r, n):
                    it = round_of(p, r)
                    for d in D2:
                        if n == 2 + d:
                            dve.wait_ge(pe_scan.sem, pe_scan.value(it, f"u_{d}"))
                            dve_scan.done(dve.tensor_copy(bass_diag(up_s[d][:, :, :].rearrange("p h n -> p (h n)")),
                                                          bass_diag(SN[d][:, P:3 * P])), f"up_{d}")
                        if n == 7 + 3 * d:
                            dve.wait_ge(act_scan.sem, act_scan.value(it, f"S1_{d}"))
                            c = cols(r, d)[0]
                            y = y_s[:, c, bass.ds(p * P, P)]
                            dve_scan.done(dve.tensor_tensor(y, SN[d][:, 3 * P:4 * P], y, ALU.add), f"y_{d}")

                pairs(dve, prep, scales, front, level, scan)

            @block.tensor
            def _(pe):
                for steps in (pe_prep, pe_front, pe_level, pe_scan):
                    steps.start(pe)
                pe.wait_ge(const_in, 16 * 8)
                pe.wait_ge(lora_ready, 2)
                head = lambda h: slice(h * P, (h + 1) * P)

                def prep(p, g, piece, it):
                    done = pe_prep.done
                    t = slice(g * TG, (g + 1) * TG)

                    def act_did(name):
                        pe.wait_ge(act_prep.sem, act_prep.value(it, name))

                    if piece == 0:
                        pe.wait_ge(w_in, p * 80 + 80)
                        pe.wait_ge(act_prep.sem, act_prep.whole(it))
                        pe.wait_ge(dve_prep.sem, dve_prep.whole(it))
                        for d in D2:
                            done(pe.matmul(PR[d][:, :], wup_s[:, d, :], wd_s[:, t], start=True, stop=True), f"xw{d}")
                    if piece == 1:
                        for d in D2:
                            act_did(f"sig{d}")
                            done(pe.matmul(PR[d][:, :], aup_s[:, d, :], ad_s[:, t], start=True, stop=True), f"xa{d}")
                    if piece == 2:
                        act_did("square")
                        done(pe.matmul(PR[0][:, :], hs_s[:, :], sq_s[:, :], start=True, stop=True), "sumsq")
                        done(pe.matmul(PR[1][:, :], gup_s[:, :], gd_s[:, t], start=True, stop=True), "xg")
                    if piece == 3:
                        pe.wait_ge(v_in, it * 16 + 16)
                        act_did("g")
                        for c in range(4):
                            mm = pe.transpose(PR[1][:, c * P:(c + 1) * P], v_s[:, c * P:(c + 1) * P], id_s[:, :])
                        done(mm, "turnv")
                    if piece == 5:
                        pe.wait_ge(dve_prep.sem, dve_prep.value(it, "rb"))
                        done(pe.matmul(PR[0][:, :], hs_s[:, :], sq_s[:, :], start=True, stop=True), "sumrb")

                def front(p, r, n):
                    it, s = round_of(p, r), r % SLOTS
                    done = pe_front.done
                    if n == 0 and r in (0, NS_CH):
                        pe.wait_ge(dve_prep.sem, dve_prep.whole(p * 3 + (1 if r == 0 else 3)))
                        pe.wait_ge(act_prep.sem, act_prep.whole(p * 3 + (1 if r == 0 else 3)))
                    if n < 4:
                        d, m = n // 2, n % 2
                        name = ("ab", "ak")[m]
                        pe.wait_ge(pool_front.sem, pool_front.value(it, f"pad{d}"))
                        if d:
                            pe.wait_ge(dve_front.sem, dve_front.value(it, f"{name}0"))
                        else:
                            pe.wait_ge(act_front.sem, act_front.last(it, ("X", "bk")[m]))
                        done(pe.matmul(FR[m][:, :], x_s[d][:, 2 + m, cols(r, d)[1]],
                                       pad_s[d][:, :, :].rearrange("p a n -> p (a n)"), start=True, stop=True),
                             f"{name}{d}")
                    if n == 4:
                        pe.wait_ge(dve_front.sem, dve_front.value(it, "ab1"))
                        pe.wait_ge(pool_front.sem, pool_front.value(it, "Z1"))
                        for d in D2:
                            for h in range(2):
                                mm = pe.transpose(FR[0][:, head(2 * d + h)], Z[r % 2][d][:, head(h)], id_s[:, :])
                        done(mm, "X")
                    if n == 5:
                        pe.wait_ge(dve_front.sem, dve_front.value(it, "ak1"))
                        for d in D2:
                            for m in range(2):
                                mm = pe.transpose(FR[1][:, head(2 * d + m)], x_s[d][:, 2 + m, cols(r, d)[1]], id_s[:, :])
                        done(mm, "bk")

                def level(p, r, n, part):
                    it, s = round_of(p, r), r % SLOTS
                    done = pe_level.done
                    for d in D2:
                        x = lambda h: X[r % 2][:, d, head(h)]
                        if part == "T":
                            if n:
                                pe.wait_ge(act_level.sem, act_level.value(it, f"Z{n - 1}_{d}"))
                            elif d == 0:
                                pe.wait_ge(act_front.sem, act_front.value(it, "X"))
                                pe.wait_ge(dve_level.sem, dve_level.last(it, f"Z{END}_1"))
                            for h in range(2):
                                mm = pe.matmul(INV[d][:, head(h)], ab_s[s][d][:, head(h)], x(h), start=True, stop=True)
                            done(mm, f"T{n}_{d}")
                        if part == "X":
                            pe.wait_ge(dve_level.sem, dve_level.value(it, f"T{n}_{d}"))
                            for h in range(2):
                                mm = pe.matmul(INV[d][:, head(2 + h)], Z[r % 2][d][:, head(h)], T[d][:, head(h)],
                                               start=True, stop=True)
                            done(mm, f"X{n}_{d}")
                        if part == "Z":
                            pe.wait_ge(dve_level.sem, dve_level.value(it, f"X{n}_{d}"))
                            for h in range(2):
                                mm = pe.transpose(INV[d][:, head(h)], x(h), id_s[:, :])
                            done(mm, f"Z{n}_{d}")
                        if part == "end":
                            pe.wait_ge(dve_level.sem, dve_level.value(it, f"T{n}_{d}"))
                            for h in range(2):
                                mm = pe.matmul(INV[d][:, head(2 + h)], T[d][:, head(h)], Z[r % 2][d][:, head(h)],
                                               start=True, stop=True)
                            done(mm, f"Z{n}_{d}")

                def scan(p, r, n):
                    it, s = round_of(p, r), r % SLOTS
                    done = pe_scan.done
                    vp = lambda h: vp_s[:, cols(r, d)[0], h, :]
                    act_did = lambda name: pe.wait_ge(act_scan.sem, act_scan.value(it, name))
                    for d in D2:
                        c, t = cols(r, d)
                        if n == d:
                            pe.wait_ge(dve_scan.sem, dve_scan.last(it, f"y_{d}"))
                            pe.wait_ge(act_scan.sem, act_scan.last(it, f"S1_{d}"))
                            pe.matmul(SN[d][:, 0:P], x_s[d][:, 0, t], S[d][:, :], start=True, stop=False)
                            for h in range(2):
                                mm = pe.matmul(SN[d][:, 0:P], ak_s[s][d][:, head(h)], vp(h), start=False, stop=h == 1)
                            done(mm, f"p_{d}")
                        if n == 2 + d:
                            if d == 0:
                                pe.wait_ge(dve_level.sem, dve_level.value(it, f"Z{END}_1"))
                            act_did(f"p_{d}")
                            for h in range(2):
                                mm = pe.matmul(SN[d][:, head(1 + h)], Z[r % 2][d][:, head(h)], p_s[d][:, :],
                                               start=True, stop=True)
                            done(mm, f"u_{d}")
                        Y = SN[d][:, 3 * P:4 * P]
                        if n == 4 + 3 * d:
                            act_did(f"uf_{d}")
                            pe.matmul(Y, x_s[d][:, 1, t], S[d][:, :], start=True, stop=False)
                            for h in range(2):
                                pe.matmul(Y, ak_s[s][d][:, head(2 + h)], vp(h), start=False, stop=False)
                        if n == 5 + 3 * d:
                            for h in range(2):
                                pe.matmul(Y, ab_s[s][d][:, head(2 + h)], up_s[d][:, h, :], start=False, stop=h == 1)
                        if n == 6 + 3 * d:
                            if d == 0:
                                pe.wait_ge(act_front.sem, act_front.value(it, "bk"))
                            pe.matmul(SN[d][:, 0:P], id_s[:, :], S[d][:, :], start=True, stop=False)
                            pe.matmul(SN[d][:, 0:P], bk_s[r % 2][:, d, 0, :], uf_s[d][:, :], start=False, stop=False)
                            mm = pe.matmul(SN[d][:, 0:P], bk_s[r % 2][:, d, 1, :], vt_s[:, c, :], start=False, stop=True)
                            done(mm, f"ys_{d}")

                pairs(pe, prep, nothing, front, level, scan)


def bass_diag(ap):
    return ap.rearrange("p (x n) -> p x n", n=HD)[:, 0:4:3, :]


def branch_output(nc, rwkvT, y_in, bonusT, gT, par, ident):
    ctx = ExitStack()
    with ctx:
        a = Arena(nc, ctx, "bo")
        sem = lambda name: ctx.enter_context(nc.semaphore("bo_" + name))
        LN_W, LN_B = 7, 8
        CG, H4 = TG // P, TG // P * HEADS
        y_s = [a.sb(f"y{i}", [P, CG, WIDTH]) for i in range(2)]
        sq_s = a.sb("sq", [P, CG * WIDTH])
        mean, var = a.sb("mean", [P, H4]), a.sb("var", [P, H4])
        bo_s = [a.sb(f"bo{i}", [P, KW, TG]) for i in range(2)]
        g_s = [a.sb(f"g{i}", [P, KW, TG]) for i in range(2)]
        par_s, id_s, eps_s = a.sb("par", [P, 9, PAIRS]), a.sb("id", [P, P]), a.sb("eps", [P, 1])
        banks = [a.ps(f"b{i}") for i in range(8)]
        par_in, eps_set = sem("par_in"), sem("eps_set")
        y_in_sb, bo_in, g_in = ([sem(f"{n}{i}") for i in range(2)] for n in ("y_in", "bo_in", "g_in"))
        stat, squares, stds, turned, mixed, stored = (
            sem("stat"), sem("squares"), sem("stds"), sem("turned"), sem("mixed"), sem("stored"))
        STAT = 6

        with nc.Block() as block:

            @block.sync
            def _(sp):
                sp.dma_start(par_s[:, :, :], par).then_inc(par_in, 16)
                sp.dma_start(id_s[:, :], ident).then_inc(par_in, 16)
                for g in range(NTG):
                    t = slice(g * TG, (g + 1) * TG)
                    if g >= 2:
                        sp.wait_ge(stored, 16 * (g - 1))
                        sp.wait_ge(turned, KW * (g - 1))
                    sp.dma_start(y_s[g % 2][:, :, :], y_in[:, g * CG:(g + 1) * CG, :]).then_inc(y_in_sb[g % 2], 16)
                    for tile, src, s in ((bo_s, bonusT, bo_in), (g_s, gT, g_in)):
                        sp.dma_start(tile[g % 2][:, :, :], src[:, :, t].rearrange("k p n -> p k n"))\
                            .then_inc(s[g % 2], 16)

            @block.gpsimd
            def _(pool):
                for g in range(NTG):
                    pool.wait_ge(mixed, 2 * KW * (g + 1))
                    pool.dma_start(rwkvT[:, :, g * TG:(g + 1) * TG].rearrange("k p n -> p k n"), bo_s[g % 2][:, :, :])\
                        .then_inc(stored, 16)
                    pool.wait_ge(stored, 16 * (g + 1))

            @block.scalar
            def _(act):
                act.wait_ge(eps_set, 1)
                for g in range(NTG):
                    act.wait_ge(stat, STAT * g + 3)
                    act.activation(sq_s[:, :], y_s[g % 2][:, :, :].rearrange("p c n -> p (c n)"), ACT.Square)\
                        .then_inc(squares, 1)
                    act.wait_ge(stat, STAT * g + 4)
                    act.activation(var[:, :], var[:, :], ACT.Sqrt, scale=1.0 / HD, bias=eps_s[:, :]).then_inc(stds, 1)

            @block.vector
            def _(dve):
                dve.memset(eps_s[:, :], LNX_EPS).then_inc(eps_set, 1)
                dve.wait_ge(par_in, 32)
                for g in range(NTG):
                    y = y_s[g % 2][:, :, :].rearrange("p c (h n) -> p (c h) n", n=HD)
                    over = lambda s: s[:, :].unsqueeze(2).broadcast_to([P, H4, HD])
                    dve.wait_ge(y_in_sb[g % 2], 16 * (g // 2 + 1))
                    dve.tensor_reduce(mean[:, :], y, AX.X, ALU.add).then_inc(stat, 1)
                    dve.wait_ge(stat, STAT * g + 1)
                    dve.tensor_scalar(mean[:, :], mean[:, :], 1.0 / HD, None, ALU.mult).then_inc(stat, 1)
                    dve.wait_ge(stat, STAT * g + 2)
                    dve.tensor_tensor(y, y, over(mean), ALU.subtract).then_inc(stat, 1)
                    dve.wait_ge(squares, g + 1)
                    dve.tensor_reduce(var[:, :], sq_s[:, :].rearrange("p (h n) -> p h n", n=HD), AX.X, ALU.add)\
                        .then_inc(stat, 1)
                    dve.wait_ge(stds, g + 1)
                    dve.reciprocal(var[:, :], var[:, :]).then_inc(stat, 1)
                    dve.wait_ge(stat, STAT * g + 5)
                    dve.tensor_tensor(y, y, over(var), ALU.mult).then_inc(stat, 1)
                    dve.wait_ge(bo_in[g % 2], 16 * (g // 2 + 1))
                    dve.wait_ge(g_in[g % 2], 16 * (g // 2 + 1))
                    for b in range(KW):
                        dve.wait_ge(turned, KW * g + b + 1)
                        o = bo_s[g % 2][:, b, :]
                        dve.scalar_tensor_tensor(out=o, in0=banks[(g * KW + b) % 8][:, :], scalar=par_s[:, LN_W, b:b + 1],
                                                 in1=o, op0=ALU.mult, op1=ALU.add).then_inc(mixed, 1)
                        dve.wait_ge(mixed, 2 * (KW * g + b) + 1)
                        dve.scalar_tensor_tensor(out=o, in0=o, scalar=par_s[:, LN_B, b:b + 1], in1=g_s[g % 2][:, b, :],
                                                 op0=ALU.add, op1=ALU.mult).then_inc(mixed, 1)

            @block.tensor
            def _(pe):
                pe.wait_ge(par_in, 32)
                for g in range(NTG):
                    pe.wait_ge(stat, STAT * (g + 1))
                    if g >= 2:
                        pe.wait_ge(mixed, 2 * KW * (g - 1))
                    for b in range(KW):
                        for c in range(CG):
                            mm = pe.transpose(banks[(g * KW + b) % 8][:, c * P:(c + 1) * P],
                                              y_s[g % 2][:, c, b * P:(b + 1) * P], id_s[:, :])
                        mm.then_inc(turned, 1)


def finish(nc, yT, xT, attnT, rwkvT, weights, ln_pre, ln_post, ln_ffn_pre, ln_ffn_post, ones):
    ctx = ExitStack()
    with ctx:
        a = Arena(nc, ctx, "fi")
        sem = lambda name: ctx.enter_context(nc.semaphore("fi_" + name))
        RING = 4
        AHEAD = 2
        FFN_KT = (8, 8, KF - 16)
        J_OUT, J_FFN, J_LAST = 3 * KD, 4 * KD, 4 * KD + 2 * KF
        JOBS = J_LAST + 3 * KD
        assert JOBS % RING == 0
        x_s = a.sb("x", [P, KD, TG])
        m_s = a.sb("m", [P, KD, TG])
        ln_s = [a.sb(f"ln{i}", [P, KD]) for i in range(4)]
        ones_s = a.sb("ones", [P, P])
        eps_s = a.sb("eps", [P, 1])
        h_hi = a.sb("h_hi", [P, KD, TG], F32R)
        h_lo = a.sb("h_lo", [P, KD, TG], F32R)
        w_s = [a.sb(f"w{i}", [P, KD * P]) for i in range(RING)]
        w_hi = [a.sb(f"whi{i}", [P, KD, P], F32R) for i in range(RING)]
        w_lo = [a.sb(f"wlo{i}", [P, KD, P], F32R) for i in range(RING)]
        s_s = [a.sb(f"s{i}", [P, TG]) for i in range(2)]
        p_s = a.sb("p", [P, TG])
        std, rstd = s_s[0], p_s
        with ExitStack() as first:
            b = Arena(nc, first, "fi")
            br_s = b.sb("br", [P, 2 * KW, TG])
            br_hi = b.sb("br_hi", [P, 2 * KW, TG], F32R)
            br_lo = b.sb("br_lo", [P, 2 * KW, TG], F32R)
            g_hi = b.sb("g_hi", [P, KD, TG], F32R)
            g_lo = b.sb("g_lo", [P, KD, TG], F32R)
            q_s = b.sb("q", [P, TG])
        f_hi = a.sb("f_hi", [P, KF, TG], F32R)
        f_lo = a.sb("f_lo", [P, KF, TG], F32R)
        banks = [a.ps(f"b{i}") for i in range(8)]
        SUM = banks[7]

        par_in, eps_set, x_in, br_in = sem("par_in"), sem("eps_set"), sem("x_in"), [sem("br_in0"), sem("br_in1")]
        squares, sums, stds, rstds = sem("squares"), sem("sums"), sem("stds"), sem("rstds")
        normed, h_hi_ready, h_lo_ready = sem("normed"), sem("h_hi_ready"), sem("h_lo_ready")
        br_hi_ready, br_lo_ready = sem("br_hi_ready"), sem("br_lo_ready")
        w_loaded = [sem(f"w_loaded{i}") for i in range(RING)]
        w_hi_ready, w_lo_ready, product_done = sem("w_hi_ready"), sem("w_lo_ready"), sem("product_done")
        gate_ready, gated, merge_step = sem("gate_ready"), sem("gated"), sem("merge_step")
        out_copied, scaled, x2_ready = sem("out_copied"), sem("scaled"), sem("x2_ready")
        silu_ready, ffn_step = sem("silu_ready"), sem("ffn_step")
        ffn_copied, y_stored = sem("ffn_copied"), sem("y_stored")
        holds = [sem("hold0"), sem("hold1")]

        def jobs(eng, t, job, after):
            j0 = t * JOBS
            with eng.Fori(0, KD // 4) as i:
                for s in range(12):
                    row = i * 12 + s
                    j, k = j0 + row, i * 4 + s // 3
                    job(j, s, KD, "merge", k, row)
                    after("gate" if s % 3 < 2 else "merge", k, s, j)
            for k in range(KD):
                job(j0 + J_OUT + k, k, KD, "out", k, J_OUT + k)
                after("out", k, k, j0 + J_OUT + k)
            after("mixed", 0, 0, 0)
            with eng.Fori(0, KF // 2) as i:
                for s in range(4):
                    row = i * 4 + J_FFN + s
                    j, k = j0 + row, i * 2 + s // 2
                    job(j, s, KD, "ffn_in", k, row)
                    after("silu" if s % 2 == 0 else "ffn_in", k, s, j)
            for s in range(3 * KD):
                job(j0 + J_LAST + s, s, FFN_KT[s % 3], "ffn_out", s // 3, J_LAST + s)
                if s % 3 == 2:
                    after("ffn_out", s // 3, s, j0 + J_LAST + s)
            after("done", 0, 0, 0)

        def nothing(*_):
            pass

        with nc.Block() as block:

            @block.sync
            def _(sp):
                sp.dma_start(ones_s[:, :], ones).then_inc(par_in, 16)
                for tile, src in zip(ln_s, (ln_pre, ln_post, ln_ffn_pre, ln_ffn_post)):
                    sp.dma_start(tile[:, :], src).then_inc(par_in, 16)

                def load(j, s, row, kt):
                    sp.wait_ge(w_lo_ready, j + 1)
                    sp.dma_start(w_s[s % RING][:, 0:kt * P],
                                 weights[bass.ds(row, 1)].rearrange("a p n -> (a p) n")[:, 0:kt * P])\
                        .then_inc(w_loaded[s % RING], 16)

                with sp.Fori(0, NTG) as t:
                    jobs(sp, t, lambda j, s, kt, kind, k, row: load(j, s, row, kt), nothing)
                for s in range(AHEAD):
                    load(NTG * JOBS + s, s, s, KD)

            @block.gpsimd
            def _(pool):
                pool.sem_inc(w_lo_ready, RING)

                def split(j, s, kt, kind, k, row):
                    pool.wait_ge(w_hi_ready, j + 1)
                    pool.tensor_tensor(w_lo[s % RING][:, 0:kt, :],
                                       w_s[s % RING][:, 0:kt * P].rearrange("p (k n) -> p k n", k=kt),
                                       w_hi[s % RING][:, 0:kt, :].bitcast(F32), ALU.subtract)\
                        .then_inc(w_lo_ready, 1)

                with pool.Fori(0, NTG) as t:
                    pool.dma_start(x_s[:, :, :], xT[bass.ds(t, 1)].rearrange("a p k n -> (a p) k n"))\
                        .then_inc(x_in, 16)
                    for b, src in enumerate((attnT, rwkvT)):
                        pool.dma_start(br_s[:, b * KW:(b + 1) * KW, :],
                                       src[:, :, bass.ds(t * TG, TG)].rearrange("k p n -> p k n"))\
                            .then_inc(br_in[b], 16)
                    jobs(pool, t, split, nothing)
                    pool.wait_ge(x2_ready, t * 16 + 16)
                    hold(pool, holds[0])
                    pool.dma_start(yT[bass.ds(t, 1)].rearrange("a p k n -> (a p) k n"), x_s[:, :, :])\
                        .then_inc(y_stored, 16)
                    pool.wait_ge(y_stored, t * 16 + 16)

            @block.scalar
            def _(act):
                def split(j, s):
                    act.wait_ge(w_loaded[s % RING], 4 * (j - s % RING) + 16)
                    act.wait_ge(product_done, j + 1)
                    act.activation(w_hi[s % RING][:, :, :], w_s[s % RING][:, :].rearrange("p (k n) -> p k n", k=KD),
                                   ACT.Copy).then_inc(w_hi_ready, 1)

                act.wait_ge(eps_set, 1)
                for s in range(AHEAD):
                    split(s, s)
                with act.Fori(0, NTG) as t:
                    def root(n):
                        act.wait_ge(sums, t * 32 + 8 * n)
                        act.activation(std[:, :], SUM[:, :], ACT.Sqrt, scale=1.0 / D, bias=eps_s[:, :])\
                            .then_inc(stds, 1)

                    def h_high(n):
                        for k in range(KD):
                            act.wait_ge(normed, t * 16 + n * KD + k + 1)
                            act.activation(h_hi[:, k, :], m_s[:, k, :], ACT.Copy).then_inc(h_hi_ready, 1)

                    act.wait_ge(x_in, t * 16 + 16)
                    for k in range(KD):
                        act.activation(m_s[:, k, :], x_s[:, k, :], ACT.Square).then_inc(squares, 1)
                    root(1)
                    for b in range(2):
                        act.wait_ge(br_in[b], t * 16 + 16)
                    act.activation(br_hi[:, :, :], br_s[:, :, :], ACT.Copy).then_inc(br_hi_ready, 1)
                    h_high(0)

                    def after(kind, k, s, j):
                        if kind == "gate":
                            act.wait_ge(product_done, j + RING + 1)
                            act.wait_ge(gated, t * KD + k + 2)
                            act.activation(s_s[s % 3][:, :], banks[s // 3 % 2 * 4 + s % 3][:, :], ACT.Sigmoid)\
                                .then_inc(gate_ready, 1)
                        if kind in ("out", "ffn_out"):
                            copied, base = (out_copied, 8) if kind == "out" else (ffn_copied, 24)
                            act.wait_ge(copied, t * KD + k + (5 if kind == "out" else 3))
                            if k >= 2:
                                act.wait_ge(sums, t * 32 + base + k - 1)
                            act.activation(s_s[k % 2][:, :], m_s[:, k, :], ACT.Square).then_inc(squares, 1)
                        if kind == "mixed":
                            root(2)
                            for k in range(KD):
                                act.wait_ge(x2_ready, t * 16 + k + 1)
                                act.activation(m_s[:, k, :], x_s[:, k, :], ACT.Square).then_inc(squares, 1)
                            root(3)
                            h_high(1)
                        if kind == "silu":
                            act.wait_ge(product_done, j + RING + 1)
                            act.wait_ge(ffn_step, t * 3 * KF + 3 * k + 1)
                            act.activation(s_s[s // 2][:, :], banks[s // 2 * 2][:, :], ACT.Silu)\
                                .then_inc(silu_ready, 1)
                        if kind == "done":
                            root(4)

                    jobs(act, t, lambda j, s, kt, kind, k, row: split(j + AHEAD, s + AHEAD), after)

            @block.vector
            def _(dve):
                dve.memset(eps_s[:, :], EPS).then_inc(eps_set, 1)
                dve.sem_inc(gated, 2)
                dve.sem_inc(merge_step, 1)
                dve.sem_inc(out_copied, 4)
                dve.sem_inc(ffn_step, 6)
                dve.sem_inc(ffn_copied, 2)
                dve.wait_ge(par_in, 80)
                with dve.Fori(0, NTG) as t:
                    def invert(n):
                        dve.wait_ge(stds, t * 4 + n + 1)
                        dve.reciprocal(rstd[:, :], std[:, :]).then_inc(rstds, 1)
                        dve.wait_ge(rstds, t * 4 + n)

                    def norm(n, ln):
                        invert(2 * n + 1)
                        for k in range(KD):
                            dve.scalar_tensor_tensor(out=m_s[:, k, :], in0=x_s[:, k, :], scalar=ln[:, k:k + 1],
                                                     in1=rstd[:, :], op0=ALU.mult, op1=ALU.mult).then_inc(normed, 1)
                        for k in range(KD):
                            dve.wait_ge(h_hi_ready, t * 16 + n * KD + k + 1)
                            dve.tensor_tensor(h_lo[:, k, :], m_s[:, k, :], h_hi[:, k, :].bitcast(F32), ALU.subtract)\
                                .then_inc(h_lo_ready, 1)

                    def add_normed(n, ln):
                        invert(2 * n + 2)
                        for k in range(KD):
                            dve.scalar_tensor_tensor(out=m_s[:, k, :], in0=m_s[:, k, :], scalar=ln[:, k:k + 1],
                                                     in1=rstd[:, :], op0=ALU.mult, op1=ALU.mult).then_inc(scaled, 1)
                            dve.wait_ge(scaled, t * 16 + n * KD + k + 1)
                            dve.tensor_tensor(x_s[:, k, :], x_s[:, k, :], m_s[:, k, :], ALU.add).then_inc(x2_ready, 1)

                    norm(0, ln_s[0])
                    dve.wait_ge(br_hi_ready, t + 1)
                    dve.tensor_tensor(br_lo[:, :, :], br_s[:, :, :], br_hi[:, :, :].bitcast(F32), ALU.subtract)\
                        .then_inc(br_lo_ready, 1)

                    def three(step, n, hi, lo, k):
                        dve.wait_ge(step, n)
                        dve.tensor_copy(hi[:, bass.ds(k, 1), :], p_s[:, :].rearrange("p (a n) -> p a n", a=1))\
                            .then_inc(step, 1)
                        dve.wait_ge(step, n + 1)
                        dve.tensor_tensor(lo[:, bass.ds(k, 1), :], p_s[:, :].rearrange("p (a n) -> p a n", a=1),
                                          hi[:, bass.ds(k, 1), :].bitcast(F32), ALU.subtract).then_inc(step, 1)

                    def after(kind, k, s, j):
                        if kind == "merge":
                            bank = s // 3 % 2 * 4
                            n = t * 3 * KD + 3 * k + 1
                            dve.wait_ge(gate_ready, t * 2 * KD + 2 * k + 2)
                            dve.wait_ge(product_done, j + RING + 1)
                            dve.wait_ge(merge_step, n)
                            dve.tensor_tensor(p_s[:, :], s_s[0][:, :], banks[bank + 2][:, :], ALU.mult)
                            dve.tensor_tensor(q_s[:, :], s_s[1][:, :], banks[bank + 3][:, :], ALU.mult)\
                                .then_inc(gated, 1)
                            dve.wait_ge(gated, t * KD + k + 3)
                            dve.tensor_tensor(p_s[:, :], p_s[:, :], q_s[:, :], ALU.add).then_inc(merge_step, 1)
                            three(merge_step, n + 1, g_hi, g_lo, k)
                        if kind in ("out", "ffn_out"):
                            dve.wait_ge(product_done, j + RING + 1)
                            if kind == "out":
                                dve.tensor_copy(m_s[:, k, :], banks[k % 4][:, :]).then_inc(out_copied, 1)
                            else:
                                dve.tensor_copy(m_s[:, k, :], banks[4 + k % 2][:, :]).then_inc(ffn_copied, 1)
                        if kind == "mixed":
                            add_normed(0, ln_s[1])
                            norm(1, ln_s[2])
                        if kind == "ffn_in":
                            n = t * 3 * KF + 3 * k + 6
                            dve.wait_ge(silu_ready, t * KF + k + 1)
                            dve.wait_ge(product_done, j + RING + 1)
                            dve.wait_ge(ffn_step, n)
                            dve.tensor_tensor(p_s[:, :], s_s[s // 2][:, :], banks[s // 2 * 2 + 1][:, :], ALU.mult)\
                                .then_inc(ffn_step, 1)
                            three(ffn_step, n + 1, f_hi, f_lo, k)
                        if kind == "done":
                            add_normed(1, ln_s[3])

                    jobs(dve, t, nothing, after)

            @block.tensor
            def _(pe):
                pe.sem_inc(product_done, RING)
                pe.sem_inc(stds, 1)
                pe.wait_ge(par_in, 80)
                with pe.Fori(0, NTG) as t:
                    def add_squares(n, k, sq):
                        if k == 0:
                            pe.wait_ge(stds, t * 4 + n)
                        pe.wait_ge(squares, t * 32 + (n - 1) * KD + k + 1)
                        pe.matmul(SUM[:, :], ones_s[:, :], sq, start=k == 0, stop=k == KD - 1)\
                            .then_inc(sums, 1)

                    for k in range(KD):
                        add_squares(1, k, m_s[:, k, :])
                    pe.wait_ge(h_lo_ready, t * 16 + KD)
                    pe.wait_ge(br_lo_ready, t + 1)
                    hold(pe, holds[1])

                    def job(j, s, kt, kind, k, row):
                        pe.wait_ge(w_lo_ready, j + RING + 1)
                        whi, wlo = w_hi[s % RING], w_lo[s % RING]

                        def part(out, w0, n, xs, **flags):
                            return product(pe, out[:, :], (lambda k: whi[:, w0 + k, :], lambda k: wlo[:, w0 + k, :]),
                                           tuple((lambda k, x=x: x[:, k, :]) for x in xs), n, **flags)

                        if kind == "merge":
                            bank = s // 3 % 2 * 4
                            if s % 3 == 0:
                                pe.wait_ge(gated, t * KD + k + 1)
                            if s % 3 < 2:
                                mm = part(banks[bank + s % 3], 0, KD, (h_hi, h_lo))
                            else:
                                part(banks[bank + 2], 0, KW, (br_hi[:, 0:KW, :], br_lo[:, 0:KW, :]))
                                mm = part(banks[bank + 3], KW, KW, (br_hi[:, KW:2 * KW, :], br_lo[:, KW:2 * KW, :]))
                        elif kind == "out":
                            if s == 0:
                                pe.wait_ge(merge_step, (t + 1) * 3 * KD + 1)
                            pe.wait_ge(out_copied, t * KD + s + 1)
                            mm = part(banks[s % 4], 0, KD, (g_hi, g_lo))
                        elif kind == "ffn_in":
                            if s % 2 == 0:
                                pe.wait_ge(ffn_step, t * 3 * KF + 3 * k + 1)
                            mm = part(banks[s], 0, KD, (h_hi, h_lo))
                        else:
                            if s == 0:
                                pe.wait_ge(ffn_step, (t + 1) * 3 * KF + 6)
                            if s % 3 == 0:
                                pe.wait_ge(ffn_copied, t * KD + s // 3 + 1)
                            k0 = 8 * (s % 3)
                            mm = part(banks[4 + s // 3 % 2], 0, kt, (f_hi[:, k0:k0 + kt, :], f_lo[:, k0:k0 + kt, :]),
                                      start=s % 3 == 0, stop=s % 3 == 2)
                        mm.then_inc(product_done, 1)

                    def after(kind, k, s, j):
                        if kind in ("out", "ffn_out") and k >= 1:
                            add_squares(2 if kind == "out" else 4, k - 1, s_s[(k - 1) % 2][:, :])
                        if kind == "mixed":
                            add_squares(2, KD - 1, s_s[1][:, :])
                            for k in range(KD):
                                add_squares(3, k, m_s[:, k, :])
                            pe.wait_ge(h_lo_ready, t * 16 + 2 * KD)
                            hold(pe, holds[1])
                        if kind == "done":
                            add_squares(4, KD - 1, s_s[1][:, :])

                    jobs(pe, t, job, after)


def blocks(w):
    k, c = w.shape
    return np.ascontiguousarray(w.reshape(k // P, P, c // P, P).transpose(2, 1, 0, 3)).reshape(c // P, P, k)


def columns(v):
    return np.ascontiguousarray(v.reshape(-1, P).T)


def shape_constants():
    r = np.arange(P)
    c = {}
    c["ones"] = np.ones((P, P), np.float32)
    c["ident"] = np.eye(P, dtype=np.float32)
    c["headsum"] = (r[:, None] // HD == r[None, :] // HD).astype(np.float32)
    swap = np.zeros((P, P), np.float32)
    e = np.arange(0, P, 2)
    swap[e + 1, e] = -1.0
    swap[e, e + 1] = 1.0
    c["swap"] = swap
    t = np.arange(N_PROMPT)
    nf = HD // 4
    inv = (ROPE_THETA ** (-np.arange(nf, dtype=np.float32) / nf)).astype(np.float32)
    ang = np.concatenate([(t // GRID_W).astype(np.float32)[:, None] * inv,
                          (t % GRID_W).astype(np.float32)[:, None] * inv], -1)
    tab = ang[:, (r % HD) // 2].T
    tab = np.concatenate([tab, tab[:, :N_SAMPLE]], 1)
    c["cos"], c["sin"] = np.cos(tab).astype(np.float32), np.sin(tab).astype(np.float32)
    s, q = r[:, None], r[None, :]
    strict = [(s < q), (s > q)]
    loose = [(s <= q), (s >= q)]
    c["causal"] = np.stack([np.stack([strict[d], loose[d]]) for d in range(2)]).astype(np.float32)
    c["pair"] = np.stack([strict[d] & (s // 2 == q // 2) for d in range(2)]).astype(np.float32)
    levels = np.zeros((2, LEVELS, P, P), np.float32)
    for d in range(2):
        for n in range(LEVELS):
            m = 2 << n
            levels[d, n] = (s // (2 * m) == q // (2 * m)) & ((s // m) % 2 == 1 - d) & ((q // m) % 2 == d)
    c["levels"] = levels
    c["restart"] = np.where(np.arange(TG) % P == 0, 0.0, 1.0).astype(np.float32)[None].repeat(P, 0)
    return {n: np.ascontiguousarray(x) for n, x in c.items()}


PARAMS = ("k_k", "k_a", "r_k", "w0", "a0", "lnx_w", "lnx_b")
CONSTS = ("ones", "ident", "headsum", "swap", "cos", "sin", "causal", "pair", "levels", "restart")


def build(nc, at):
    def scratch(name, shape):
        return nc.dram_tensor(name, shape, F32, kind="Internal").ap()

    uT = scratch("uT", [NB_IN, P, N])
    qkT = scratch("qkT", [(B_V - B_Q) * P, N])
    attnT = scratch("attnT", [WIDTH, N])
    y = scratch("y", [P, NCH, WIDTH])
    bonusT, gT, rwkvT = (scratch(n, [KW, P, N]) for n in ("bonusT", "gT", "rwkvT"))
    with nc.sbuf_tensor("h_hi", [P, KD, N], F32R) as h_hi, nc.sbuf_tensor("h_lo", [P, KD, N], F32R) as h_lo:
        project(nc, (h_hi, h_lo), uT, at["xT"], at["w_in"], at["ln_mix_pre"], at["mu"], at["ones"])
    rope(nc, qkT, uT, at["gains"], at["cos"], at["sin"], at["headsum"], at["swap"])
    attention(nc, attnT, qkT, uT, at["ident"], 0, N_PROMPT, "ap")
    attention(nc, attnT, qkT, uT, at["ident"], N_PROMPT, N_SAMPLE, "as")
    recurrence(nc, y, bonusT, gT, uT, at["w_up"], at["a_up"], at["g_up"], at["par"], at)
    branch_output(nc, rwkvT, y, bonusT, gT, at["par"], at["ident"])
    finish(nc, at["yT"], at["xT"], attnT.rearrange("(k p) n -> k p n", p=P), rwkvT, at["w_rest"],
           at["ln_mix_pre"], at["ln_mix_post"], at["ln_ffn_pre"], at["ln_ffn_post"], at["ones"])


def layout(inputs):
    f = {n: np.asarray(v)[0] for n, v in inputs.items()}
    x = np.concatenate([f["x_prompt"], f["x_sample"]], 0)
    out = {"xT": np.ascontiguousarray(x.reshape(NTG, TG, KD, P).transpose(0, 3, 2, 1))}
    w_in, gate = f["w_in"][:, :NB_IN * P], f["w_in"][:, NB_IN * P:]
    out["w_in"] = blocks(w_in)
    for n in ("ln_mix_pre", "ln_mix_post", "ln_ffn_pre", "ln_ffn_post"):
        out[n] = columns(f[n])
    mu = np.concatenate([np.zeros(B_R * P, np.float32), f["shift_mu"]])
    out["mu"] = columns(mu)
    out["gains"] = columns(np.concatenate([f["q_gain"]] * HEADS + [f["k_gain"]] * 2))
    out["par"] = np.ascontiguousarray(np.stack(
        [columns(v) for n in PARAMS for v in np.reshape(f[n], (-1, WIDTH))], 1))
    for n in ("w_up", "a_up", "g_up"):
        out[n] = np.ascontiguousarray(f[n].reshape(P, PAIRS, P).transpose(1, 0, 2))
    branch = blocks(f["w_branch"].reshape(2 * WIDTH, D))
    last = blocks(f["w_ffn_out"])
    last = np.pad(last, ((0, 0), (0, 0), (0, 3 * D - D_FF))).reshape(KD, P, 3, D).transpose(0, 2, 1, 3)
    out["w_rest"] = np.ascontiguousarray(np.concatenate([
        np.stack([blocks(gate[:, :D]), blocks(gate[:, D:]), branch], 1).reshape(3 * KD, P, D),
        blocks(f["w_out"]),
        np.stack([blocks(f["w_ffn_in"][:, :D_FF]), blocks(f["w_ffn_in"][:, D_FF:])], 1).reshape(2 * KF, P, D),
        last.reshape(3 * KD, P, D)], 0))
    return {**out, **{n: v for n, v in shape_constants().items() if n in CONSTS}}


def kernel(**inputs):
    import concourse.bacc as bacc
    from concourse.bass_utils import run_bass_kernel_spmd

    nc = bacc.Bacc("TRN2", target_bir_lowering=False, num_devices=1)
    arrays = layout(inputs)
    at = {n: nc.dram_tensor(n, v.shape, F32, kind="ExternalInput").ap() for n, v in arrays.items()}
    at["yT"] = nc.dram_tensor("yT", (NTG, P, KD, TG), F32, kind="ExternalOutput").ap()
    build(nc, at)
    got = run_bass_kernel_spmd(nc, [arrays], core_ids=[0]).results[0]["yT"]
    y = got.transpose(0, 3, 2, 1).reshape(N, D)
    return y[None, :N_PROMPT], y[None, N_PROMPT:]
```

```python
from contextlib import ExitStack

import numpy as np

import concourse.bass as bass
from concourse import mybir

F32 = mybir.dt.float32
F32R = mybir.dt.float32r
ALU = mybir.AluOpType
ACT = mybir.ActivationFunctionType
AX = mybir.AxisListType

P = 128
D = 1024
KD = D // P
N_PROMPT, N_SAMPLE = 1024, 512
N = N_PROMPT + N_SAMPLE
TG = 512
NTG = N // TG
NCH = N // P
HD = 64
HEADS = 8
WIDTH = HEADS * HD
KW = WIDTH // P
D_FF = 2816
KF = D_FF // P
KFH = KF // 2
EPS = 1e-6
LNX_EPS = 64e-5
GRID_W = 64
ROPE_THETA = 10000.0
DECAY_SCALE = float(np.exp(-0.5))

B_Q, B_K, B_V, B_R, B_RK, B_RV, B_WD, B_AD, B_GD = 0, 4, 5, 6, 10, 14, 18, 19, 20
NB_IN = 21


class Arena:

    def __init__(self, nc, ctx, tag):
        self.nc, self.ctx, self.tag = nc, ctx, tag

    def sb(self, name, shape, dt=F32):
        return self.ctx.enter_context(self.nc.sbuf_tensor(f"{self.tag}_{name}", shape, dt))

    def ps(self, name, shape=(P, TG), dt=F32):
        return self.ctx.enter_context(self.nc.psum_tensor(f"{self.tag}_{name}", list(shape), dt))


def product(pe, out, w, x, kt, start=True, stop=True):
    for k in range(kt):
        for part, (a, b) in enumerate(((0, 0), (1, 0), (0, 1))):
            mm = pe.matmul(out, w[a](k), x[b](k), start=start and k == 0 and part == 0,
                           stop=stop and k == kt - 1 and part == 2)
    return mm


def hold(eng, holds):
    eng.sem_inc(holds, 1)


def project(nc, hT, uT, xT, w_in, ln_pre, mu, ones):
    ctx = ExitStack()
    with ctx:
        a = Arena(nc, ctx, "pr")
        sem = lambda name: ctx.enter_context(nc.semaphore("pr_" + name))
        h_hi, h_lo = hT
        NS = 1540
        x_s = a.sb("x", [P, KD, TG])
        h_s = a.sb("h", [P, KD, TG])
        std = a.sb("std", [P, TG])
        rstd = a.sb("rstd", [P, TG])
        ln_s = a.sb("ln", [P, KD])
        mu_s = a.sb("mu", [P, NB_IN])
        mu1 = a.sb("mu1", [P, NB_IN])
        muh = a.sb("muh", [P, NB_IN])
        ones_s = a.sb("ones", [P, P])
        eps_s = a.sb("eps", [P, 1])
        w_s = [a.sb(f"w{i}", [P, KD * P]) for i in range(2)]
        w_hi = [a.sb(f"whi{i}", [P, KD, P], F32R) for i in range(2)]
        w_lo = [a.sb(f"wlo{i}", [P, KD, P], F32R) for i in range(2)]
        u_s = [a.sb(f"u{i}", [P, NS]) for i in range(2)]
        z_s = [a.sb(f"z{i}", [P, NS - 2]) for i in range(2)]
        t_s = a.sb("t", [P, NS - 2])
        banks = [a.ps(f"b{i}") for i in range(8)]

        par_in, x_in = sem("par_in"), sem("x_in")
        squares, sums, stds, rstds, normed = sem("squares"), sem("sums"), sem("stds"), sem("rstds"), sem("normed")
        h_hi_ready, h_lo_ready = sem("h_hi_ready"), sem("h_lo_ready")
        mu_ready, pads_zero = sem("mu_ready"), sem("pads_zero")
        w_loaded = [sem(f"w_loaded{i}") for i in range(2)]
        w_hi_ready, w_lo_ready = sem("w_hi_ready"), sem("w_lo_ready")
        u_product, u_copied, mixed, z_ready = sem("u_product"), sem("u_copied"), sem("mixed"), sem("z_ready")
        z_stored = [sem(f"z_stored{i}") for i in range(2)]
        z_free = [sem(f"z_free{i}") for i in range(2)]
        BODY = 2
        ROUNDS = (NB_IN - 1) // BODY

        with nc.Block() as block:

            @block.sync
            def _(sp):
                sp.dma_start(ones_s[:, :], ones).then_inc(par_in, 16)
                sp.dma_start(ln_s[:, :], ln_pre).then_inc(par_in, 16)
                sp.dma_start(mu_s[:, :], mu).then_inc(par_in, 16)

                def load(j, slot):
                    sp.wait_ge(w_hi_ready, j + 1)
                    sp.wait_ge(w_lo_ready, j + 1)
                    sp.dma_start(w_s[slot][:, :], w_in[bass.ds(j, 1)].rearrange("a p n -> (a p) n"))\
                        .then_inc(w_loaded[slot], 16)

                for g in range(NTG):
                    if g:
                        sp.wait_ge(normed, KD * g)
                    sp.dma_start(x_s[:, :, :], xT[g]).then_inc(x_in, 16)
                    if g == 0:
                        load(0, 0)

                with sp.Fori(0, ROUNDS) as i:
                    load(i * BODY + 1, 1)
                    load(i * BODY + 2, 0)

            @block.gpsimd
            def _(pool):
                def store(j, slot, n):
                    pool.wait_ge(z_ready, j + 3)
                    dst = uT[bass.ds(j, 1)].rearrange("a p n -> (a p) n")
                    pool.dma_start(dst[:, 0:N_PROMPT], z_s[slot][:, 0:N_PROMPT]).then_inc(z_stored[slot], 16)
                    pool.dma_start(dst[:, N_PROMPT:N], z_s[slot][:, N_PROMPT + 2:N + 2])\
                        .then_inc(z_stored[slot], 16)
                    pool.wait_ge(z_stored[slot], n)
                    pool.sem_inc(z_free[slot], 1)

                for s in range(BODY):
                    pool.sem_inc(z_free[s], 1)
                with pool.Fori(0, ROUNDS) as i:
                    for s in range(BODY):
                        store(i * BODY + s, s, i * 32 + 32)
                store(NB_IN - 1, 0, 32 * ROUNDS + 32)

            @block.scalar
            def _(act):
                act.sem_inc(w_hi_ready, 2)
                act.sem_inc(u_copied, 2)
                act.wait_ge(pads_zero, 3)

                def split(slot, loads, j):
                    act.wait_ge(w_loaded[slot], loads)
                    act.wait_ge(u_product, j + 1)
                    act.activation(w_hi[slot][:, :, :], w_s[slot][:, :].rearrange("p (k n) -> p k n", k=KD),
                                   ACT.Copy).then_inc(w_hi_ready, 1)

                for g in range(NTG):
                    act.wait_ge(x_in, 16 * (g + 1))
                    for k in range(KD):
                        if g:
                            act.wait_ge(h_lo_ready, KD * (g - 1) + k + 1)
                        act.activation(h_s[:, k, :], x_s[:, k, :], ACT.Square).then_inc(squares, 1)
                    act.wait_ge(sums, g + 1)
                    act.activation(std[:, :], banks[6 + g % 2][:, :], ACT.Sqrt, scale=1.0 / D,
                                   bias=eps_s[:, :]).then_inc(stds, 1)
                    for k in range(KD):
                        act.wait_ge(normed, KD * g + k + 1)
                        act.activation(h_hi[:, k, g * TG:(g + 1) * TG], h_s[:, k, :], ACT.Copy).then_inc(h_hi_ready, 1)
                    if g == 0:
                        split(0, 16, 0)

                def evacuate(slot, j):
                    act.wait_ge(u_product, j + 3)
                    act.wait_ge(z_ready, j + 1)
                    for g in range(NTG):
                        c = 1 + g * TG + (2 if g == 2 else 0)
                        ins = act.activation(u_s[slot][:, c:c + TG], banks[slot * NTG + g][:, :], ACT.Copy)
                    ins.then_inc(u_copied, 1)

                with act.Fori(0, ROUNDS) as i:
                    split(1, i * 16 + 16, i * BODY + 1)
                    evacuate(0, i * BODY)
                    split(0, i * 16 + 32, i * BODY + 2)
                    evacuate(1, i * BODY + 1)
                evacuate(0, NB_IN - 1)

            @block.vector
            def _(dve):
                dve.sem_inc(w_lo_ready, 2)
                dve.sem_inc(z_ready, 2)
                dve.memset(eps_s[:, :], EPS).then_inc(pads_zero, 1)
                for s in range(2):
                    dve.memset(u_s[s][:, :], 0.0).then_inc(pads_zero, 1)

                def split(slot, j):
                    dve.wait_ge(w_hi_ready, j + 3)
                    dve.wait_ge(u_product, j + 1)
                    dve.tensor_tensor(w_lo[slot][:, :, :], w_s[slot][:, :].rearrange("p (k n) -> p k n", k=KD),
                                      w_hi[slot][:, :, :].bitcast(F32), ALU.subtract).then_inc(w_lo_ready, 1)

                dve.wait_ge(par_in, 48)
                dve.tensor_scalar(mu1[:, :], mu_s[:, :], -1.0, 1.0, ALU.mult, ALU.add)
                dve.tensor_scalar(muh[:, :], mu_s[:, :], 0.5, None, ALU.mult).then_inc(mu_ready, 1)
                for g in range(NTG):
                    dve.wait_ge(stds, g + 1)
                    dve.reciprocal(rstd[:, :], std[:, :]).then_inc(rstds, 1)
                    dve.wait_ge(rstds, g + 1)
                    for k in range(KD):
                        dve.scalar_tensor_tensor(out=h_s[:, k, :], in0=x_s[:, k, :], scalar=ln_s[:, k:k + 1],
                                                 in1=rstd[:, :], op0=ALU.mult, op1=ALU.mult).then_inc(normed, 1)
                    for k in range(KD):
                        dve.wait_ge(h_hi_ready, KD * g + k + 1)
                        t = slice(g * TG, (g + 1) * TG)
                        dve.tensor_tensor(h_lo[:, k, t], h_s[:, k, :], h_hi[:, k, t].bitcast(F32), ALU.subtract)\
                            .then_inc(h_lo_ready, 1)
                    if g == 0:
                        split(0, 0)

                def shift(slot, j, stored):
                    col = bass.ds(j, 1)
                    dve.wait_ge(u_copied, j + 3)
                    dve.wait_ge(z_free[slot], stored)
                    dve.wait_ge(z_ready, j + 2)
                    dve.tensor_tensor(t_s[:, :], u_s[slot][:, 0:NS - 2], u_s[slot][:, 2:NS], ALU.add)
                    dve.tensor_scalar(z_s[slot][:, :], u_s[slot][:, 1:NS - 1], mu1[:, col], None, ALU.mult)\
                        .then_inc(mixed, 1)
                    dve.wait_ge(mixed, j + 1)
                    dve.scalar_tensor_tensor(out=z_s[slot][:, :], in0=t_s[:, :], scalar=muh[:, col],
                                             in1=z_s[slot][:, :], op0=ALU.mult, op1=ALU.add).then_inc(z_ready, 1)

                dve.wait_ge(mu_ready, 1)
                with dve.Fori(0, ROUNDS) as i:
                    split(1, i * BODY + 1)
                    shift(0, i * BODY, i + 1)
                    split(0, i * BODY + 2)
                    shift(1, i * BODY + 1, i + 1)
                shift(0, NB_IN - 1, ROUNDS + 1)

            @block.tensor
            def _(pe):
                pe.sem_inc(u_product, 2)
                pe.wait_ge(par_in, 48)

                def sum_squares(g):
                    if g >= 2:
                        pe.wait_ge(stds, g - 1)
                    for k in range(KD):
                        pe.wait_ge(squares, KD * g + k + 1)
                        mm = pe.matmul(banks[6 + g % 2][:, :], ones_s[:, :], h_s[:, k, :],
                                       start=k == 0, stop=k == KD - 1)
                    mm.then_inc(sums, 1)

                def multiply(slot, j, copied, groups=range(NTG)):
                    pe.wait_ge(w_lo_ready, j + 3)
                    pe.wait_ge(w_hi_ready, j + 3)
                    pe.wait_ge(u_copied, copied)
                    for g in groups:
                        t = slice(g * TG, (g + 1) * TG)
                        mm = product(pe, banks[slot * NTG + g][:, :],
                                     (lambda k: w_hi[slot][:, k, :], lambda k: w_lo[slot][:, k, :]),
                                     (lambda k: h_hi[:, k, t], lambda k: h_lo[:, k, t]), KD)
                    return mm

                for g in range(NTG):
                    sum_squares(g)
                    if g:
                        pe.wait_ge(h_lo_ready, KD * g)
                        multiply(0, 0, 1, (g - 1,))
                pe.wait_ge(h_lo_ready, KD * NTG)
                multiply(0, 0, 1, (NTG - 1,)).then_inc(u_product, 1)
                with pe.Fori(0, ROUNDS) as i:
                    multiply(1, i * BODY + 1, i * BODY + 2).then_inc(u_product, 1)
                    multiply(0, i * BODY + 2, i * BODY + 3).then_inc(u_product, 1)


def rope(nc, qkT, uT, gains, cos, sin, headsum, swap):
    ctx = ExitStack()
    with ctx:
        a = Arena(nc, ctx, "ro")
        sem = lambda name: ctx.enter_context(nc.semaphore("ro_" + name))
        NB = B_V
        q_s = [a.sb(f"q{i}", [P, N]) for i in range(2)]
        sq_s = a.sb("sq", [P, N])
        std, n_s, o_s = ([a.sb(f"{m}{i}", [P, N]) for i in range(2)] for m in ("std", "n", "o"))
        c_s = a.sb("c", [P, N])
        cos_s, sin_s = a.sb("cos", [P, N]), a.sb("sin", [P, N])
        g_s = a.sb("g", [P, NB])
        sum_s, swap_s, eps_s = a.sb("sum", [P, P]), a.sb("swap", [P, P]), a.sb("eps", [P, 1])
        sum_ps, rot_ps = a.ps("sums", [P, N]), a.ps("rot", [P, N])
        tables_in = sem("tables_in")
        par_in, eps_set, q_in = sem("par_in"), sem("eps_set"), [sem("q_in0"), sem("q_in1")]
        squares, sums, stds, inverted, normed = sem("squares"), sem("sums"), sem("stds"), sem("inverted"), sem("normed")
        rotated, with_cos, with_sin, summed, stored = (
            sem("rotated"), sem("with_cos"), sem("with_sin"), sem("summed"), sem("stored"))

        with nc.Block() as block:

            @block.sync
            def _(sp):
                for tile, src in ((sum_s, headsum), (swap_s, swap), (g_s, gains)):
                    sp.dma_start(tile[:, :], src).then_inc(par_in, 16)
                for b in range(NB):
                    if b == 1:
                        for tile, src in ((cos_s, cos), (sin_s, sin)):
                            sp.dma_start(tile[:, :], src).then_inc(tables_in, 16)
                    if b >= 2:
                        sp.wait_ge(normed, b - 1)
                    sp.dma_start(q_s[b % 2][:, :], uT[b]).then_inc(q_in[b % 2], 16)

            @block.gpsimd
            def _(pool):
                pool.wait_ge(tables_in, 32)
                for b in range(NB):
                    pool.wait_ge(normed, b + 1)
                    if b:
                        pool.wait_ge(summed, b)
                    pool.tensor_tensor(c_s[:, :], n_s[b % 2][:, :], cos_s[:, :], ALU.mult).then_inc(with_cos, 1)
                    pool.wait_ge(with_sin, b + 1)
                    pool.wait_ge(with_cos, b + 1)
                    pool.tensor_tensor(o_s[b % 2][:, :], o_s[b % 2][:, :], c_s[:, :], ALU.add).then_inc(summed, 1)
                    pool.wait_ge(summed, b + 1)
                    if b:
                        pool.wait_ge(stored, 16 * b)
                    pool.dma_start(qkT[b * P:(b + 1) * P, :], o_s[b % 2][:, :]).then_inc(stored, 16)
                pool.wait_ge(stored, 16 * NB)

            @block.scalar
            def _(act):
                act.wait_ge(eps_set, 1)
                for b in range(NB):
                    act.wait_ge(q_in[b % 2], 16 * (b // 2 + 1))
                    if b:
                        act.wait_ge(sums, 3 * b)
                    act.activation(sq_s[:, :], q_s[b % 2][:, :], ACT.Square).then_inc(squares, 1)
                    if b >= 2:
                        act.wait_ge(normed, b - 1)
                    for g in range(NTG):
                        act.wait_ge(sums, 3 * b + g + 1)
                        t = slice(g * TG, (g + 1) * TG)
                        act.activation(std[b % 2][:, t], sum_ps[:, t], ACT.Sqrt, scale=1.0 / HD, bias=eps_s[:, :])\
                            .then_inc(stds, 1)

            @block.vector
            def _(dve):
                dve.memset(eps_s[:, :], EPS).then_inc(eps_set, 1)
                dve.wait_ge(par_in, 48)

                def norm(b):
                    dve.wait_ge(stds, 3 * b + 3)
                    dve.reciprocal(std[b % 2][:, :], std[b % 2][:, :]).then_inc(inverted, 1)
                    dve.wait_ge(inverted, b + 1)
                    if b >= 2:
                        dve.wait_ge(rotated, 3 * (b - 1))
                        dve.wait_ge(with_cos, b - 1)
                    dve.scalar_tensor_tensor(out=n_s[b % 2][:, :], in0=q_s[b % 2][:, :], scalar=g_s[:, b:b + 1],
                                             in1=std[b % 2][:, :], op0=ALU.mult, op1=ALU.mult).then_inc(normed, 1)

                def sine(b):
                    if b == 0:
                        dve.wait_ge(tables_in, 32)
                    if b >= 2:
                        dve.wait_ge(stored, 16 * (b - 1))
                    for g in range(NTG):
                        t = slice(g * TG, (g + 1) * TG)
                        dve.wait_ge(rotated, 3 * b + g + 1)
                        ins = dve.tensor_tensor(o_s[b % 2][:, t], rot_ps[:, t], sin_s[:, t], ALU.mult)
                    ins.then_inc(with_sin, 1)

                norm(0)
                for b in range(NB):
                    if b + 1 < NB:
                        norm(b + 1)
                    sine(b)

            @block.tensor
            def _(pe):
                pe.wait_ge(par_in, 48)

                def sum_squares(b):
                    pe.wait_ge(squares, b + 1)
                    if b:
                        pe.wait_ge(stds, 3 * b)
                    for g in range(NTG):
                        t = slice(g * TG, (g + 1) * TG)
                        pe.matmul(sum_ps[:, t], sum_s[:, :], sq_s[:, t], start=True, stop=True).then_inc(sums, 1)

                sum_squares(0)
                for b in range(NB):
                    if b + 1 < NB:
                        sum_squares(b + 1)
                    pe.wait_ge(normed, b + 1)
                    if b:
                        pe.wait_ge(with_sin, b)
                    for g in range(NTG):
                        t = slice(g * TG, (g + 1) * TG)
                        pe.matmul(rot_ps[:, t], swap_s[:, :], n_s[b % 2][:, t], start=True, stop=True)\
                            .then_inc(rotated, 1)


def attention(nc, attnT, qkT, uT, ident, t0, n, tag):
    ctx = ExitStack()
    with ctx:
        a = Arena(nc, ctx, tag)
        sems = []

        def sem(name):
            sems.append(nc.alloc_semaphore(name=f"{tag}_{name}"))
            return sems[-1]

        NT, NG = n // P, n // TG
        NU = NT * NG
        SCALE = HD ** -0.5
        q_s = [a.sb(f"q{i}", [HD, n]) for i in range(2)]
        k_s = [a.sb(f"k{i}", [HD, n]) for i in range(2)]
        q_hi, q_lo, k_hi, k_lo = ([a.sb(f"{m}{i}", [P, n], F32R) for i in range(2)]
                                  for m in ("q_hi", "q_lo", "k_hi", "k_lo"))
        zero_s, one_s = a.sb("zero", [P, n]), a.sb("one", [P, n])
        v_s = a.sb("v", [P, n])
        va = a.sb("va", [P, NT, 2, P])
        e_s = a.sb("e", [P, NT, n])
        vh = [a.sb(f"vh{i}", [P, NT, P]) for i in range(2)]
        o_s = [a.sb(f"o{i}", [HD, n]) for i in range(2)]
        mx = [a.sb(f"mx{i}", [P, NT]) for i in range(2)]
        mrow = [a.sb(f"mrow{i}", [NT, P], F32R) for i in range(2)]
        rec = a.sb("rec", [HD, TG])
        id_s = a.sb("id", [P, P])
        first = [a.ps(f"first{i}", [P, NG * TG]) for i in range(2)]
        second = [a.ps(f"second{i}") for i in range(2)]
        third = [a.ps(f"third{i}") for i in range(2)]

        par_in, v_in, ones_set = sem("par_in"), sem("v_in"), sem("ones_set")
        v_turned, va_ready = sem("v_turned"), sem("va_ready")
        q_in, k_in = [sem("q_in0"), sem("q_in1")], [sem("k_in0"), sem("k_in1")]
        row_zero, row_in = sem("row_zero"), [sem("row_in0"), sem("row_in1")]
        scored, max_ready, max_turned, mrow_ready = sem("scored"), sem("max_ready"), sem("max_turned"), sem("mrow_ready")
        hi_ready, lo_ready = sem("hi_ready"), sem("lo_ready")
        shifted, exp_ready, summed, norm_step = sem("shifted"), sem("exp_ready"), sem("summed"), sem("norm_step")
        vh_ready, o_stored, o_free = sem("vh_ready"), [sem("o_stored0"), sem("o_stored1")], sem("o_free")

        def heads(first_stage, second_stage):
            def both(eng):
                first_stage(0, 0, 0)
                with eng.Fori(0, HEADS // 2 - 1) as i:
                    first_stage(i * 2 + 1, 1, i)
                    second_stage(i * 2, 0, i)
                    first_stage(i * 2 + 2, 0, i + 1)
                    second_stage(i * 2 + 1, 1, i)
                last = HEADS // 2 - 1
                first_stage(HEADS - 1, 1, last)
                second_stage(HEADS - 2, 0, last)
                second_stage(HEADS - 1, 1, last)
            return both

        with nc.Block() as block:

            @block.sync
            def _(sp):
                sp.dma_start(id_s[:, :], ident).then_inc(par_in, 16)
                sp.dma_start(v_s[:, :], uT[B_V][:, t0:t0 + n]).then_inc(v_in, 16)

                def load(h, s, i):
                    sp.wait_ge(shifted, h * NU + NU)
                    sp.dma_start(q_s[s][0:HD, :], qkT[bass.ds(h * HD, HD), t0:t0 + n]).then_inc(q_in[s], 16)
                    kv = h // 4
                    sp.dma_start(k_s[s][0:HD, :], qkT[bass.ds(kv * HD + WIDTH, HD), t0:t0 + n])\
                        .then_inc(k_in[s], 16)

                def load_row(h, s, i):
                    sp.wait_ge(mrow_ready, h + 2)
                    sp.dma_start(q_hi[s][HD:HD + 1, :].bitcast(F32).rearrange("a (t p) -> a t p", p=P),
                                 mrow[s][:, :].bitcast(F32))\
                        .then_inc(row_in[s], 16)

                load(0, 0, 0)
                load_row(0, 0, 0)
                with sp.Fori(0, HEADS // 2 - 1) as i:
                    load(i * 2 + 1, 1, i)
                    load_row(i * 2 + 1, 1, i)
                    load(i * 2 + 2, 0, i)
                    load_row(i * 2 + 2, 0, i)
                load(HEADS - 1, 1, 0)
                load_row(HEADS - 1, 1, 0)

            @block.gpsimd
            def _(pool):
                def values(h, s, i):
                    kv = h // 4
                    pool.wait_ge(summed, h * NG + NG)
                    pool.tensor_copy(vh[s][:, :, :], va[:, :, bass.ds(kv, 1), :].rearrange("p t a c -> p t (a c)"))\
                        .then_inc(vh_ready, 1)

                def store(h, s, i):
                    pool.wait_ge(norm_step, h * 2 * NG + 2 * NG + 2)
                    pool.dma_start(attnT[bass.ds(h * HD, HD), t0:t0 + n], o_s[s][:, :]).then_inc(o_stored[s], 16)
                    pool.wait_ge(o_stored[s], i * 16 + 16)
                    pool.sem_inc(o_free, 1)

                pool.sem_inc(o_free, 2)
                pool.wait_ge(va_ready, NT)
                heads(values, store)(pool)

            @block.scalar
            def _(act):
                def exponents(h, s, i):
                    for u in range(NU):
                        kt, g = u // NG, u % NG
                        act.wait_ge(shifted, h * NU + 2 * NU + u + 1)
                        act.activation(e_s[:, kt, g * TG:(g + 1) * TG], second[u % 2][:, :], ACT.Exp, scale=SCALE)\
                            .then_inc(exp_ready, 1)

                def high_parts(h, s, i):
                    for x_in, x, hi in ((q_in, q_s, q_hi), (k_in, k_s, k_hi)):
                        act.wait_ge(x_in[s], i * 16 + 16)
                        act.activation(hi[s][0:HD, :], x[s][:, :], ACT.Copy).then_inc(hi_ready, 1)

                act.sem_inc(exp_ready, 2)
                heads(high_parts, exponents)(act)

            @block.vector
            def _(dve):
                dve.sem_inc(mrow_ready, 1)
                dve.sem_inc(max_ready, 2)
                dve.sem_inc(norm_step, 2)
                dve.memset(zero_s[:, :], 0.0).then_inc(ones_set, 1)
                dve.memset(one_s[:, :], 1.0).then_inc(ones_set, 1)
                dve.memset(va[:, :, :, :], 1.0).then_inc(ones_set, 1)
                dve.wait_ge(ones_set, 3)
                for s in range(2):
                    for tile in (q_hi, q_lo, k_hi, k_lo):
                        dve.tensor_copy(tile[s][HD:P, :], zero_s[HD:P, :]).then_inc(ones_set, 1)
                dve.wait_ge(ones_set, 11)
                for s in range(2):
                    dve.tensor_copy(k_hi[s][HD:HD + 1, :], one_s[HD:HD + 1, :]).then_inc(ones_set, 1)
                for t in range(NT):
                    dve.wait_ge(v_turned, t + 1)
                    dve.tensor_copy(va[:, t, :, 0:HD],
                                    third[t % 2][:, 0:P].rearrange("p (a b) -> p a b", a=2)).then_inc(va_ready, 1)

                def maxima(h, s, i):
                    dve.wait_ge(shifted, h * NU + NU)
                    dve.tensor_copy(q_hi[s][HD:HD + 1, :], zero_s[HD:HD + 1, :]).then_inc(row_zero, 1)
                    for m, (x, hi, lo) in enumerate(((q_s, q_hi, q_lo), (k_s, k_hi, k_lo))):
                        dve.wait_ge(hi_ready, h * 2 + m + 1)
                        dve.tensor_tensor(lo[s][0:HD, :], x[s][:, :], hi[s][0:HD, :].bitcast(F32), ALU.subtract)\
                            .then_inc(lo_ready, 1)
                    for t in range(NT):
                        dve.wait_ge(scored, h * NT + t + 1)
                        dve.tensor_reduce(mx[s][:, t:t + 1], first[t % 2][:, :], AX.X, ALU.max).then_inc(max_ready, 1)
                    dve.wait_ge(max_turned, h + 1)
                    dve.tensor_scalar(mrow[s][:, :], first[0][0:NT, 0:P], -1.0, None, ALU.mult)\
                        .then_inc(mrow_ready, 1)

                def normalise(h, s, i):
                    dve.wait_ge(o_free, h + 1)
                    for g in range(NG):
                        n0 = h * 2 * NG + 2 * g + 2
                        dve.wait_ge(summed, h * NG + 2 * NG + g + 1)
                        dve.wait_ge(norm_step, n0)
                        dve.reciprocal(rec[:, :], third[g % 2][HD:P, :]).then_inc(norm_step, 1)
                        dve.wait_ge(norm_step, n0 + 1)
                        dve.tensor_tensor(o_s[s][:, g * TG:(g + 1) * TG], third[g % 2][0:HD, :], rec[:, :],
                                          ALU.mult).then_inc(norm_step, 1)

                dve.wait_ge(ones_set, 13)
                heads(maxima, normalise)(dve)

            @block.tensor
            def _(pe):
                pe.sem_inc(shifted, 2 * NU)
                pe.sem_inc(summed, 2 * NG)
                pe.wait_ge(par_in, 16)
                pe.wait_ge(v_in, 16)
                for t in range(NT):
                    if t >= 2:
                        pe.wait_ge(va_ready, t - 1)
                    pe.transpose(third[t % 2][:, 0:P], v_s[:, t * P:(t + 1) * P], id_s[:, :]).then_inc(v_turned, 1)
                pe.wait_ge(va_ready, NT)

                def scores(h, s, t):
                    if t == 0:
                        pe.wait_ge(hi_ready, h * 2 + 2)
                        pe.wait_ge(row_zero, h + 1)
                        pe.wait_ge(mrow_ready, h + 1)
                    pe.wait_ge(max_ready, h * NT + t + 1)
                    for g in range(NG):
                        mm = pe.matmul(first[t % 2][:, g * TG:(g + 1) * TG], q_hi[s][:, t * P:(t + 1) * P],
                                       k_hi[s][:, g * TG:(g + 1) * TG], start=True, stop=True)
                    mm.then_inc(scored, 1)

                def turn_maxima(h, s):
                    pe.wait_ge(max_ready, h * NT + NT + 2)
                    pe.transpose(first[0][0:NT, 0:P], mx[s][:, :], id_s[:, :]).then_inc(max_turned, 1)

                def shifted_scores(h, s, i, more):
                    pe.wait_ge(row_in[s], i * 16 + 16)
                    pe.wait_ge(lo_ready, h * 2 + 2)
                    for u in range(NU):
                        kt, g = u // NG, u % NG
                        pe.wait_ge(exp_ready, h * NU + u + 1)
                        keys, queries = slice(kt * P, (kt + 1) * P), slice(g * TG, (g + 1) * TG)
                        product(pe, second[u % 2][:, :], (lambda _: k_hi[s][:, keys], lambda _: k_lo[s][:, keys]),
                                (lambda _: q_hi[s][:, queries], lambda _: q_lo[s][:, queries]), 1).then_inc(shifted, 1)
                        if more and u % NG == NG - 1:
                            scores(h + 1, 1 - s, kt)

                def with_values(h, s, i, more):
                    pe.wait_ge(vh_ready, h + 1)
                    for g in range(NG):
                        pe.wait_ge(norm_step, h * 2 * NG + 2)
                        for kt in range(NT):
                            if g == 0:
                                pe.wait_ge(exp_ready, h * NU + (kt + 1) * NG + 2)
                            mm = pe.matmul(third[g % 2][:, :], vh[s][:, kt, :], e_s[:, kt, g * TG:(g + 1) * TG],
                                           start=kt == 0, stop=kt == NT - 1)
                            if more and g == 0 and kt == NT // 2 - 1:
                                turn_maxima(h + 1, 1 - s)
                        mm.then_inc(summed, 1)

                def first_stage(h, s, i):
                    if isinstance(h, int) and h == 0:
                        for t in range(NT):
                            scores(h, s, t)
                        turn_maxima(h, s)

                def second_stage(h, s, i):
                    more = not (isinstance(h, int) and h == HEADS - 1)
                    shifted_scores(h, s, i, more)
                    with_values(h, s, i, more)

                heads(first_stage, second_stage)(pe)
        nc.clear_and_free_semaphores(sems)
        nc.all_engine_barrier()

LEVELS = 6
PAIRS = KW


class Steps:
    CREDIT = 3

    def __init__(self, sem, names):
        self.sem, self.names, self.n = sem, names, len(names)
        self.at = {name: i + 1 for i, name in enumerate(names)}
        self.next = 0

    def start(self, eng):
        eng.sem_inc(self.sem, self.CREDIT * self.n)

    def value(self, rnd, name):
        return rnd * self.n + (self.CREDIT * self.n + self.at[name])

    def last(self, rnd, name):
        return rnd * self.n + ((self.CREDIT - 1) * self.n + self.at[name])

    def whole(self, rounds, back=0):
        return rounds * self.n + (self.CREDIT - back) * self.n

    def done(self, ins, name):
        assert self.names[self.next % self.n] == name, (name, self.names[self.next % self.n])
        self.next += 1
        ins.then_inc(self.sem, 1)


def recurrence(nc, y_out, bonusT, gT, uT, w_up, a_up, g_up, par, consts):
    ctx = ExitStack()
    with ctx:
        a = Arena(nc, ctx, "rw")
        sem = lambda name: ctx.enter_context(nc.semaphore("rw_" + name))
        C = DECAY_SCALE
        NPAR = 9
        K_K, K_A, R_K, W0, A0 = 0, 1, 2, 3, 5
        SLOTS = 3
        NS_CH = N_SAMPLE // P
        G_SAMPLE = N_PROMPT // TG
        wd_s, ad_s, gd_s = (a.sb(n, [P, N]) for n in ("wd", "ad", "gd"))
        par_s = a.sb("par", [P, NPAR, PAIRS])
        rkh_s, ka1_s = a.sb("rkh", [P, PAIRS]), a.sb("ka1", [P, PAIRS])
        hs_s, id_s = a.sb("hs", [P, P]), a.sb("id", [P, P])
        restart_s = a.sb("restart", [P, TG])
        causal_s, pair_s = a.sb("causal", [P, 2, 2, P]), a.sb("pair", [P, 2, P])
        level_s = a.sb("level", [P, 2, LEVELS, P])
        wup_s, aup_s, gup_s = a.sb("wup", [P, 2, P]), a.sb("aup", [P, 2, P]), a.sb("gup", [P, P])
        r_s, k_s, v_s = (a.sb(n, [P, TG]) for n in ("r", "k", "v"))
        bo_s, gt_s = (a.sb(n, [P, TG]) for n in ("bo", "gt"))
        x_s = [a.sb(f"x{d}", [P, 4, N]) for d in range(2)]
        mid_s, end_s, scale_s = (a.sb(n, [P, 2, NCH]) for n in ("mid", "end", "scale"))
        vt_s, vp_s = a.sb("vt", [P, NCH, P]), a.sb("vp", [P, NCH, 2, P])
        y_s = a.sb("y", [P, NCH, WIDTH])
        kk_s, t_s, kb_s, sq_s = (a.sb(n, [P, TG]) for n in ("kk", "t", "kb", "sq"))
        sig_s, al_s, cum_s = ([a.sb(f"{n}{d}", [P, TG]) for d in range(2)] for n in ("sig", "al", "cum"))
        e_s = [a.sb(f"e{i}", [P, TG]) for i in range(3)]
        pad_s = [a.sb(f"pad{d}", [P, 4, P]) for d in range(2)]
        ab_s, ak_s = ([[a.sb(f"{n}{s}{d}", [P, 4 * P]) for d in range(2)] for s in range(SLOTS)] for n in ("ab", "ak"))
        bk_s = [a.sb(f"bk{s}", [P, 2, 2, P]) for s in range(2)]
        Z = [[a.sb(f"Z{s}{d}", [P, 2 * P]) for d in range(2)] for s in range(2)]
        X = [a.sb(f"X{s}", [P, 2, 2 * P]) for s in range(2)]
        T = [a.sb(f"T{d}", [P, 2 * P]) for d in range(2)]
        p_s = [a.sb(f"p{d}", [P, P]) for d in range(2)]
        up_s = [a.sb(f"up{d}", [P, 2, P]) for d in range(2)]
        uf_s = [a.sb(f"uf{d}", [P, P]) for d in range(2)]
        S = [a.sb(f"S{d}", [P, P]) for d in range(2)]
        banks = [a.ps(f"b{i}") for i in range(8)]
        FR, INV, SN, PR = banks[0:2], banks[2:4], banks[4:6], banks[6:8]

        tables_in = sem("tables_in")
        const_in, lora_in, w_in = sem("const_in"), sem("lora_in"), sem("w_in")
        r_in, k_in, v_in = sem("r_in"), sem("k_in"), sem("v_in")
        bonus_stored, g_stored, y_stored = sem("bonus_stored"), sem("g_stored"), sem("y_stored")
        zeroed, lora_ready, par_ready = sem("zeroed"), sem("lora_ready"), sem("par_ready")
        exps_done, scales_done, holds = sem("exps_done"), sem("scales_done"), [sem("hold0"), sem("hold1")]

        D2 = range(2)
        dve_prep = Steps(sem("dve_prep"), [
            "kkraw", "cum0", "mid0", "end0", "cum1", "mid1", "end1", "clamp", *(f"invert{c}" for c in range(4)), "kk",
            "kfac0", "kfac1", "centre0", "before0", "centre1", "before1", "kb", "rb",
            *(f"{n}{d}" for d in D2 for n in ("xr", "xa", "xb", "xk")), "bonus", "vp0", "vp1"])
        act_prep = Steps(sem("act_prep"), [
            "sig0", "sig1", "al0", "al1", "square", "norm", "g", "vt",
            *(f"{n}{d}" for d in D2 for n in ("er", "ea", "eb"))])
        pool_prep = Steps(sem("pool_prep"), ["kdir0", "kdir1", "kka0", "kka1"])
        pe_prep = Steps(sem("pe_prep"), ["xw0", "xw1", "xa0", "xa1", "sumsq", "xg", "turnv", "sumrb"])
        pool_front = Steps(sem("pool_front"), ["pad0", "pad1", "Zp0", "Zp1", "Z0", "Z1"])
        pe_front = Steps(sem("pe_front"), ["ab0", "ak0", "ab1", "ak1", "X", "bk"])
        dve_front = Steps(sem("dve_front"), ["ab0", "ak0", "ab1", "ak1"])
        act_front = Steps(sem("act_front"), ["X", "bk"])
        END = LEVELS - 1
        pe_level = Steps(sem("pe_level"), [
            *(f"{m}{n}_{d}" for n in range(END) for m in ("T", "X", "Z") for d in D2),
            *(f"{m}{END}_{d}" for m in ("T", "Z") for d in D2)])
        dve_level = Steps(sem("dve_level"), [
            *(f"{m}{n}_{d}" for n in range(END) for m in ("T", "X") for d in D2),
            *(f"{m}{END}_{d}" for m in ("T", "Z") for d in D2)])
        act_level = Steps(sem("act_level"), [f"Z{n}_{d}" for n in range(END) for d in D2])
        pe_scan = Steps(sem("pe_scan"), [f"{m}_{d}" for m in ("p", "u", "ys") for d in D2])
        dve_scan = Steps(sem("dve_scan"), [f"{m}_{d}" for m in ("up", "y") for d in D2])
        act_scan = Steps(sem("act_scan"), [*(f"{m}_{d}" for m in ("p", "uf") for d in D2),
                                           *(f"S{h}_{d}" for d in D2 for h in range(2))])

        def cols(r, d):
            c = NCH - 1 - r if d else (r + NCH - NS_CH if r < NS_CH else r - NS_CH)
            return c, slice(c * P, (c + 1) * P)

        PIECES = 27
        NEXT = 6 * LEVELS * 3

        def pair(p, last, prep, scales, front, level, scan):
            def between(place):
                if place < 2 * PIECES:
                    prep(p, place // PIECES, place % PIECES, p * 3 + (place // PIECES + 1))
                elif place == 2 * PIECES:
                    scales(p, 0, N_PROMPT // P, p * 2 + 1)
                elif not last and NEXT <= place < NEXT + 2 * PIECES and place % 2 == 0:
                    prep(p + 1, G_SAMPLE, (place - NEXT) // 2, p * 3 + 3)
                elif not last and place == NEXT + 2 * PIECES:
                    scales(p + 1, N_PROMPT // P, NCH, p * 2 + 2)

            for r in range(NCH):
                for n in range(LEVELS):
                    place = 3 * (r * LEVELS + n)
                    level(p, r, n, "T")
                    if r:
                        scan(p, r - 1, 2 * n)
                    between(place)
                    level(p, r, n, "X" if n < END else "end")
                    if r:
                        scan(p, r - 1, 2 * n + 1)
                    between(place + 1)
                    if n < END:
                        level(p, r, n, "Z")
                    if r < NCH - 1:
                        front(p, r + 1, n)
                    between(place + 2)
            for n in range(LEVELS):
                scan(p, NCH - 1, 2 * n)
                scan(p, NCH - 1, 2 * n + 1)
                if not last:
                    front(p + 1, 0, n)

        def pairs(eng, *stages):
            prep, scales, front = stages[:3]
            for piece in range(PIECES):
                prep(0, G_SAMPLE, piece, 0)
            scales(0, N_PROMPT // P, NCH, 0)
            for n in range(LEVELS):
                front(0, 0, n)
            with eng.Fori(0, PAIRS - 1) as p:
                pair(p, False, *stages)
            pair(PAIRS - 1, True, *stages)

        def nothing(*_):
            pass

        def heads(ap):
            return ap.rearrange("p (h n) -> p h n", n=P)

        def both(mask):
            return mask.unsqueeze(1).broadcast_to([P, 2, P])

        def round_of(p, r):
            return p * NCH + r

        with nc.Block() as block:

            @block.sync
            def _(sp):
                for tile, src in ((hs_s, consts["headsum"]), (id_s, consts["ident"]), (par_s, par),
                                  (restart_s, consts["restart"])):
                    sp.dma_start(tile[:], src).then_inc(const_in, 16)
                for tile, b in ((wd_s, B_WD), (ad_s, B_AD), (gd_s, B_GD)):
                    sp.dma_start(tile[:, :], uT[b]).then_inc(lora_in, 16)
                sp.sem_inc(bonus_stored, 16)
                sp.sem_inc(g_stored, 16)
                sp.wait_ge(zeroed, 1)
                with sp.Fori(0, PAIRS) as p:
                    sp.wait_ge(pe_prep.sem, pe_prep.whole(p * NTG))
                    for src, tile in ((w_up, wup_s), (a_up, aup_s)):
                        for d in D2:
                            h = slice(d * HD, (d + 1) * HD)
                            sp.dma_start(tile[h, d, :], src[bass.ds(p, 1), h, :].rearrange("a p n -> (a p) n"))\
                                .then_inc(w_in, 16)
                    sp.dma_start(gup_s[:, :], g_up[bass.ds(p, 1)].rearrange("a p n -> (a p) n")).then_inc(w_in, 16)
                    for i, g in enumerate((G_SAMPLE, 0, 1)):
                        it, t = p * NTG + i, slice(g * TG, (g + 1) * TG)
                        sp.wait_ge(dve_prep.sem, dve_prep.whole(it))
                        sp.wait_ge(pe_prep.sem, pe_prep.whole(it))
                        sp.wait_ge(pool_prep.sem, pool_prep.whole(it))
                        hold(sp, holds[1])
                        for tile, b, s in ((k_s, B_RK, k_in), (v_s, B_RV, v_in), (r_s, B_R, r_in)):
                            sp.dma_start(tile[:, :], uT[bass.ds(p + b, 1), :, t].rearrange("a p n -> (a p) n"))\
                                .then_inc(s, 16)
                        dst = lambda z: z[bass.ds(p, 1), :, t].rearrange("a p n -> (a p) n")
                        sp.wait_ge(act_prep.sem, act_prep.value(it, "g"))
                        hold(sp, holds[1])
                        sp.dma_start(dst(gT), gt_s[:, :]).then_inc(g_stored, 16)
                        sp.wait_ge(dve_prep.sem, dve_prep.value(it, "bonus"))
                        sp.dma_start(dst(bonusT), bo_s[:, :]).then_inc(bonus_stored, 16)
                first = (PAIRS - 1) * P
                for pairs_done, part in ((PAIRS - 1, slice(0, first)), (PAIRS, slice(first, WIDTH))):
                    sp.wait_ge(dve_scan.sem, dve_scan.whole(pairs_done * NCH))
                    sp.dma_start(y_out[:, :, part], y_s[:, :, part]).then_inc(y_stored, 16)
                sp.wait_ge(y_stored, 32)
                sp.wait_ge(bonus_stored, 16 * (PAIRS * NTG + 1))
                sp.wait_ge(g_stored, 16 * (PAIRS * NTG + 1))

            @block.gpsimd
            def _(pool):
                pool_prep.start(pool)
                pool_front.start(pool)
                pool.wait_ge(const_in, 64)
                pool.wait_ge(tables_in, 64)
                pool.wait_ge(zeroed, 1)

                def prep(p, g, piece, it):
                    if piece == 13:
                        for d in D2:
                            kd = (kb_s, t_s)[d]
                            if d:
                                pool.wait_ge(pool_prep.sem, pool_prep.value(it, "kdir0"))
                            pool.wait_ge(dve_prep.sem, dve_prep.value(it, f"kfac{d}"))
                            pool_prep.done(pool.tensor_tensor(kd[:, :], kd[:, :], k_s[:, :], ALU.mult), f"kdir{d}")
                        for d in D2:
                            pool.wait_ge(pool_prep.sem, pool_prep.value(it, ("kdir1", "kka0")[d]))
                            pool_prep.done(pool.tensor_tensor(al_s[d][:, :], al_s[d][:, :], kk_s[:, :], ALU.mult),
                                           f"kka{d}")

                def front(p, r, n):
                    it, s = round_of(p, r), r % SLOTS
                    if n == 0:
                        if r in (0, NS_CH):
                            pool.wait_ge(dve_prep.sem, dve_prep.whole(p * 3 + (1 if r == 0 else 3)))
                        pool.wait_ge(pe_front.sem, pe_front.last(it, "ak1"))
                        four = lambda ap: ap.broadcast_to([P, 2, 2, P])
                        for d in D2:
                            pool.wait_ge(pool_front.sem, pool_front.last(it, "Z1") if d == 0 else
                                         pool_front.value(it, "pad0"))
                            pool_front.done(pool.tensor_tensor(
                                pad_s[d][:, :, :].rearrange("p (a h) n -> p a h n", a=2),
                                four(x_s[d][:, 0:2, cols(r, d)[1]].unsqueeze(2)),
                                four(hs_s[:, 0:P:HD].unsqueeze(1).unsqueeze(3)), ALU.mult), f"pad{d}")
                    if n == 3:
                        pool.wait_ge(pe_scan.sem, pe_scan.value(it - 2, "u_1"))
                        for d in D2:
                            pool.wait_ge(pool_front.sem, pool_front.value(it, ("pad1", "Zp0")[d]))
                            pool.wait_ge(dve_front.sem, dve_front.value(it, f"ab{d}"))
                            pool_front.done(pool.tensor_tensor(heads(Z[r % 2][d][:, :]), heads(ab_s[s][d][:, 0:2 * P]),
                                                               both(pair_s[:, d, :]), ALU.mult), f"Zp{d}")
                        for d in D2:
                            pool.wait_ge(pool_front.sem, pool_front.value(it, ("Zp1", "Z0")[d]))
                            z = heads(Z[r % 2][d][:, :])
                            pool_front.done(pool.tensor_tensor(z, z, both(id_s[:, :]), ALU.add), f"Z{d}")

                pairs(pool, prep, nothing, front, nothing, nothing)

            @block.scalar
            def _(act):
                for steps in (act_prep, act_front, act_level, act_scan):
                    steps.start(act)
                act.wait_ge(lora_in, 48)
                act.activation(wd_s[:, :], wd_s[:, :], ACT.Tanh).then_inc(lora_ready, 1)
                act.activation(gd_s[:, :], gd_s[:, :], ACT.Sigmoid).then_inc(lora_ready, 1)
                act.dma_start(causal_s[:, :, :, :], consts["causal"].rearrange("d a p n -> p d a n"))\
                    .then_inc(tables_in, 16)
                act.dma_start(pair_s[:, :, :], consts["pair"].rearrange("d p n -> p d n")).then_inc(tables_in, 16)
                for d in D2:
                    act.dma_start(level_s[:, d, :, :], consts["levels"][d].rearrange("l p n -> p l n"))\
                        .then_inc(tables_in, 16)
                act.wait_ge(const_in, 64)
                act.wait_ge(zeroed, 1)
                par = lambda n, p: par_s[:, n, bass.ds(p, 1)]

                def prep(p, g, piece, it):
                    done = act_prep.done

                    def pe_did(name):
                        act.wait_ge(pe_prep.sem, pe_prep.value(it, name))

                    if piece == 0:
                        act.wait_ge(dve_prep.sem, dve_prep.whole(it))
                        act.wait_ge(pool_prep.sem, pool_prep.whole(it))
                        for d in D2:
                            pe_did(f"xw{d}")
                            hold(act, holds[0])
                            done(act.activation(sig_s[d][:, :], PR[d][:, :], ACT.Sigmoid, bias=par(W0 + d, p)), f"sig{d}")
                    if piece == 3:
                        for d in D2:
                            pe_did(f"xa{d}")
                            hold(act, holds[0])
                            done(act.activation(al_s[d][:, :], PR[d][:, :], ACT.Sigmoid, bias=par(A0 + d, p)), f"al{d}")
                    if piece == 4:
                        act.wait_ge(dve_prep.sem, dve_prep.value(it, "kkraw"))
                        act.wait_ge(pe_prep.sem, pe_prep.whole(it))
                        done(act.activation(sq_s[:, :], kk_s[:, :], ACT.Square), "square")
                    if piece == 6:
                        pe_did("sumsq")
                        done(act.activation(t_s[:, :], PR[0][:, :], ACT.Sqrt), "norm")
                    if piece == 7:
                        act.wait_ge(g_stored, it * 16 + 16)
                        pe_did("xg")
                        done(act.activation(gt_s[:, :], PR[1][:, :], ACT.Copy), "g")
                    if piece == 10:
                        if g != G_SAMPLE:
                            act.wait_ge(pe_scan.sem, pe_scan.whole(p * NCH))
                        elif not (isinstance(p, int) and p == 0):
                            act.wait_ge(pe_scan.sem, pe_scan.whole(p * NCH, NCH - NS_CH))
                        pe_did("turnv")
                        done(act.activation(vt_s[:, 4 * g:4 * g + 4, :].rearrange("p a b -> p (a b)"), PR[1][:, :],
                                            ACT.Copy), "vt")
                    (l0, b0), (l1, b1) = ((cum_s[d], sig_s[d]) for d in D2)
                    parts = {16: (0, 0, l0, -C), 17: (0, 1, b0, -C), 18: (0, 2, l0, C),
                             21: (1, 0, b1, C), 22: (1, 1, l1, C), 24: (1, 2, b1, -C)}
                    if piece in parts:
                        d, n, src, scale = parts[piece]
                        act.wait_ge(dve_prep.sem, dve_prep.value(it, ("xr0", "xa0", "xk0")[n] if d else "before0"))
                        done(act.activation(e_s[n][:, :], src[:, :], ACT.Exp, scale=scale),
                             ("er", "ea", "eb")[n] + str(d))

                def scales(p, c0, c1, n):
                    act.wait_ge(dve_prep.sem, dve_prep.whole(p * 3 + (1 if c0 else 3)))
                    for tile in (mid_s, end_s):
                        act.activation(tile[:, :, c0:c1], tile[:, :, c0:c1], ACT.Exp, scale=-C).then_inc(exps_done, 1)

                def front(p, r, n):
                    it, s = round_of(p, r), r % SLOTS
                    if n == 4:
                        act.wait_ge(dve_level.sem, dve_level.whole(it, 1))
                        act.wait_ge(pe_front.sem, pe_front.value(it, "X"))
                        act_front.done(act.activation(X[r % 2][:, :, :].rearrange("p a n -> p (a n)"), FR[0][:, :],
                                                      ACT.Copy), "X")
                    if n == 5:
                        act.wait_ge(pe_scan.sem, pe_scan.value(it - 2, "ys_1"))
                        act.wait_ge(pe_front.sem, pe_front.value(it, "bk"))
                        act_front.done(act.activation(bk_s[r % 2][:, :, :, :].rearrange("p a b n -> p (a b n)"),
                                                      FR[1][:, :], ACT.Copy), "bk")

                def level(p, r, n, part):
                    it, s = round_of(p, r), r % SLOTS
                    if part == "Z":
                        for d in D2:
                            act.wait_ge(pe_level.sem, pe_level.value(it, f"Z{n}_{d}"))
                            act_level.done(act.activation(Z[r % 2][d][:, :], INV[d][:, 0:2 * P], ACT.Copy), f"Z{n}_{d}")

                def scan(p, r, n):
                    it = round_of(p, r)
                    for d in D2:
                        if n == d:
                            act.wait_ge(pe_scan.sem, pe_scan.value(it, f"p_{d}"))
                            act_scan.done(act.activation(p_s[d][:, :], SN[d][:, 0:P], ACT.Copy), f"p_{d}")
                        if n == 2 + d:
                            act.wait_ge(dve_scan.sem, dve_scan.value(it, f"up_{d}"))
                            act_scan.done(act.activation(uf_s[d][:, :].rearrange("p (h n) -> p h n", h=2),
                                                         bass_diag(SN[d][:, P:3 * P]), ACT.Copy), f"uf_{d}")
                        if n == 6 + 3 * d:
                            if d == 0 and r in (0, NS_CH):
                                act.wait_ge(scales_done, p * 2 + (3 if r == 0 else 4))
                            c = cols(r, d)[0]
                            act.wait_ge(pe_scan.sem, pe_scan.value(it, f"ys_{d}"))
                            for h in range(2):
                                q = slice(h * HD, (h + 1) * HD)
                                act_scan.done(act.activation(S[d][q, q], SN[d][q, q], ACT.Copy,
                                                             scale=scale_s[q, d, c:c + 1]), f"S{h}_{d}")

                pairs(act, prep, scales, front, level, scan)

            @block.vector
            def _(dve):
                for steps in (dve_prep, dve_front, dve_level, dve_scan):
                    steps.start(dve)
                dve.sem_inc(scales_done, 2)
                for tile in (wup_s, aup_s, vp_s, y_s, scale_s, *up_s, *S):
                    ins = dve.memset(tile[:], 0.0)
                ins.then_inc(zeroed, 1)
                dve.wait_ge(zeroed, 1)
                dve.wait_ge(const_in, 64)
                dve.tensor_scalar(rkh_s[:, :], par_s[:, R_K, :], 0.5, None, ALU.mult)
                dve.tensor_scalar(ka1_s[:, :], par_s[:, K_A, :], -1.0, 1.0, ALU.mult, ALU.add).then_inc(par_ready, 1)
                dve.wait_ge(par_ready, 1)
                par = lambda n, p: par_s[:, n, bass.ds(p, 1)]
                chunks = lambda tile: tile[:, :].rearrange("p (c n) -> p c n", n=P)

                def prep(p, g, piece, it):
                    def own(name):
                        dve.wait_ge(dve_prep.sem, dve_prep.value(it, name))

                    def act_did(name):
                        dve.wait_ge(act_prep.sem, act_prep.value(it, name))

                    done = dve_prep.done
                    t, c4 = slice(g * TG, (g + 1) * TG), slice(4 * g, 4 * g + 4)

                    def ends(d):
                        own(f"cum{d}")
                        done(dve.tensor_copy(mid_s[:, d, c4], chunks(cum_s[d])[:, :, P // 2 - 1]), f"mid{d}")
                        done(dve.tensor_tensor(end_s[:, d, c4], chunks(cum_s[d])[:, :, P - 1],
                                               chunks(cum_s[d])[:, :, P // 2 - 1], ALU.subtract), f"end{d}")

                    for d in D2:
                        if piece == 4 + 2 * d:
                            act_did(f"sig{d}")
                            done(dve.tensor_tensor_scan(cum_s[d][:, :], restart_s[:, :], sig_s[d][:, :], 0.0,
                                                        ALU.mult, ALU.add), f"cum{d}")
                        if piece == 5 + 2 * d:
                            ends(d)
                        if piece == 14 + 2 * d:
                            own(f"end{d}")
                            done(dve.tensor_tensor(chunks(cum_s[d]), chunks(cum_s[d]),
                                                   mid_s[:, d, c4].unsqueeze(2).broadcast_to([P, 4, P]),
                                                   ALU.subtract), f"centre{d}")
                        if piece == 15 + 2 * d:
                            own(f"centre{d}")
                            done(dve.tensor_tensor(sig_s[d][:, :], cum_s[d][:, :], sig_s[d][:, :], ALU.subtract),
                                 f"before{d}")
                    if piece == 3:
                        dve.wait_ge(scales_done, p * 2 + (1 if g == G_SAMPLE else 2))
                        dve.wait_ge(k_in, it * 16 + 16)
                        dve.wait_ge(dve_prep.sem, dve_prep.whole(it))
                        dve.wait_ge(pool_prep.sem, pool_prep.whole(it))
                        done(dve.tensor_scalar(kk_s[:, :], k_s[:, :], par(K_K, p), None, ALU.mult), "kkraw")
                    if piece == 8:
                        act_did("norm")
                        done(dve.tensor_scalar(t_s[:, :], t_s[:, :], 1e-12, None, ALU.max), "clamp")
                        own("clamp")
                    if 8 <= piece < 12:
                        c = piece - 8
                        part = slice(c * P, (c + 1) * P)
                        done(dve.reciprocal(t_s[:, part], t_s[:, part]), f"invert{c}")
                    if piece == 12:
                        own("invert3")
                        done(dve.tensor_tensor(kk_s[:, :], kk_s[:, :], t_s[:, :], ALU.mult), "kk")
                    if piece == 13:
                        own("kk")
                        for d in D2:
                            act_did(f"al{d}")
                            done(dve.tensor_scalar((kb_s, t_s)[d][:, :], al_s[d][:, :], par(K_A, p),
                                                   ka1_s[:, bass.ds(p, 1)], ALU.mult, ALU.add), f"kfac{d}")
                    if piece == 18:
                        act_did("square")
                        dve.wait_ge(pe_prep.sem, pe_prep.value(it, "sumsq"))
                        dve.wait_ge(pool_prep.sem, pool_prep.value(it, "kdir1"))
                        done(dve.tensor_tensor(sq_s[:, :], kb_s[:, :], t_s[:, :], ALU.add), "kb")
                    if piece == 19:
                        own("kb")
                        dve.wait_ge(r_in, it * 16 + 16)
                        done(dve.scalar_tensor_tensor(out=sq_s[:, :], in0=r_s[:, :], scalar=rkh_s[:, bass.ds(p, 1)],
                                                      in1=sq_s[:, :], op0=ALU.mult, op1=ALU.mult), "rb")
                    for d in D2:
                        if piece == (20, 24)[d]:
                            act_did(f"er{d}")
                            done(dve.tensor_tensor(x_s[d][:, 1, t], r_s[:, :], e_s[0][:, :], ALU.mult), f"xr{d}")
                        if piece == (21, 24)[d]:
                            act_did(f"ea{d}")
                            done(dve.scalar_tensor_tensor(out=x_s[d][:, 0, t], in0=kk_s[:, :], scalar=-1.0,
                                                          in1=e_s[1][:, :], op0=ALU.mult, op1=ALU.mult), f"xa{d}")
                        if piece == (22, 25)[d]:
                            act_did(f"eb{d}")
                            dve.wait_ge(pool_prep.sem, pool_prep.value(it, "kka1"))
                            done(dve.tensor_tensor(x_s[d][:, 2, t], al_s[d][:, :], e_s[2][:, :], ALU.mult), f"xb{d}")
                        if piece == (23, 25)[d]:
                            done(dve.tensor_tensor(x_s[d][:, 3, t], (kb_s, t_s)[d][:, :], e_s[2][:, :], ALU.mult),
                                 f"xk{d}")
                    if piece == 26:
                        dve.wait_ge(pe_prep.sem, pe_prep.value(it, "sumrb"))
                        dve.wait_ge(v_in, it * 16 + 16)
                        dve.wait_ge(bonus_stored, it * 16 + 16)
                        done(dve.tensor_tensor(bo_s[:, :], PR[0][:, :], v_s[:, :], ALU.mult), "bonus")
                        act_did("vt")
                        for h in range(2):
                            q = slice(h * HD, (h + 1) * HD)
                            done(dve.tensor_copy(vp_s[:, c4, h, q], vt_s[:, c4, q]), f"vp{h}")

                def scales(p, c0, c1, n):
                    dve.wait_ge(exps_done, 2 * n + 2)
                    dve.tensor_tensor(scale_s[:, 0, c0:c1 - 1], end_s[:, 0, c0:c1 - 1], mid_s[:, 0, c0 + 1:c1], ALU.mult)
                    dve.tensor_tensor(scale_s[:, 1, c0 + 1:c1], mid_s[:, 1, c0 + 1:c1], end_s[:, 1, c0:c1 - 1],
                                      ALU.mult).then_inc(scales_done, 1)

                def front(p, r, n):
                    it, s = round_of(p, r), r % SLOTS
                    if n == 0:
                        if isinstance(p, int) and p == 0 and r == 0:
                            dve.wait_ge(tables_in, 64)
                        dve.wait_ge(pe_scan.sem, pe_scan.whole(it, 2))
                    if n < 4:
                        d, m = n // 2, n % 2
                        tile, name = ((ab_s, "ab"), (ak_s, "ak"))[m]
                        dve.wait_ge(pe_front.sem, pe_front.value(it, f"{name}{d}"))
                        four = lambda ap: ap.rearrange("p (a h n) -> p a h n", a=2, h=2)
                        mask = causal_s[:, d, :, :].unsqueeze(2).broadcast_to([P, 2, 2, P])
                        dve_front.done(dve.tensor_tensor(four(tile[s][d][:, :]), four(FR[m][:, :]), mask, ALU.mult),
                                       f"{name}{d}")

                def level(p, r, n, part):
                    it, s = round_of(p, r), r % SLOTS
                    for d in D2:
                        if part == "T":
                            dve.wait_ge(pe_level.sem, pe_level.value(it, f"T{n}_{d}"))
                            dve_level.done(dve.tensor_tensor(heads(T[d][:, :]), heads(INV[d][:, 0:2 * P]),
                                                             both(level_s[:, d, n, :]), ALU.mult), f"T{n}_{d}")
                        if part == "X":
                            dve.wait_ge(pe_level.sem, pe_level.value(it, f"X{n}_{d}"))
                            x = X[r % 2][:, d, :]
                            dve_level.done(dve.tensor_tensor(x, INV[d][:, 2 * P:4 * P], x, ALU.add), f"X{n}_{d}")
                        if part == "end":
                            dve.wait_ge(pe_level.sem, pe_level.value(it, f"Z{n}_{d}"))
                            dve_level.done(dve.tensor_tensor(Z[r % 2][d][:, :], INV[d][:, 2 * P:4 * P], Z[r % 2][d][:, :],
                                                             ALU.add), f"Z{n}_{d}")

                def scan(p, r, n):
                    it = round_of(p, r)
                    for d in D2:
                        if n == 2 + d:
                            dve.wait_ge(pe_scan.sem, pe_scan.value(it, f"u_{d}"))
                            dve_scan.done(dve.tensor_copy(bass_diag(up_s[d][:, :, :].rearrange("p h n -> p (h n)")),
                                                          bass_diag(SN[d][:, P:3 * P])), f"up_{d}")
                        if n == 7 + 3 * d:
                            dve.wait_ge(act_scan.sem, act_scan.value(it, f"S1_{d}"))
                            c = cols(r, d)[0]
                            y = y_s[:, c, bass.ds(p * P, P)]
                            dve_scan.done(dve.tensor_tensor(y, SN[d][:, 3 * P:4 * P], y, ALU.add), f"y_{d}")

                pairs(dve, prep, scales, front, level, scan)

            @block.tensor
            def _(pe):
                for steps in (pe_prep, pe_front, pe_level, pe_scan):
                    steps.start(pe)
                pe.wait_ge(const_in, 64)
                pe.wait_ge(lora_ready, 2)
                head = lambda h: slice(h * P, (h + 1) * P)

                def prep(p, g, piece, it):
                    done = pe_prep.done
                    t = slice(g * TG, (g + 1) * TG)

                    def act_did(name):
                        pe.wait_ge(act_prep.sem, act_prep.value(it, name))

                    if piece == 0:
                        pe.wait_ge(w_in, p * 80 + 80)
                        pe.wait_ge(act_prep.sem, act_prep.whole(it))
                        pe.wait_ge(dve_prep.sem, dve_prep.whole(it))
                        for d in D2:
                            done(pe.matmul(PR[d][:, :], wup_s[:, d, :], wd_s[:, t], start=True, stop=True), f"xw{d}")
                    if piece == 2:
                        for d in D2:
                            act_did(f"sig{d}")
                            done(pe.matmul(PR[d][:, :], aup_s[:, d, :], ad_s[:, t], start=True, stop=True), f"xa{d}")
                    if piece == 5:
                        act_did("square")
                        done(pe.matmul(PR[0][:, :], hs_s[:, :], sq_s[:, :], start=True, stop=True), "sumsq")
                        done(pe.matmul(PR[1][:, :], gup_s[:, :], gd_s[:, t], start=True, stop=True), "xg")
                    if piece == 9:
                        pe.wait_ge(v_in, it * 16 + 16)
                        act_did("g")
                        for c in range(4):
                            mm = pe.transpose(PR[1][:, c * P:(c + 1) * P], v_s[:, c * P:(c + 1) * P], id_s[:, :])
                        done(mm, "turnv")
                    if piece == 20:
                        pe.wait_ge(dve_prep.sem, dve_prep.value(it, "rb"))
                        done(pe.matmul(PR[0][:, :], hs_s[:, :], sq_s[:, :], start=True, stop=True), "sumrb")

                def front(p, r, n):
                    it, s = round_of(p, r), r % SLOTS
                    done = pe_front.done
                    if n == 0 and r in (0, NS_CH):
                        pe.wait_ge(dve_prep.sem, dve_prep.whole(p * 3 + (1 if r == 0 else 3)))
                        pe.wait_ge(act_prep.sem, act_prep.whole(p * 3 + (1 if r == 0 else 3)))
                    if n < 4:
                        d, m = n // 2, n % 2
                        name = ("ab", "ak")[m]
                        pe.wait_ge(pool_front.sem, pool_front.value(it, f"pad{d}"))
                        if d:
                            pe.wait_ge(dve_front.sem, dve_front.value(it, f"{name}0"))
                        else:
                            pe.wait_ge(act_front.sem, act_front.last(it, ("X", "bk")[m]))
                        done(pe.matmul(FR[m][:, :], x_s[d][:, 2 + m, cols(r, d)[1]],
                                       pad_s[d][:, :, :].rearrange("p a n -> p (a n)"), start=True, stop=True),
                             f"{name}{d}")
                    if n == 4:
                        pe.wait_ge(dve_front.sem, dve_front.value(it, "ab1"))
                        pe.wait_ge(pool_front.sem, pool_front.value(it, "Z1"))
                        for d in D2:
                            for h in range(2):
                                mm = pe.transpose(FR[0][:, head(2 * d + h)], Z[r % 2][d][:, head(h)], id_s[:, :])
                        done(mm, "X")
                    if n == 5:
                        pe.wait_ge(dve_front.sem, dve_front.value(it, "ak1"))
                        for d in D2:
                            for m in range(2):
                                mm = pe.transpose(FR[1][:, head(2 * d + m)], x_s[d][:, 2 + m, cols(r, d)[1]], id_s[:, :])
                        done(mm, "bk")

                def level(p, r, n, part):
                    it, s = round_of(p, r), r % SLOTS
                    done = pe_level.done
                    for d in D2:
                        x = lambda h: X[r % 2][:, d, head(h)]
                        if part == "T":
                            if n:
                                pe.wait_ge(act_level.sem, act_level.value(it, f"Z{n - 1}_{d}"))
                            elif d == 0:
                                pe.wait_ge(act_front.sem, act_front.value(it, "X"))
                                pe.wait_ge(dve_level.sem, dve_level.last(it, f"Z{END}_1"))
                            for h in range(2):
                                mm = pe.matmul(INV[d][:, head(h)], ab_s[s][d][:, head(h)], x(h), start=True, stop=True)
                            done(mm, f"T{n}_{d}")
                        if part == "X":
                            pe.wait_ge(dve_level.sem, dve_level.value(it, f"T{n}_{d}"))
                            for h in range(2):
                                mm = pe.matmul(INV[d][:, head(2 + h)], Z[r % 2][d][:, head(h)], T[d][:, head(h)],
                                               start=True, stop=True)
                            done(mm, f"X{n}_{d}")
                        if part == "Z":
                            pe.wait_ge(dve_level.sem, dve_level.value(it, f"X{n}_{d}"))
                            for h in range(2):
                                mm = pe.transpose(INV[d][:, head(h)], x(h), id_s[:, :])
                            done(mm, f"Z{n}_{d}")
                        if part == "end":
                            pe.wait_ge(dve_level.sem, dve_level.value(it, f"T{n}_{d}"))
                            for h in range(2):
                                mm = pe.matmul(INV[d][:, head(2 + h)], T[d][:, head(h)], Z[r % 2][d][:, head(h)],
                                               start=True, stop=True)
                            done(mm, f"Z{n}_{d}")

                def scan(p, r, n):
                    it, s = round_of(p, r), r % SLOTS
                    done = pe_scan.done
                    vp = lambda h: vp_s[:, cols(r, d)[0], h, :]
                    act_did = lambda name: pe.wait_ge(act_scan.sem, act_scan.value(it, name))
                    for d in D2:
                        c, t = cols(r, d)
                        if n == d:
                            pe.wait_ge(dve_scan.sem, dve_scan.last(it, f"y_{d}"))
                            pe.wait_ge(act_scan.sem, act_scan.last(it, f"S1_{d}"))
                            pe.matmul(SN[d][:, 0:P], x_s[d][:, 0, t], S[d][:, :], start=True, stop=False)
                            for h in range(2):
                                mm = pe.matmul(SN[d][:, 0:P], ak_s[s][d][:, head(h)], vp(h), start=False, stop=h == 1)
                            done(mm, f"p_{d}")
                        if n == 2 + d:
                            if d == 0:
                                pe.wait_ge(dve_level.sem, dve_level.value(it, f"Z{END}_1"))
                            act_did(f"p_{d}")
                            for h in range(2):
                                mm = pe.matmul(SN[d][:, head(1 + h)], Z[r % 2][d][:, head(h)], p_s[d][:, :],
                                               start=True, stop=True)
                            done(mm, f"u_{d}")
                        Y = SN[d][:, 3 * P:4 * P]
                        if n == 4 + 3 * d:
                            act_did(f"uf_{d}")
                            pe.matmul(Y, x_s[d][:, 1, t], S[d][:, :], start=True, stop=False)
                            for h in range(2):
                                pe.matmul(Y, ak_s[s][d][:, head(2 + h)], vp(h), start=False, stop=False)
                        if n == 5 + 3 * d:
                            for h in range(2):
                                pe.matmul(Y, ab_s[s][d][:, head(2 + h)], up_s[d][:, h, :], start=False, stop=h == 1)
                        if n == 6 + 3 * d:
                            if d == 0:
                                pe.wait_ge(act_front.sem, act_front.value(it, "bk"))
                            pe.matmul(SN[d][:, 0:P], id_s[:, :], S[d][:, :], start=True, stop=False)
                            pe.matmul(SN[d][:, 0:P], bk_s[r % 2][:, d, 0, :], uf_s[d][:, :], start=False, stop=False)
                            mm = pe.matmul(SN[d][:, 0:P], bk_s[r % 2][:, d, 1, :], vt_s[:, c, :], start=False, stop=True)
                            done(mm, f"ys_{d}")

                pairs(pe, prep, nothing, front, level, scan)


def bass_diag(ap):
    return ap.rearrange("p (x n) -> p x n", n=HD)[:, 0:4:3, :]


def branch_output(nc, rwkvT, y_in, bonusT, gT, par, ident):
    ctx = ExitStack()
    with ctx:
        a = Arena(nc, ctx, "bo")
        sem = lambda name: ctx.enter_context(nc.semaphore("bo_" + name))
        LN_W, LN_B = 7, 8
        CG, H4 = TG // P, TG // P * HEADS
        y_s = [a.sb(f"y{i}", [P, CG, WIDTH]) for i in range(2)]
        sq_s = a.sb("sq", [P, CG * WIDTH])
        mean, var = a.sb("mean", [P, H4]), a.sb("var", [P, H4])
        bo_s = [a.sb(f"bo{i}", [P, KW, TG]) for i in range(2)]
        g_s = [a.sb(f"g{i}", [P, KW, TG]) for i in range(2)]
        par_s, id_s, eps_s = a.sb("par", [P, 9, PAIRS]), a.sb("id", [P, P]), a.sb("eps", [P, 1])
        banks = [a.ps(f"b{i}") for i in range(8)]
        par_in, eps_set = sem("par_in"), sem("eps_set")
        y_in_sb, bo_in, g_in = ([sem(f"{n}{i}") for i in range(2)] for n in ("y_in", "bo_in", "g_in"))
        stat, squares, stds, turned, mixed, stored = (
            sem("stat"), sem("squares"), sem("stds"), sem("turned"), sem("mixed"), sem("stored"))
        STAT = 6

        with nc.Block() as block:

            @block.sync
            def _(sp):
                sp.dma_start(par_s[:, :, :], par).then_inc(par_in, 16)
                sp.dma_start(id_s[:, :], ident).then_inc(par_in, 16)
                for g in range(NTG):
                    t = slice(g * TG, (g + 1) * TG)
                    if g >= 2:
                        sp.wait_ge(stored, 16 * (g - 1))
                        sp.wait_ge(turned, KW * (g - 1))
                    sp.dma_start(y_s[g % 2][:, :, :], y_in[:, g * CG:(g + 1) * CG, :]).then_inc(y_in_sb[g % 2], 16)
                    for tile, src, s in ((bo_s, bonusT, bo_in), (g_s, gT, g_in)):
                        sp.dma_start(tile[g % 2][:, :, :], src[:, :, t].rearrange("k p n -> p k n"))\
                            .then_inc(s[g % 2], 16)

            @block.gpsimd
            def _(pool):
                for g in range(NTG):
                    pool.wait_ge(mixed, 2 * KW * (g + 1))
                    pool.dma_start(rwkvT[:, :, g * TG:(g + 1) * TG].rearrange("k p n -> p k n"), bo_s[g % 2][:, :, :])\
                        .then_inc(stored, 16)
                    pool.wait_ge(stored, 16 * (g + 1))

            @block.scalar
            def _(act):
                act.wait_ge(eps_set, 1)
                for g in range(NTG):
                    act.wait_ge(stat, STAT * g + 3)
                    act.activation(sq_s[:, :], y_s[g % 2][:, :, :].rearrange("p c n -> p (c n)"), ACT.Square)\
                        .then_inc(squares, 1)
                    act.wait_ge(stat, STAT * g + 4)
                    act.activation(var[:, :], var[:, :], ACT.Sqrt, scale=1.0 / HD, bias=eps_s[:, :]).then_inc(stds, 1)

            @block.vector
            def _(dve):
                dve.memset(eps_s[:, :], LNX_EPS).then_inc(eps_set, 1)
                dve.wait_ge(par_in, 32)
                for g in range(NTG):
                    y = y_s[g % 2][:, :, :].rearrange("p c (h n) -> p (c h) n", n=HD)
                    over = lambda s: s[:, :].unsqueeze(2).broadcast_to([P, H4, HD])
                    dve.wait_ge(y_in_sb[g % 2], 16 * (g // 2 + 1))
                    dve.tensor_reduce(mean[:, :], y, AX.X, ALU.add).then_inc(stat, 1)
                    dve.wait_ge(stat, STAT * g + 1)
                    dve.tensor_scalar(mean[:, :], mean[:, :], 1.0 / HD, None, ALU.mult).then_inc(stat, 1)
                    dve.wait_ge(stat, STAT * g + 2)
                    dve.tensor_tensor(y, y, over(mean), ALU.subtract).then_inc(stat, 1)
                    dve.wait_ge(squares, g + 1)
                    dve.tensor_reduce(var[:, :], sq_s[:, :].rearrange("p (h n) -> p h n", n=HD), AX.X, ALU.add)\
                        .then_inc(stat, 1)
                    dve.wait_ge(stds, g + 1)
                    dve.reciprocal(var[:, :], var[:, :]).then_inc(stat, 1)
                    dve.wait_ge(stat, STAT * g + 5)
                    dve.tensor_tensor(y, y, over(var), ALU.mult).then_inc(stat, 1)
                    dve.wait_ge(bo_in[g % 2], 16 * (g // 2 + 1))
                    dve.wait_ge(g_in[g % 2], 16 * (g // 2 + 1))
                    for b in range(KW):
                        dve.wait_ge(turned, KW * g + b + 1)
                        o = bo_s[g % 2][:, b, :]
                        dve.scalar_tensor_tensor(out=o, in0=banks[(g * KW + b) % 8][:, :], scalar=par_s[:, LN_W, b:b + 1],
                                                 in1=o, op0=ALU.mult, op1=ALU.add).then_inc(mixed, 1)
                        dve.wait_ge(mixed, 2 * (KW * g + b) + 1)
                        dve.scalar_tensor_tensor(out=o, in0=o, scalar=par_s[:, LN_B, b:b + 1], in1=g_s[g % 2][:, b, :],
                                                 op0=ALU.add, op1=ALU.mult).then_inc(mixed, 1)

            @block.tensor
            def _(pe):
                pe.wait_ge(par_in, 32)
                for g in range(NTG):
                    pe.wait_ge(stat, STAT * (g + 1))
                    if g >= 2:
                        pe.wait_ge(mixed, 2 * KW * (g - 1))
                    for b in range(KW):
                        for c in range(CG):
                            mm = pe.transpose(banks[(g * KW + b) % 8][:, c * P:(c + 1) * P],
                                              y_s[g % 2][:, c, b * P:(b + 1) * P], id_s[:, :])
                        mm.then_inc(turned, 1)


def finish(nc, yT, xT, attnT, rwkvT, weights, ln_pre, ln_post, ln_ffn_pre, ln_ffn_post, ones):
    ctx = ExitStack()
    with ctx:
        a = Arena(nc, ctx, "fi")
        sem = lambda name: ctx.enter_context(nc.semaphore("fi_" + name))
        RING = 4
        AHEAD = 2
        FFN_KT = (8, 8, KF - 16)
        J_OUT, J_FFN, J_LAST = 3 * KD, 4 * KD, 4 * KD + 2 * KF
        JOBS = J_LAST + 3 * KD
        assert JOBS % RING == 0
        x_s = a.sb("x", [P, KD, TG])
        m_s = a.sb("m", [P, KD, TG])
        ln_s = [a.sb(f"ln{i}", [P, KD]) for i in range(4)]
        ones_s = a.sb("ones", [P, P])
        eps_s = a.sb("eps", [P, 1])
        h_hi = a.sb("h_hi", [P, KD, TG], F32R)
        with ExitStack() as early:
            xn_s = Arena(nc, early, "fi").sb("next", [P, KD, TG])
        h_lo = a.sb("h_lo", [P, KD, TG], F32R)
        w_s = [a.sb(f"w{i}", [P, KD * P]) for i in range(RING)]
        w_hi = [a.sb(f"whi{i}", [P, KD, P], F32R) for i in range(RING)]
        w_lo = [a.sb(f"wlo{i}", [P, KD, P], F32R) for i in range(RING)]
        s_s = [a.sb(f"s{i}", [P, TG]) for i in range(2)]
        p_s = a.sb("p", [P, TG])
        std, rstd = s_s[0], p_s
        with ExitStack() as first:
            b = Arena(nc, first, "fi")
            br_s = b.sb("br", [P, 2 * KW, TG])
            br_hi = b.sb("br_hi", [P, 2 * KW, TG], F32R)
            br_lo = b.sb("br_lo", [P, 2 * KW, TG], F32R)
            g_hi = b.sb("g_hi", [P, KD, TG], F32R)
            g_lo = b.sb("g_lo", [P, KD, TG], F32R)
            q_s = b.sb("q", [P, TG])
        f_hi = a.sb("f_hi", [P, KF, TG], F32R)
        f_lo = a.sb("f_lo", [P, KF, TG], F32R)
        banks = [a.ps(f"b{i}") for i in range(8)]
        SUM, NEXT_SUM = banks[7], banks[6]
        next_sq = [m_s[:, KD - 2, :], m_s[:, KD - 1, :]]
        next_rstd, next_std = next_sq
        ADDS = KD - 2
        NEXT_SQUARES = {2: (0, 1, 2), 3: (3, 4, 5), 4: (6, 7)}

        par_in, eps_set, x_in, br_in = sem("par_in"), sem("eps_set"), sem("x_in"), [sem("br_in0"), sem("br_in1")]
        squares, sums, stds, rstds = sem("squares"), sem("sums"), sem("stds"), sem("rstds")
        normed, h_hi_ready, h_lo_ready = sem("normed"), sem("h_hi_ready"), sem("h_lo_ready")
        br_hi_ready, br_lo_ready = sem("br_hi_ready"), sem("br_lo_ready")
        w_loaded = [sem(f"w_loaded{i}") for i in range(RING)]
        w_hi_ready, w_lo_ready, product_done = sem("w_hi_ready"), sem("w_lo_ready"), sem("product_done")
        gate_ready, gated, merge_step = sem("gate_ready"), sem("gated"), sem("merge_step")
        out_copied, scaled, x2_ready = sem("out_copied"), sem("scaled"), sem("x2_ready")
        added, next_added = sem("added"), sem("next_added")
        silu_ready, ffn_step = sem("silu_ready"), sem("ffn_step")
        xn_in, next_squares, next_sums = sem("xn_in"), sem("next_squares"), sem("next_sums")
        next_stds, next_rstds = sem("next_stds"), sem("next_rstds")
        ffn_copied, y_stored = sem("ffn_copied"), sem("y_stored")
        holds = [sem("hold0"), sem("hold1")]

        def jobs(eng, t, job, after):
            j0 = t * JOBS
            with eng.Fori(0, KD // 4) as i:
                for s in range(12):
                    row = i * 12 + s
                    j, k = j0 + row, i * 4 + s // 3
                    job(j, s, KD, "merge", k, row)
                    after("gate" if s % 3 < 2 else "merge", k, s, j)
            for k in range(KD):
                job(j0 + J_OUT + k, k, KD, "out", k, J_OUT + k)
                after("out", k, k, j0 + J_OUT + k)
            after("mixed", 0, 0, 0)
            with eng.Fori(0, KF // 2) as i:
                for s in range(4):
                    row = i * 4 + J_FFN + s
                    j, k = j0 + row, i * 2 + s // 2
                    job(j, s, KD, "ffn_in", k, row)
                    after("silu" if s % 2 == 0 else "ffn_in", k, s, j)
            for s in range(3 * KD):
                job(j0 + J_LAST + s, s, FFN_KT[s % 3], "ffn_out", s // 3, J_LAST + s)
                if s % 3 == 2:
                    after("ffn_out", s // 3, s, j0 + J_LAST + s)
            after("done", 0, 0, 0)

        def nothing(*_):
            pass

        def groups(eng, group):
            group(0)
            with eng.Fori(1, NTG - 1) as t:
                group(t)
            group(NTG - 1)

        def is_first(t):
            return isinstance(t, int) and t == 0

        def is_last(t):
            return isinstance(t, int) and t == NTG - 1

        with nc.Block() as block:

            @block.sync
            def _(sp):
                sp.dma_start(xn_s[:, :, :], xT[0]).then_inc(xn_in, 16)
                sp.dma_start(ones_s[:, :], ones).then_inc(par_in, 16)
                for tile, src in zip(ln_s, (ln_pre, ln_post, ln_ffn_pre, ln_ffn_post)):
                    sp.dma_start(tile[:, :], src).then_inc(par_in, 16)

                def load(j, s, row, kt):
                    sp.wait_ge(w_lo_ready, j + 1)
                    sp.dma_start(w_s[s % RING][:, 0:kt * P],
                                 weights[bass.ds(row, 1)].rearrange("a p n -> (a p) n")[:, 0:kt * P])\
                        .then_inc(w_loaded[s % RING], 16)

                tokens = lambda z, t: z[bass.ds(t, 1)].rearrange("a p k n -> (a p) k n")

                def store(t):
                    sp.wait_ge(x2_ready, t * 16 + 16)
                    hold(sp, holds[0])
                    sp.dma_start(tokens(yT, t), x_s[:, :, :]).then_inc(y_stored, 16)
                    sp.wait_ge(y_stored, t * 16 + 16)
                    hold(sp, holds[0])

                def after(kind, k, t):
                    if kind == "out" and k == 0:
                        if not is_first(t):
                            store(t - 1)
                        sp.dma_start(x_s[:, :, :], tokens(xT, t)).then_inc(x_in, 16)
                    if kind == "ffn_out" and k == 1 and not is_last(t):
                        sp.wait_ge(product_done, t * JOBS + J_LAST + RING)
                        hold(sp, holds[0])
                        sp.dma_start(xn_s[:, :, :], tokens(xT, t + 1)).then_inc(xn_in, 16)

                groups(sp, lambda t: jobs(sp, t, lambda j, s, kt, kind, k, row: load(j, s, row, kt),
                                          lambda kind, k, s, j: after(kind, k, t)))
                for s in range(AHEAD):
                    load(NTG * JOBS + s, s, s, KD)
                store(NTG - 1)

            @block.gpsimd
            def _(pool):
                pool.sem_inc(w_lo_ready, RING)

                def split(j, s, kt, kind, k, row):
                    pool.wait_ge(w_hi_ready, j + 1)
                    pool.tensor_tensor(w_lo[s % RING][:, 0:kt, :],
                                       w_s[s % RING][:, 0:kt * P].rearrange("p (k n) -> p k n", k=kt),
                                       w_hi[s % RING][:, 0:kt, :].bitcast(F32), ALU.subtract)\
                        .then_inc(w_lo_ready, 1)

                groups(pool, lambda t: jobs(pool, t, split, nothing))

            @block.scalar
            def _(act):
                def split(j, s):
                    act.wait_ge(w_loaded[s % RING], 4 * (j - s % RING) + 16)
                    act.wait_ge(product_done, j + 1)
                    act.activation(w_hi[s % RING][:, :, :], w_s[s % RING][:, :].rearrange("p (k n) -> p k n", k=KD),
                                   ACT.Copy).then_inc(w_hi_ready, 1)

                def next_square(t, k):
                    if k == 0:
                        act.wait_ge(xn_in, t * 16 + 16)
                    if k >= 2:
                        act.wait_ge(next_added, t * ADDS + k - 1)
                    act.activation(next_sq[k % 2], xn_s[:, k, :], ACT.Square).then_inc(next_squares, 1)

                def next_root(t):
                    act.wait_ge(next_sums, t * 2 + 2)
                    act.activation(next_std, NEXT_SUM[:, :], ACT.Sqrt, scale=1.0 / D, bias=eps_s[:, :])\
                        .then_inc(next_stds, 1)

                def h_high(t, k, n, src):
                    act.wait_ge(normed, t * 16 + n * KD + k + 1)
                    act.activation(h_hi[:, k, :], src[:, k, :], ACT.Copy).then_inc(h_hi_ready, 1)

                def load_branches(t):
                    for b, src in enumerate((attnT, rwkvT)):
                        act.dma_start(br_s[:, b * KW:(b + 1) * KW, :],
                                      src[:, :, bass.ds(t * TG, TG)].rearrange("k p n -> p k n")).then_inc(br_in[b], 16)

                def group(t):
                    def root(n):
                        act.wait_ge(sums, t * (KD + 4) + (2, KD + 2, KD + 4)[n])
                        act.activation(std[:, :], SUM[:, :], ACT.Sqrt, scale=1.0 / D, bias=eps_s[:, :])\
                            .then_inc(stds, 1)

                    for b in range(2):
                        act.wait_ge(br_in[b], t * 16 + 16)
                        act.activation(br_hi[:, b * KW:(b + 1) * KW, :], br_s[:, b * KW:(b + 1) * KW, :], ACT.Copy)\
                            .then_inc(br_hi_ready, 1)
                    if not is_first(t):
                        act.wait_ge(rstds, t * 3)

                    def after(kind, k, s, j):
                        if kind == "gate":
                            act.wait_ge(product_done, j + RING + 1)
                            act.wait_ge(gated, t * KD + k + 2)
                            act.activation(s_s[s % 3][:, :], banks[s // 3 % 2 * 4 + s % 3][:, :], ACT.Sigmoid)\
                                .then_inc(gate_ready, 1)
                        if kind in ("out", "ffn_out"):
                            copied, base = (out_copied, 0) if kind == "out" else (ffn_copied, ADDS)
                            act.wait_ge(copied, t * KD + k + (5 if kind == "out" else 3))
                            if k >= 2:
                                act.wait_ge(added, t * (2 * ADDS) + base + k - 1)
                            act.activation(s_s[k % 2][:, :], m_s[:, k, :], ACT.Square).then_inc(squares, 1)
                        if kind == "ffn_out" and not is_last(t):
                            for b in NEXT_SQUARES.get(k, ()):
                                next_square(t + 1, b)
                            if k == 5:
                                next_root(t + 1)
                            if k == 6:
                                for b in range(KD):
                                    h_high(t + 1, b, 0, xn_s)
                        if kind == "mixed":
                            root(0)
                            for k in range(KD):
                                act.wait_ge(x2_ready, t * 16 + k + 1)
                                act.activation(m_s[:, k, :], x_s[:, k, :], ACT.Square).then_inc(squares, 1)
                            root(1)
                            for k in range(KD):
                                h_high(t, k, 1, m_s)
                        if kind == "silu":
                            act.wait_ge(product_done, j + RING + 1)
                            act.wait_ge(ffn_step, t * 3 * KF + 3 * k + 1)
                            act.activation(s_s[s // 2][:, :], banks[s // 2 * 2][:, :], ACT.Silu)\
                                .then_inc(silu_ready, 1)
                        if kind == "done":
                            if not is_last(t):
                                load_branches(t + 1)
                            root(2)

                    jobs(act, t, lambda j, s, kt, kind, k, row: split(j + AHEAD, s + AHEAD), after)

                act.wait_ge(eps_set, 1)
                for k in range(KD):
                    next_square(0, k)
                load_branches(0)
                next_root(0)
                for s in range(AHEAD):
                    split(s, s)
                for k in range(KD):
                    h_high(0, k, 0, xn_s)
                groups(act, group)

            @block.vector
            def _(dve):
                dve.memset(eps_s[:, :], EPS).then_inc(eps_set, 1)
                dve.sem_inc(gated, 2)
                dve.sem_inc(merge_step, 1)
                dve.sem_inc(out_copied, 4)
                dve.sem_inc(ffn_step, 6)
                dve.sem_inc(ffn_copied, 2)
                dve.wait_ge(par_in, 80)
                def next_norm(t):
                    dve.wait_ge(next_stds, t + 1)
                    dve.reciprocal(next_rstd, next_std).then_inc(next_rstds, 1)
                    dve.wait_ge(next_rstds, t + 1)
                    for k in range(KD):
                        dve.scalar_tensor_tensor(out=xn_s[:, k, :], in0=xn_s[:, k, :], scalar=ln_s[0][:, k:k + 1],
                                                 in1=next_rstd, op0=ALU.mult, op1=ALU.mult).then_inc(normed, 1)
                    dve.wait_ge(normed, t * 16 + KD)

                def next_add(t, k):
                    dve.wait_ge(next_squares, t * KD + k + 1)
                    if k >= 2:
                        dve.wait_ge(next_added, t * ADDS + k - 1)
                    dve.tensor_tensor(next_sq[k % 2], next_sq[k % 2], next_sq[1 - k % 2], ALU.add).then_inc(next_added, 1)

                def branches_low(t):
                    for b in range(2):
                        part = slice(b * KW, (b + 1) * KW)
                        dve.wait_ge(br_hi_ready, t * 2 + b + 1)
                        dve.tensor_tensor(br_lo[:, part, :], br_s[:, part, :], br_hi[:, part, :].bitcast(F32),
                                          ALU.subtract).then_inc(br_lo_ready, 1)

                def h_low(t, k, n, src):
                    dve.wait_ge(h_hi_ready, t * 16 + n * KD + k + 1)
                    dve.tensor_tensor(h_lo[:, k, :], src[:, k, :], h_hi[:, k, :].bitcast(F32), ALU.subtract)\
                        .then_inc(h_lo_ready, 1)

                def group(t):
                    def invert(n):
                        dve.wait_ge(stds, t * 3 + n + 2)
                        dve.reciprocal(rstd[:, :], std[:, :]).then_inc(rstds, 1)
                        dve.wait_ge(rstds, t * 3 + n + 1)

                    def norm():
                        invert(1)
                        for k in range(KD):
                            dve.scalar_tensor_tensor(out=m_s[:, k, :], in0=x_s[:, k, :], scalar=ln_s[2][:, k:k + 1],
                                                     in1=rstd[:, :], op0=ALU.mult, op1=ALU.mult).then_inc(normed, 1)
                        for k in range(KD):
                            h_low(t, k, 1, m_s)

                    def add_normed(n, ln):
                        invert(2 * n)
                        if n == 1 and not is_last(t):
                            branches_low(t + 1)
                        for k in range(KD):
                            dve.scalar_tensor_tensor(out=m_s[:, k, :], in0=m_s[:, k, :], scalar=ln[:, k:k + 1],
                                                     in1=rstd[:, :], op0=ALU.mult, op1=ALU.mult).then_inc(scaled, 1)
                            dve.wait_ge(scaled, t * 16 + n * KD + k + 1)
                            dve.tensor_tensor(x_s[:, k, :], x_s[:, k, :], m_s[:, k, :], ALU.add).then_inc(x2_ready, 1)

                    if is_first(t):
                        branches_low(t)

                    def add_squares(n, k):
                        dve.wait_ge(squares, t * 24 + n * KD + k + 1)
                        if k >= 2:
                            dve.wait_ge(added, t * (2 * ADDS) + n // 2 * ADDS + k - 1)
                        dve.tensor_tensor(s_s[k % 2][:, :], s_s[k % 2][:, :], s_s[1 - k % 2][:, :], ALU.add)\
                            .then_inc(added, 1)

                    def three(step, n, hi, lo, k):
                        dve.wait_ge(step, n)
                        dve.tensor_copy(hi[:, bass.ds(k, 1), :], p_s[:, :].rearrange("p (a n) -> p a n", a=1))\
                            .then_inc(step, 1)
                        dve.wait_ge(step, n + 1)
                        dve.tensor_tensor(lo[:, bass.ds(k, 1), :], p_s[:, :].rearrange("p (a n) -> p a n", a=1),
                                          hi[:, bass.ds(k, 1), :].bitcast(F32), ALU.subtract).then_inc(step, 1)

                    def after(kind, k, s, j):
                        if kind == "merge":
                            bank = s // 3 % 2 * 4
                            n = t * 3 * KD + 3 * k + 1
                            dve.wait_ge(gate_ready, t * 2 * KD + 2 * k + 2)
                            dve.wait_ge(product_done, j + RING + 1)
                            dve.wait_ge(merge_step, n)
                            dve.tensor_tensor(p_s[:, :], s_s[0][:, :], banks[bank + 2][:, :], ALU.mult)
                            dve.tensor_tensor(q_s[:, :], s_s[1][:, :], banks[bank + 3][:, :], ALU.mult)\
                                .then_inc(gated, 1)
                            dve.wait_ge(gated, t * KD + k + 3)
                            dve.tensor_tensor(p_s[:, :], p_s[:, :], q_s[:, :], ALU.add).then_inc(merge_step, 1)
                            three(merge_step, n + 1, g_hi, g_lo, k)
                        if kind in ("out", "ffn_out"):
                            dve.wait_ge(product_done, j + RING + 1)
                            if kind == "out":
                                dve.tensor_copy(m_s[:, k, :], banks[k % 4][:, :]).then_inc(out_copied, 1)
                            else:
                                dve.tensor_copy(m_s[:, k, :], banks[4 + k % 2][:, :]).then_inc(ffn_copied, 1)
                            if k >= 2:
                                add_squares(0 if kind == "out" else 2, k - 1)
                        if kind == "ffn_out" and not is_last(t):
                            for b in NEXT_SQUARES.get(k, ()):
                                if 1 <= b <= ADDS:
                                    next_add(t + 1, b)
                            if k == 5:
                                next_norm(t + 1)
                            if k == 6:
                                for b in range(KD):
                                    h_low(t + 1, b, 0, xn_s)
                        if kind == "mixed":
                            dve.wait_ge(x_in, t * 16 + 16)
                            add_normed(0, ln_s[1])
                            norm()
                        if kind == "ffn_in":
                            n = t * 3 * KF + 3 * k + 6
                            dve.wait_ge(silu_ready, t * KF + k + 1)
                            dve.wait_ge(product_done, j + RING + 1)
                            dve.wait_ge(ffn_step, n)
                            dve.tensor_tensor(p_s[:, :], s_s[s // 2][:, :], banks[s // 2 * 2 + 1][:, :], ALU.mult)\
                                .then_inc(ffn_step, 1)
                            three(ffn_step, n + 1, f_hi, f_lo, k)
                        if kind == "done":
                            add_normed(1, ln_s[3])

                    jobs(dve, t, nothing, after)

                for k in range(1, ADDS + 1):
                    next_add(0, k)
                next_norm(0)
                for k in range(KD):
                    h_low(0, k, 0, xn_s)
                groups(dve, group)

            @block.tensor
            def _(pe):
                pe.sem_inc(product_done, RING)
                pe.sem_inc(stds, 1)
                pe.wait_ge(par_in, 80)
                def next_sum(t):
                    pe.wait_ge(next_squares, t * KD + KD)
                    pe.wait_ge(next_added, t * ADDS + ADDS)
                    for b in range(2):
                        pe.matmul(NEXT_SUM[:, :], ones_s[:, :], next_sq[b], start=b == 0, stop=b == 1)\
                            .then_inc(next_sums, 1)

                def group(t):
                    def sum_squares(n):
                        pe.wait_ge(stds, t * 3 + n + 1)
                        pe.wait_ge(added, t * (2 * ADDS) + n // 2 * ADDS + ADDS)
                        pe.matmul(SUM[:, :], ones_s[:, :], s_s[0][:, :], start=True, stop=False).then_inc(sums, 1)
                        pe.wait_ge(squares, t * 24 + n * KD + KD)
                        pe.matmul(SUM[:, :], ones_s[:, :], s_s[1][:, :], start=False, stop=True).then_inc(sums, 1)

                    pe.wait_ge(h_lo_ready, t * 16 + KD)
                    pe.wait_ge(stds, t * 3 + 1)
                    hold(pe, holds[1])

                    def job(j, s, kt, kind, k, row):
                        pe.wait_ge(w_lo_ready, j + RING + 1)
                        whi, wlo = w_hi[s % RING], w_lo[s % RING]

                        def part(out, w0, n, xs, **flags):
                            return product(pe, out[:, :], (lambda k: whi[:, w0 + k, :], lambda k: wlo[:, w0 + k, :]),
                                           tuple((lambda k, x=x: x[:, k, :]) for x in xs), n, **flags)

                        if kind == "merge":
                            bank = s // 3 % 2 * 4
                            if s % 3 == 0:
                                pe.wait_ge(gated, t * KD + k + 1)
                            if s % 3 < 2:
                                mm = part(banks[bank + s % 3], 0, KD, (h_hi, h_lo))
                            else:
                                pe.wait_ge(br_lo_ready, t * 2 + 1)
                                part(banks[bank + 2], 0, KW, (br_hi[:, 0:KW, :], br_lo[:, 0:KW, :]))
                                pe.wait_ge(br_lo_ready, t * 2 + 2)
                                mm = part(banks[bank + 3], KW, KW, (br_hi[:, KW:2 * KW, :], br_lo[:, KW:2 * KW, :]))
                        elif kind == "out":
                            if s == 0:
                                pe.wait_ge(merge_step, (t + 1) * 3 * KD + 1)
                            pe.wait_ge(out_copied, t * KD + s + 1)
                            mm = part(banks[s % 4], 0, KD, (g_hi, g_lo))
                        elif kind == "ffn_in":
                            if s % 2 == 0:
                                pe.wait_ge(ffn_step, t * 3 * KF + 3 * k + 1)
                            mm = part(banks[s], 0, KD, (h_hi, h_lo))
                        else:
                            if s == 0:
                                pe.wait_ge(ffn_step, (t + 1) * 3 * KF + 6)
                            if s % 3 == 0:
                                pe.wait_ge(ffn_copied, t * KD + s // 3 + 1)
                            k0 = 8 * (s % 3)
                            mm = part(banks[4 + s // 3 % 2], 0, kt, (f_hi[:, k0:k0 + kt, :], f_lo[:, k0:k0 + kt, :]),
                                      start=s % 3 == 0, stop=s % 3 == 2)
                        mm.then_inc(product_done, 1)

                    def after(kind, k, s, j):
                        if kind == "ffn_out" and k == 5 and not is_last(t):
                            next_sum(t + 1)
                        if kind == "mixed":
                            sum_squares(0)
                            pe.wait_ge(stds, t * 3 + 2)
                            for k in range(KD):
                                pe.wait_ge(squares, t * 24 + KD + k + 1)
                                pe.matmul(SUM[:, :], ones_s[:, :], m_s[:, k, :], start=k == 0, stop=k == KD - 1)\
                                    .then_inc(sums, 1)
                            pe.wait_ge(h_lo_ready, t * 16 + 2 * KD)
                            hold(pe, holds[1])
                        if kind == "done":
                            sum_squares(2)

                    jobs(pe, t, job, after)

                next_sum(0)
                groups(pe, group)


def blocks(w):
    k, c = w.shape
    return np.ascontiguousarray(w.reshape(k // P, P, c // P, P).transpose(2, 1, 0, 3)).reshape(c // P, P, k)


def columns(v):
    return np.ascontiguousarray(v.reshape(-1, P).T)


def shape_constants():
    r = np.arange(P)
    c = {}
    c["ones"] = np.ones((P, P), np.float32)
    c["ident"] = np.eye(P, dtype=np.float32)
    c["headsum"] = (r[:, None] // HD == r[None, :] // HD).astype(np.float32)
    swap = np.zeros((P, P), np.float32)
    e = np.arange(0, P, 2)
    swap[e + 1, e] = -1.0
    swap[e, e + 1] = 1.0
    c["swap"] = swap
    t = np.arange(N_PROMPT)
    nf = HD // 4
    inv = (ROPE_THETA ** (-np.arange(nf, dtype=np.float32) / nf)).astype(np.float32)
    ang = np.concatenate([(t // GRID_W).astype(np.float32)[:, None] * inv,
                          (t % GRID_W).astype(np.float32)[:, None] * inv], -1)
    tab = ang[:, (r % HD) // 2].T
    tab = np.concatenate([tab, tab[:, :N_SAMPLE]], 1)
    c["cos"], c["sin"] = np.cos(tab).astype(np.float32), np.sin(tab).astype(np.float32)
    s, q = r[:, None], r[None, :]
    strict = [(s < q), (s > q)]
    loose = [(s <= q), (s >= q)]
    c["causal"] = np.stack([np.stack([strict[d], loose[d]]) for d in range(2)]).astype(np.float32)
    c["pair"] = np.stack([strict[d] & (s // 2 == q // 2) for d in range(2)]).astype(np.float32)
    levels = np.zeros((2, LEVELS, P, P), np.float32)
    for d in range(2):
        for n in range(LEVELS):
            m = 2 << n
            levels[d, n] = (s // (2 * m) == q // (2 * m)) & ((s // m) % 2 == 1 - d) & ((q // m) % 2 == d)
    c["levels"] = levels
    c["restart"] = np.where(np.arange(TG) % P == 0, 0.0, 1.0).astype(np.float32)[None].repeat(P, 0)
    return {n: np.ascontiguousarray(x) for n, x in c.items()}


PARAMS = ("k_k", "k_a", "r_k", "w0", "a0", "lnx_w", "lnx_b")
CONSTS = ("ones", "ident", "headsum", "swap", "cos", "sin", "causal", "pair", "levels", "restart")


def build(nc, at):
    def scratch(name, shape):
        return nc.dram_tensor(name, shape, F32, kind="Internal").ap()

    uT = scratch("uT", [NB_IN, P, N])
    qkT = scratch("qkT", [(B_V - B_Q) * P, N])
    attnT = scratch("attnT", [WIDTH, N])
    y = scratch("y", [P, NCH, WIDTH])
    bonusT, gT, rwkvT = (scratch(n, [KW, P, N]) for n in ("bonusT", "gT", "rwkvT"))
    with nc.sbuf_tensor("h_hi", [P, KD, N], F32R) as h_hi, nc.sbuf_tensor("h_lo", [P, KD, N], F32R) as h_lo:
        project(nc, (h_hi, h_lo), uT, at["xT"], at["w_in"], at["ln_mix_pre"], at["mu"], at["ones"])
    rope(nc, qkT, uT, at["gains"], at["cos"], at["sin"], at["headsum"], at["swap"])
    attention(nc, attnT, qkT, uT, at["ident"], 0, N_PROMPT, "ap")
    attention(nc, attnT, qkT, uT, at["ident"], N_PROMPT, N_SAMPLE, "as")
    recurrence(nc, y, bonusT, gT, uT, at["w_up"], at["a_up"], at["g_up"], at["par"], at)
    branch_output(nc, rwkvT, y, bonusT, gT, at["par"], at["ident"])
    finish(nc, at["yT"], at["xT"], attnT.rearrange("(k p) n -> k p n", p=P), rwkvT, at["w_rest"],
           at["ln_mix_pre"], at["ln_mix_post"], at["ln_ffn_pre"], at["ln_ffn_post"], at["ones"])


def layout(inputs):
    f = {n: np.asarray(v)[0] for n, v in inputs.items()}
    x = np.concatenate([f["x_prompt"], f["x_sample"]], 0)
    out = {"xT": np.ascontiguousarray(x.reshape(NTG, TG, KD, P).transpose(0, 3, 2, 1))}
    w_in, gate = f["w_in"][:, :NB_IN * P], f["w_in"][:, NB_IN * P:]
    out["w_in"] = blocks(w_in)
    for n in ("ln_mix_pre", "ln_mix_post", "ln_ffn_pre", "ln_ffn_post"):
        out[n] = columns(f[n])
    mu = np.concatenate([np.zeros(B_R * P, np.float32), f["shift_mu"]])
    out["mu"] = columns(mu)
    out["gains"] = columns(np.concatenate([f["q_gain"]] * HEADS + [f["k_gain"]] * 2))
    out["par"] = np.ascontiguousarray(np.stack(
        [columns(v) for n in PARAMS for v in np.reshape(f[n], (-1, WIDTH))], 1))
    for n in ("w_up", "a_up", "g_up"):
        out[n] = np.ascontiguousarray(f[n].reshape(P, PAIRS, P).transpose(1, 0, 2))
    branch = blocks(f["w_branch"].reshape(2 * WIDTH, D))
    last = blocks(f["w_ffn_out"])
    last = np.pad(last, ((0, 0), (0, 0), (0, 3 * D - D_FF))).reshape(KD, P, 3, D).transpose(0, 2, 1, 3)
    out["w_rest"] = np.ascontiguousarray(np.concatenate([
        np.stack([blocks(gate[:, :D]), blocks(gate[:, D:]), branch], 1).reshape(3 * KD, P, D),
        blocks(f["w_out"]),
        np.stack([blocks(f["w_ffn_in"][:, :D_FF]), blocks(f["w_ffn_in"][:, D_FF:])], 1).reshape(2 * KF, P, D),
        last.reshape(3 * KD, P, D)], 0))
    return {**out, **{n: v for n, v in shape_constants().items() if n in CONSTS}}


def kernel(**inputs):
    import concourse.bacc as bacc
    from concourse.bass_utils import run_bass_kernel_spmd

    nc = bacc.Bacc("TRN2", target_bir_lowering=False, num_devices=1)
    arrays = layout(inputs)
    at = {n: nc.dram_tensor(n, v.shape, F32, kind="ExternalInput").ap() for n, v in arrays.items()}
    at["yT"] = nc.dram_tensor("yT", (NTG, P, KD, TG), F32, kind="ExternalOutput").ap()
    build(nc, at)
    got = run_bass_kernel_spmd(nc, [arrays], core_ids=[0]).results[0]["yT"]
    y = got.transpose(0, 3, 2, 1).reshape(N, D)
    return y[None, :N_PROMPT], y[None, N_PROMPT:]
```
